# Optimizing a Trainium2 kernel written in Bass

```python
import functools
import jax, jax.numpy as jnp
from jax import lax
import numpy as np

D_MODEL = 1024
BATCH = 1
SEQ = 128
DEPTH = 2
DEC_BATCH = 1
DEC_SEQ = 128
PAST_LEN = 128

GRID_W = 64
GLA_HEADS = 4
GLA_DK = 64
GLA_DV = 128
GLA_GATE_RANK = 16
GLA_GATE_TAU = 16.0
GLA_CHUNK = 64
NA_HEADS = 8
NA_DH = 64
NA_WIN_R = 8
NA_WIN_C = 16
NA_QBLK_C = 16
NA_KBLK_C = NA_QBLK_C + NA_WIN_C
Q_BLOCK = 128
CONV_CH = 512
CONV_K = 31
FF_DENSE = 2816
N_EXPERTS = 8
TOP_K = 2
FF_EXPERT = 3584
ROPE_BASE = 10000.0
LN_EPS = 1e-5
DN_ALPHA = (2 * DEPTH) ** 0.25
DN_BETA = (8 * DEPTH) ** -0.25
N_DENSE = (DEPTH + 1) // 2
N_MOE = DEPTH // 2
GLA_QK_W = GLA_HEADS * GLA_DK
GLA_V_W = GLA_HEADS * GLA_DV
NA_W = NA_HEADS * NA_DH
IN_SPLITS = (GLA_QK_W, GLA_QK_W, GLA_V_W, GLA_V_W, 2 * GLA_GATE_RANK, NA_W, NA_W, NA_W, 2 * CONV_CH, 3 * D_MODEL)
IN_COLS = sum(IN_SPLITS)

kernel_name = 'hybrid_gla_natten_conformer_dit_step'

def _ln(x, g, b):
    xf = x.astype(jnp.float32)
    mu = jnp.mean(xf, -1, keepdims=True)
    var = jnp.mean(jnp.square(xf - mu), -1, keepdims=True)
    return (xf - mu) * lax.rsqrt(var + LN_EPS) * g + b

def _rope_axis(x, pos):
    n = x.shape[-1] // 2
    inv = ROPE_BASE ** (-jnp.arange(n, dtype=jnp.float32) / n)
    ang = pos.astype(jnp.float32)[:, None] * inv[None, :]
    cos, sin = jnp.cos(ang)[:, None, :], jnp.sin(ang)[:, None, :]
    x1, x2 = x[..., :n], x[..., n:]
    return jnp.concatenate([x1 * cos - x2 * sin, x1 * sin + x2 * cos], -1)

def _rope2d(x):
    t = jnp.arange(x.shape[1])
    half = x.shape[-1] // 2
    return jnp.concatenate([_rope_axis(x[..., :half], t // GRID_W), _rope_axis(x[..., half:], t % GRID_W)], -1)

def _gla_scan(q, k, v, g, s0):
    b_, l_, h_, _ = q.shape
    dv = v.shape[-1]
    n = l_ // GLA_CHUNK

    def chunks(a):
        return a.astype(jnp.float32).reshape(b_, n, GLA_CHUNK, h_, a.shape[-1]).transpose(1, 0, 3, 2, 4)

    causal = jnp.tril(jnp.ones((GLA_CHUNK, GLA_CHUNK), dtype=bool))[:, :, None]

    def step(s, inp):
        qc, kc, vc, gc = inp
        cum = jnp.cumsum(gc, axis=2)
        rel = jnp.where(causal, cum[:, :, :, None, :] - cum[:, :, None, :, :], -jnp.inf)
        att = jnp.einsum('bhtd,bhsd,bhtsd->bhts', qc, kc, jnp.exp(rel))
        o = jnp.einsum('bhts,bhsv->bhtv', att, vc) + jnp.einsum('bhtd,bhdv->bhtv', qc * jnp.exp(cum), s)
        last = cum[:, :, -1:, :]
        s = jnp.exp(last[:, :, 0, :])[..., None] * s + jnp.einsum('bhsd,bhsv->bhdv', kc * jnp.exp(last - cum), vc)
        return s, o

    s_fin, o = lax.scan(step, s0.astype(jnp.float32), (chunks(q), chunks(k), chunks(v), chunks(g)))
    o = o.transpose(1, 0, 3, 2, 4).reshape(b_, l_, h_, dv)
    return o, s_fin

def _gla_bidir(q, k, v, g_f, g_b, s0_f, s0_b):
    o_f, s_f = _gla_scan(q, k, v, g_f, s0_f)
    fl = lambda a: jnp.flip(a, 1)
    o_b, s_b = _gla_scan(fl(q), fl(k), fl(v), fl(g_b), s0_b)
    return o_f + fl(o_b), s_f, s_b

def _ctx_attention(q, k, v):
    b_, l_, h_, dh = q.shape
    nb = l_ // Q_BLOCK
    qb = q.astype(jnp.float32).reshape(b_, nb, Q_BLOCK, h_, dh).transpose(1, 0, 2, 3, 4)
    kf, vf = k.astype(jnp.float32), v.astype(jnp.float32)

    def blk(qi):
        s = jnp.einsum('bqhd,bkhd->bhqk', qi, kf) * dh ** -0.5
        return jnp.einsum('bhqk,bkhd->bqhd', jax.nn.softmax(s, -1), vf)

    o = lax.map(blk, qb)
    return o.transpose(1, 0, 2, 3, 4).reshape(b_, l_, h_ * dh)

def _na_latent(q, k_lat, v_lat, k_ctx, v_ctx, rpb):
    b_, l_, h_, dh = q.shape
    rows = l_ // GRID_W
    kr = min(NA_WIN_R, rows)
    ncb = GRID_W // NA_QBLK_C
    r = jnp.arange(rows)
    j = jnp.arange(ncb)
    rs = jnp.clip(r - kr // 2, 0, rows - kr)
    ks = jnp.clip(j * NA_QBLK_C - NA_WIN_C // 2, 0, GRID_W - NA_KBLK_C)
    key_row = rs[:, None] + jnp.arange(kr)[None, :]
    key_col = ks[:, None] + jnp.arange(NA_KBLK_C)[None, :]
    nk = kr * NA_KBLK_C
    idx = (key_row[:, None, :, None] * GRID_W + key_col[None, :, None, :]).reshape(rows, ncb, nk)
    q_col = j[:, None] * NA_QBLK_C + jnp.arange(NA_QBLK_C)[None, :]
    cs = jnp.clip(q_col - NA_WIN_C // 2, 0, GRID_W - NA_WIN_C)
    kc3 = key_col[:, None, :]
    valid = (kc3 >= cs[..., None]) & (kc3 < cs[..., None] + NA_WIN_C)
    dc = jnp.clip(kc3 - q_col[..., None], -(NA_WIN_C - 1), NA_WIN_C - 1)
    dr = key_row - r[:, None]
    bias = rpb[:, (dr + NA_WIN_R - 1)[:, None, None, :, None], (dc + NA_WIN_C - 1)[None, :, :, None, :]]
    bias = bias.reshape(h_, rows, ncb, NA_QBLK_C, nk).transpose(1, 2, 0, 3, 4).astype(jnp.float32)
    mask = jnp.broadcast_to(valid[:, :, None, :], (ncb, NA_QBLK_C, kr, NA_KBLK_C)).reshape(ncb, NA_QBLK_C, nk)
    scale = dh ** -0.5
    qg = q.astype(jnp.float32).reshape(b_, rows, ncb, NA_QBLK_C, h_, dh)
    kg = k_lat.astype(jnp.float32)[:, idx]
    vg = v_lat.astype(jnp.float32)[:, idx]
    kcx, vcx = k_ctx.astype(jnp.float32), v_ctx.astype(jnp.float32)
    s_loc = jnp.einsum('brjqhd,brjkhd->brjhqk', qg, kg) * scale + bias[None]
    s_loc = jnp.where(mask[None, None, :, None], s_loc, -jnp.inf)
    s_ctx = jnp.einsum('brjqhd,bchd->brjhqc', qg, kcx) * scale
    p = jax.nn.softmax(jnp.concatenate([s_loc, s_ctx], -1), -1)
    o = jnp.einsum('brjhqk,brjkhd->brjqhd', p[..., :nk], vg) + jnp.einsum('brjhqc,bchd->brjqhd', p[..., nk:], vcx)
    return o.reshape(b_, l_, h_ * dh)

def _conv_module(u, lp):
    a, gt = jnp.split(u, 2, -1)
    z = (a * jax.nn.sigmoid(gt)).astype(jnp.float32)
    w = lp['cv_w'].astype(jnp.float32)[:, None, :]
    z = lax.conv_general_dilated(z, w, (1,), [(CONV_K // 2, CONV_K // 2)],
                                 dimension_numbers=('NWC', 'WIO', 'NWC'),
                                 feature_group_count=CONV_CH) + lp['cv_b']
    z = jax.nn.silu(_ln(z, lp['cv_ln_g'], lp['cv_ln_b']))
    return z @ lp['w_br_cv']

def _mixer(h, lp, latent, ctx_k, ctx_v, s0):
    b_, l_, _ = h.shape
    offs = [int(o) for o in np.cumsum(IN_SPLITS)[:-1]]
    z = jnp.einsum('bld,dn->bln', h, lp['w_in'])
    qa, ka, va, ra, gda, qb, kb, vb, cvi, mg = jnp.split(z, offs, axis=-1)
    qa = qa.astype(jnp.float32).reshape(b_, l_, GLA_HEADS, GLA_DK) * GLA_DK ** -0.5
    ka = ka.astype(jnp.float32).reshape(b_, l_, GLA_HEADS, GLA_DK)
    if latent:
        qa, ka = _rope2d(qa), _rope2d(ka)
    va = va.reshape(b_, l_, GLA_HEADS, GLA_DV)
    glog = jnp.einsum('blnr,nrk->blnk', gda.reshape(b_, l_, 2, GLA_GATE_RANK), lp['gla_w_gup']) + lp['gla_b_g']
    glog = (jax.nn.log_sigmoid(glog.astype(jnp.float32)) / GLA_GATE_TAU).reshape(b_, l_, 2, GLA_HEADS, GLA_DK)
    if s0 is None:
        s0 = jnp.zeros((b_, 2, GLA_HEADS, GLA_DK, GLA_DV), jnp.float32)
    o, s_f, s_b = _gla_bidir(qa, ka, va, glog[:, :, 0], glog[:, :, 1], s0[:, 0], s0[:, 1])
    o = o * lax.rsqrt(jnp.mean(jnp.square(o), -1, keepdims=True) + LN_EPS) * lp['gla_norm']
    y_a = (o.reshape(b_, l_, GLA_V_W) * jax.nn.silu(ra)) @ lp['w_br_gla']
    qb = qb.reshape(b_, l_, NA_HEADS, NA_DH)
    kb = kb.reshape(b_, l_, NA_HEADS, NA_DH)
    vb = vb.reshape(b_, l_, NA_HEADS, NA_DH)
    if latent:
        att = _na_latent(qb, kb, vb, ctx_k, ctx_v, lp['na_rpb'])
    else:
        att = _ctx_attention(qb, kb, vb)
    y_b = att @ lp['w_br_na']
    y_c = _conv_module(cvi, lp)
    g = jax.nn.sigmoid(mg.reshape(b_, l_, 3, D_MODEL))
    m = g[:, :, 0] * y_a + g[:, :, 1] * y_b + g[:, :, 2] * y_c
    return m @ lp['w_out'], kb, vb, jnp.stack([s_f, s_b], 1)

def _swiglu(h, wg, wu, wd):
    return (jax.nn.silu(h @ wg) * (h @ wu)) @ wd

def _moe(h, w_router, wg, wu, wd):
    b_, l_, d_ = h.shape
    t = h.reshape(b_ * l_, d_)
    logits = (t @ w_router).astype(jnp.float32)
    top_v, top_i = lax.top_k(logits, TOP_K)
    top_w = jax.nn.softmax(top_v, -1)
    gates = jnp.sum(jax.nn.one_hot(top_i, N_EXPERTS, dtype=jnp.float32) * top_w[..., None], axis=1)
    y = jnp.zeros((b_ * l_, d_), jnp.float32)
    for e in range(N_EXPERTS):
        y = y + gates[:, e:e + 1] * _swiglu(t, wg[e], wu[e], wd[e])
    return y.reshape(b_, l_, d_)

def _layer(x, cond, lp, ffn, latent, ctx_k, ctx_v, s0):
    mod = jax.nn.silu(cond) @ lp['w_mod'] + lp['b_mod']
    sh1, sc1, g1, sh2, sc2, g2 = jnp.split(mod[:, None, :], 6, -1)
    h = x * (1 + sc1) + sh1
    mix, kb, vb, s = _mixer(h, lp, latent, ctx_k, ctx_v, s0)
    x = _ln(DN_ALPHA * x + g1 * mix, lp['ln_g'][0], lp['ln_b'][0])
    h = x * (1 + sc2) + sh2
    x = _ln(DN_ALPHA * x + g2 * ffn(h), lp['ln_g'][1], lp['ln_b'][1])
    return x, kb, vb, s

def setup_inputs(seed: int = 0) -> dict:
    key = jax.random.key(seed)
    ks = iter(jax.random.split(key, 40))
    nrm = lambda shape, s: jax.random.normal(next(ks), shape, jnp.float32) * s
    D = D_MODEL
    return {
        'x_prompt': nrm((BATCH, SEQ, D), 1.0),
        'x_sample': nrm((DEC_BATCH, DEC_SEQ, D), 1.0),
        'cache_na_k': nrm((DEC_BATCH, DEPTH, PAST_LEN, NA_HEADS, NA_DH), 1.0),
        'cache_na_v': nrm((DEC_BATCH, DEPTH, PAST_LEN, NA_HEADS, NA_DH), 1.0),
        'state_gla': nrm((DEC_BATCH, DEPTH, 2, GLA_HEADS, GLA_DK, GLA_DV), 1.0),
        'c': nrm((DEC_BATCH, D), 1.0),
        'c_ctx': nrm((D,), 1.0),
        'w_mod': nrm((DEPTH, D, 6 * D), D ** -0.5),
        'b_mod': nrm((DEPTH, 6 * D), 0.02),
        'w_in': nrm((DEPTH, D, IN_COLS), D ** -0.5),
        'gla_w_gup': nrm((DEPTH, 2, GLA_GATE_RANK, GLA_QK_W), GLA_GATE_RANK ** -0.5),
        'gla_b_g': nrm((DEPTH, 2, GLA_QK_W), 0.1),
        'gla_norm': 1.0 + nrm((DEPTH, GLA_HEADS, GLA_DV), 0.01),
        'w_br_gla': nrm((DEPTH, GLA_V_W, D), GLA_V_W ** -0.5),
        'na_rpb': nrm((DEPTH, NA_HEADS, 2 * NA_WIN_R - 1, 2 * NA_WIN_C - 1), 0.1),
        'w_br_na': nrm((DEPTH, NA_W, D), NA_W ** -0.5),
        'cv_w': nrm((DEPTH, CONV_K, CONV_CH), CONV_K ** -0.5),
        'cv_b': nrm((DEPTH, CONV_CH), 0.02),
        'cv_ln_g': 1.0 + nrm((DEPTH, CONV_CH), 0.01),
        'cv_ln_b': nrm((DEPTH, CONV_CH), 0.01),
        'w_br_cv': nrm((DEPTH, CONV_CH, D), CONV_CH ** -0.5),
        'w_out': nrm((DEPTH, D, D), D ** -0.5 * DN_BETA),
        'ln_g': 1.0 + nrm((DEPTH, 2, D), 0.01),
        'ln_b': nrm((DEPTH, 2, D), 0.01),
        'ffd_w_gate': nrm((N_DENSE, D, FF_DENSE), D ** -0.5),
        'ffd_w_up': nrm((N_DENSE, D, FF_DENSE), D ** -0.5),
        'ffd_w_down': nrm((N_DENSE, FF_DENSE, D), FF_DENSE ** -0.5 * DN_BETA),
        'moe_w_router': nrm((N_MOE, D, N_EXPERTS), D ** -0.5),
        'moe_w_gate': nrm((N_MOE, N_EXPERTS, D, FF_EXPERT), D ** -0.5),
        'moe_w_up': nrm((N_MOE, N_EXPERTS, D, FF_EXPERT), D ** -0.5),
        'moe_w_down': nrm((N_MOE, N_EXPERTS, FF_EXPERT, D), FF_EXPERT ** -0.5 * DN_BETA),
    }

def reference(x_prompt, x_sample, cache_na_k, cache_na_v, state_gla, c, c_ctx,
              w_mod, b_mod, w_in, gla_w_gup, gla_b_g, gla_norm, w_br_gla, na_rpb, w_br_na,
              cv_w, cv_b, cv_ln_g, cv_ln_b, w_br_cv, w_out, ln_g, ln_b,
              ffd_w_gate, ffd_w_up, ffd_w_down,
              moe_w_router, moe_w_gate, moe_w_up, moe_w_down):
    y_prompt = x_prompt
    y_sample = x_sample
    ctx_cond = c_ctx[None, :]
    ks_l, vs_l, ss_l = [], [], []
    for l in range(DEPTH):
        lp = {'w_mod': w_mod[l], 'b_mod': b_mod[l], 'w_in': w_in[l],
              'gla_w_gup': gla_w_gup[l], 'gla_b_g': gla_b_g[l], 'gla_norm': gla_norm[l],
              'w_br_gla': w_br_gla[l], 'na_rpb': na_rpb[l], 'w_br_na': w_br_na[l],
              'cv_w': cv_w[l], 'cv_b': cv_b[l], 'cv_ln_g': cv_ln_g[l], 'cv_ln_b': cv_ln_b[l],
              'w_br_cv': w_br_cv[l], 'w_out': w_out[l], 'ln_g': ln_g[l], 'ln_b': ln_b[l]}
        i = l // 2
        if l % 2 == 0:
            ffn = functools.partial(_swiglu, wg=ffd_w_gate[i], wu=ffd_w_up[i], wd=ffd_w_down[i])
        else:
            ffn = functools.partial(_moe, w_router=moe_w_router[i], wg=moe_w_gate[i],
                                    wu=moe_w_up[i], wd=moe_w_down[i])
        y_prompt, kb, vb, s = _layer(y_prompt, ctx_cond, lp, ffn, False, None, None, None)
        ks_l.append(kb)
        vs_l.append(vb)
        ss_l.append(s)
        y_sample = _layer(y_sample, c, lp, ffn, True, cache_na_k[:, l], cache_na_v[:, l], state_gla[:, l])[0]
    new_cache_na_k = jnp.stack(ks_l, 1)
    new_cache_na_v = jnp.stack(vs_l, 1)
    new_state_gla = jnp.stack(ss_l, 1)
    return (y_prompt, y_sample, new_cache_na_k, new_cache_na_v, new_state_gla)


_drawn_inputs = setup_inputs


def setup_inputs(seed=0):
    import zlib

    import numpy as np

    out = dict(_drawn_inputs(seed))
    spreads = {}
    factors = {'state_gla': 8.0,
     'gla_norm': 104.437,
     'na_rpb': 22.914,
     'cv_b': 8.0,
     'cv_ln_g': 109.846,
     'cv_ln_b': 45.967,
     'cache_na_k': 5.049,
     'cache_na_v': 3.976}
    for name, (base, spread) in spreads.items():
        noise = np.random.default_rng([zlib.crc32(name.encode()), seed]).standard_normal(out[name].shape)
        drawn = base * np.exp(spread * noise) if base else spread * noise
        out[name] = __import__('jax').numpy.asarray(drawn.astype(out[name].dtype))
    for name, factor in factors.items():
        out[name] = (out[name] * factor).astype(out[name].dtype)
    return out
```

```python
from collections import Counter
from contextlib import ExitStack

import numpy as np

import concourse.bass as bass
from concourse import mybir

F32 = mybir.dt.float32
I32 = mybir.dt.int32
ALU = mybir.AluOpType
ACT = mybir.ActivationFunctionType
X = mybir.AxisListType.X

P = 128
G = 2
T = G * P
D = 1024
KD = D // P
DEPTH = 2
GLA_H, GLA_DK, GLA_DV, RANK, CHUNK, SUB = 4, 64, 128, 16, 64, 16
HP = GLA_H * GLA_DK // P
NA_H, NA_DH = 8, 64
PAIRS = NA_H // 2
CONV, TAPS = 512, 31
CC = CONV // P
ZW = P + TAPS - 1
FF_D, FF_E, EXPERTS = 2816, 3584, 8
GRID_W, WIN_R, WIN_C = 64, 8, 16
EPS = 1e-5
ALPHA = (2 * DEPTH) ** 0.25
BIG = 1000.0
EXP_CAP = 80.0
RING = 4
XRING = 7
W = 4096

SPLIT = dict(qk=0, v=512, r=1024, gda=1536, qb=1568, kb=2080, vb=2592, cva=3104, cvg=3616, mg=4128)
MG = [f"mg{n}" for n in range(6)]
SPLIT.update({m: 4128 + 512 * n for n, m in enumerate(MG)})

CONSTS = ["ident", "tri_f", "tri_b", "mask_f", "mask_b", "rot", "cos", "sin", "window", "slots", "before", "ones", "flip"]


def shape_constants():
    i = np.arange(P)
    r, c = i[:, None], i[None, :]
    same = r // CHUNK == c // CHUNK
    t = {"ident": r == c, "ones": np.ones((P, P)), "before": r < c}
    t["flip"] = (r // GRID_W == c // GRID_W) & (r % GRID_W + c % GRID_W == GRID_W - 1)
    t["mask_f"] = same & (r <= c)
    t["mask_b"] = same & (r >= c)
    t["tri_f"] = t["mask_f"] / 16.0
    t["tri_b"] = t["mask_b"] / 16.0
    rot = np.zeros((P, P))
    n = GLA_DK // 4
    for m in range(P):
        rot[m + n if m % (2 * n) < n else m - n, m] = -1.0 if m % (2 * n) < n else 1.0
    t["rot"] = rot
    inv = np.float32(10000.0) ** (-np.arange(n, dtype=np.float32) / np.float32(n))
    d = i % GLA_DK
    pos = np.where((d < GLA_DK // 2)[:, None], c // GRID_W, c % GRID_W).astype(np.float32)
    ang = pos * inv[d % n][:, None].astype(np.float32)
    t["cos"], t["sin"] = np.cos(ang), np.sin(ang)
    start = np.clip(r % GRID_W - WIN_C // 2, 0, GRID_W - WIN_C)
    t["window"] = np.where((c % GRID_W >= start) & (c % GRID_W < start + WIN_C), 0.0, -1e30)
    t["slots"] = np.broadcast_to(c, (P, P))
    half = np.stack([i < 64, i >= 64], 1)
    return np.concatenate([np.asarray(t[k], np.float32) for k in CONSTS] + [half.astype(np.float32)], 1)


FCHUNKS = [(a, min(512, FF_D - a)) for a in range(0, FF_D, 512)]


def plan():
    prods, units = [("vecs",)], []
    last = {}

    def p(*name):
        prods.append(name)

    def u(name, *users):
        units.append(name)
        last[name] = users[-1]

    for l in range(DEPTH):
        p("mod", l)
        for i in range(12):
            u(("mod", l, i), ("mod", l))
        for g in range(G):
            p("hT", l, g, 0), p("hT", l, g, 1)
        for i in range(2):
            p("cva", l, i)
        for i in range(2):
            p("cvg", l, i)
        u(("cva", l), ("cva", l, 1)), u(("cvg", l), ("cvg", l, 1))
        p("gda", l), p("q", l), p("k", l)
        u(("qk", l), ("k", l))
        p("glog", l, 0), p("glog", l, 1), p("v", l, 0), p("v", l, 1)
        u(("v", l), ("v", l, 1))
        p("rope", l), p("cum", l, 0), p("cum", l, 1)
        for n in ("qb", "kb"):
            p(n, l, 0), p(n, l, 1)
            u((n, l), (n, l, 1))
        p("keT", l, 0), p("att", l, 0, 0), p("att", l, 0, 1)
        p("vb", l, 0), p("vb", l, 1), u(("vb", l), ("vb", l, 1))
        p("kv", l, 0, 0), p("kv", l, 0, 1)
        p("r", l, 0), p("r", l, 1), u(("r", l), ("r", l, 1))
        p("o", l, 0)
        p("mg", l, 0, 0), p("mg", l, 1, 0), u(("mg0", l), ("mg", l, 1, 0))
        p("oT", l, 0)
        p("mg", l, 0, 1), p("mg", l, 1, 1), u(("mg1", l), ("mg", l, 1, 1))
        p("keT", l, 1), p("att", l, 1, 0), p("att", l, 1, 1)
        p("mg", l, 0, 2), p("mg", l, 1, 2), u(("mg2", l), ("mg", l, 1, 2))
        p("kv", l, 1, 0), p("kv", l, 1, 1)
        p("mg", l, 0, 3), p("mg", l, 1, 3), u(("mg3", l), ("mg", l, 1, 3))
        p("o", l, 1)
        p("mg", l, 0, 4), p("mg", l, 1, 4), u(("mg4", l), ("mg", l, 1, 4))
        p("oT", l, 1)
        p("mg", l, 0, 5), p("mg", l, 1, 5), u(("mg5", l), ("mg", l, 1, 5))
        p("kbtok", l), p("kctxT", l), p("bias", l, 0), p("bias", l, 1)
        p("sc", l, 0, 0), p("sc", l, 0, 1)
        p("cvtok", l, 0), p("cvtok", l, 1)
        p("cvT", l, 0), p("cvT", l, 1)
        p("PT", l, 0, 0), p("PT", l, 0, 1)
        for i in range(4):
            p("sc", l, 1, i)
        for b in (0, 2):
            for g in range(G):
                p("y", l, b, g, 0), p("y", l, b, g, 1)
            u(("br", l, b), ("y", l, b, 1, 1))
        p("attT", l, 0)
        for i in range(4):
            p("PT", l, 1, i)
        p("attT", l, 1)
        for g in range(G):
            p("y", l, 1, g, 0), p("y", l, 1, g, 1)
        u(("br", l, 1), ("y", l, 1, 1, 1))
        for g in range(G):
            p("gbc", l, 0, g, 0), p("gbc", l, 0, g, 1)
        for g in range(G):
            p("mT", l, g, 0), p("mT", l, g, 1)
        for n in range(2):
            for g in range(G):
                p("mix", l, g, n)
            u(("out", l, n), ("mix", l, 1, n))
        for g in range(G):
            p("h2T", l, g, 0), p("h2T", l, g, 1)
        for g in range(G):
            p("gbc", l, 1, g, 0), p("gbc", l, 1, g, 1)
        if l == 0:
            for i in range(len(FCHUNKS)):
                for g in range(G):
                    p("G", i, g)
                for g in range(G):
                    p("U", i, g)
                u(("wg", i), ("G", i, 1)), u(("wu", i), ("U", i, 1))
                if i:
                    p("aT", i - 1, 0), p("aT", i - 1, 1)
            p("aT", len(FCHUNKS) - 1, 0), p("aT", len(FCHUNKS) - 1, 1)
            for g in range(G):
                p("Y", g, 0), p("Y", g, 1)
            for i in range(len(FCHUNKS)):
                u(("wd", i), ("Y", 1, 1))
        else:
            for g in range(G):
                p("htok", g, 0), p("htok", g, 1)
            p("logits",), p("rank",)
    return prods, units, last


DOWN = len(FCHUNKS) - 1
PRODS, UNITS, LAST = plan()
PIDX = {n: i for i, n in enumerate(PRODS)}
UIDX = {n: i for i, n in enumerate(UNITS)}
NB = 8
PBASE = [len([i for i in range(len(PRODS)) if i % NB == b]) for b in range(NB)]
UBASE = [len([i for i in range(len(UNITS)) if i % RING == s]) if s < RING else 0 for s in range(XRING)]

EC = FF_E // 512
EPRODS = [("hg", 0), ("hg", 1), ("ST",)]
EUNITS = []
for _i in range(EC):
    EPRODS += [("G", _i), ("U", _i)] + ([("T", _i - 1)] if _i else [])
    EUNITS += [("g", _i), ("u", _i)]
EPRODS += [("D", 0), ("D", 1), ("T", EC - 1)] + [("SC", g, n) for g in range(G) for n in range(2)]
EUNITS += [("d", _i) for _i in range(EC)]
EPIDX = {n: i for i, n in enumerate(EPRODS)}
EUIDX = {n: i for i, n in enumerate(EUNITS)}
EPER = [len([i for i in range(len(EPRODS)) if i % NB == b]) for b in range(NB)]
EUPER = [len([i for i in range(len(EUNITS)) if i % XRING == s]) for s in range(XRING)]


def build(nc, a, outs):
    y_prompt, y_sample, new_k, new_v, new_state = outs
    with ExitStack() as ctx:
        def sb(name, n, parts=P):
            return ctx.enter_context(nc.sbuf_tensor(name, [parts, n], F32))

        def sem(name):
            return ctx.enter_context(nc.semaphore(name))

        ring = sb("ring", RING * W)
        x = sb("x", G * D)
        hT = sb("hT", KD * T)
        cst = sb("cst", len(CONSTS) * P + 2)
        vecs = sb("vecs", 392)
        condT = sb("condT", 16)
        modT = sb("modT", 48 * G)
        wgda = sb("wgda", KD * 32)
        gdaT = sb("gdaT", T)
        gup = sb("gup", 512)
        z = sb("z", CC * G * ZW)
        A = sb("A", GLA_H * P)
        stat = sb("stat", 64)
        ref = sb("ref", 64)
        route = sb("route", 256)
        flag = ctx.enter_context(nc.sbuf_tensor("flag", [P, 1], I32))
        arena = sb("arena", 27136)
        at = [0]

        def carve(n):
            at[0] += n
            assert at[0] <= 27136
            return arena[:, at[0] - n:at[0]]

        gates = carve(6 * T * 4)
        rows = gates[:, 0:4 * P]
        acc = carve(G * CONV)
        qT, kT = carve(512), carve(512)
        v = carve(G * 512)
        r = carve(G * 512)
        glog = carve(G * 512)
        gtmp = carve(G * 512)
        cum = carve(G * 512)
        pg = carve(6656)
        qarg, karg, klarg, ecum = pg[:, 0:512], pg[:, 512:2560], pg[:, 2560:3072], pg[:, 3072:3584]
        qpad, qepad, ke = pg[:, 3584:4608], pg[:, 4608:5632], pg[:, 5632:6656]
        S0, S1 = carve(512), carve(512)
        o = carve(G * 512)
        qbT = carve(NA_H * T)
        kbT = carve(PAIRS * T)
        vb = carve(G * 512)
        kctxT = carve(512)
        Pm, PT = pg[:, 0:2048], pg[:, 2048:4096]
        bias, kctx = pg[:, 4096:5120], pg[:, 5120:5632]
        kbtok, vctx = qT, kT
        attT = cum
        diag1 = arena[:, 10240:12288]
        gbc1 = pg[:, 0:2048]
        ln1 = arena[:, 8192:10240]
        mtmp = pg[:, 2048:4096]
        at[0] = 0
        xslots = carve((XRING - RING) * W)
        htok = carve(G * D)
        sil, act = carve(1024), carve(1024)
        eT = carve(EC * 4 * P)
        yd = carve(D)
        moe_y = carve(G * D)
        ln2 = carve(2 * D)
        gbc2 = carve(G * D)
        diag2 = eT[:, 0:2048]
        dT = xslots[:, 0:22 * T]
        ftmp = xslots[:, 8192:8192 + 2048]
        hg, S, S2, S2T = hT[:, 0:1024], hT[:, 1024:1280], hT[:, 1280:1536], hT[:, 1536:1792]

        ps = ctx.enter_context(nc.psum_tensor("ps", [P, NB, 512], F32))

        def C(name):
            i = CONSTS.index(name)
            return cst[:, i * P:(i + 1) * P]

        half = [cst[:, len(CONSTS) * P + i:len(CONSTS) * P + i + 1] for i in range(2)]
        ident = C("ident")

        def slot(s):
            return ring[:, s * W:(s + 1) * W] if s < RING else xslots[:, (s - RING) * W:(s - RING + 1) * W]

        bank_full = [sem(f"bank_full{b}") for b in range(NB)]
        bank_free = [sem(f"bank_free{b}") for b in range(NB)]
        w_loaded = [sem(f"w_loaded{s}") for s in range(XRING)]
        down_used, mod_used = sem("down_used"), sem("mod_used")
        consts_in, x_in, vecs_in, wgda_in, gup_in = (sem(n) for n in ("consts_in", "x_in", "vecs_in", "wgda_in", "gup_in"))
        state_in, bias_in, ctx_in, vctx_in, ln_in, router_in = (
            sem(n) for n in ("state_in", "bias_in", "ctx_in", "vctx_in", "ln_in", "router_in"))
        zeroed, stored, kv_stored, state_stored = (sem(n) for n in ("zeroed", "stored", "kv_stored", "state_stored"))
        cond_ready, mod_ready, x_ready, glog_part, glog_soft, glog_ready = (
            sem(n) for n in ("cond_ready", "mod_ready", "x_ready", "glog_part", "glog_soft", "glog_ready"))
        args_ready, exps_ready, gla_ready, A_ready, o_ready, gla_var, gla_std = (
            sem(n) for n in ("args_ready", "exps_ready", "gla_ready", "A_ready", "o_ready", "gla_var", "gla_std"))
        conv_summed, P_arg, P_exp, P_ready, m_ready, var_ready, std_ready = (
            sem(n) for n in ("conv_summed", "P_arg", "P_exp", "P_ready", "m_ready", "var_ready", "std_ready"))
        diag_ready, gate_arg, gate_exp, mask_ready, sel_ready, flag_ready, y_ready = (
            sem(n) for n in ("diag_ready", "gate_arg", "gate_exp", "mask_ready", "sel_ready", "flag_ready", "y_ready"))
        dve_step, act_step, pool_step = sem("dve_step"), sem("act_step"), sem("pool_step")

        def bank(name):
            return ps[:, PIDX[name] % NB, :]

        def await_product(eng, *name):
            i = PIDX[name]
            eng.wait_ge(bank_full[i % NB], i // NB + 1)

        def await_copied(eng, *name):
            i = PIDX[name]
            eng.wait_ge(bank_free[i % NB], i // NB + 1)

        def free(ins, *name):
            ins.then_inc(bank_free[PIDX[name] % NB], 1)

        def ebank(name):
            return ps[:, EPIDX[name] % NB, :]

        def e_await_product(eng, E, *name):
            i = EPIDX[name]
            eng.wait_ge(bank_full[i % NB], E * EPER[i % NB] + (PBASE[i % NB] + i // NB + 1))

        def e_await_copied(eng, E, *name, back=0):
            i = EPIDX[name]
            eng.wait_ge(bank_free[i % NB], E * EPER[i % NB] + (PBASE[i % NB] + i // NB + 1 - back * EPER[i % NB]))

        def e_free(ins, *name):
            ins.then_inc(bank_free[EPIDX[name] % NB], 1)

        class Steps:

            def __init__(self, eng, own):
                self.eng, self.own, self.seen, self.made = eng, own, Counter(), Counter()

            def next(self, s, by=1):
                self.seen[s.name] += by
                self.eng.wait_ge(s, self.seen[s.name])

            def done(self, ins, s=None):
                s = s or self.own
                ins.then_inc(s, 1)
                self.made[s.name] += 1
                self.eng.wait_ge(s, self.made[s.name])

        def freed(eng, ins, *name):
            free(ins, *name)
            await_copied(eng, *name)

        def modcol(c, g):
            return modT[:, 2 * c + g:2 * c + g + 1]

        block = ctx.enter_context(nc.Block())

        def unit_source(name):
            kind = name[0]
            if kind == "mod":
                return a["w_mod"][name[1], :, 512 * name[2]:512 * name[2] + 512].rearrange("(c p) n -> p c n", p=P)
            if kind in SPLIT:
                return a["w_in"][name[1], :, SPLIT[kind]:SPLIT[kind] + 512].rearrange("(c p) n -> p c n", p=P)
            if kind == "br":
                w = a[("w_br_gla", "w_br_na", "w_br_cv")[name[2]]]
                return w[name[1]].rearrange("(c p) n -> p c n", p=P)
            if kind == "out":
                return a["w_out"][name[1], :, 512 * name[2]:512 * name[2] + 512].rearrange("(c p) n -> p c n", p=P)
            f0, fn = FCHUNKS[name[1]]
            if kind == "wd":
                return a["ffd_w_down"][0, f0:f0 + fn, :].rearrange("(c p) n -> p c n", p=P)
            w = a["ffd_w_gate" if kind == "wg" else "ffd_w_up"]
            return w[0, :, f0:f0 + fn].rearrange("(c p) n -> p c n", p=P)

        def unit_shape(name):
            src = unit_source(name)
            return src.shape[1], src.shape[2]

        def unit(name):
            c, n = unit_shape(name)
            return slot(UIDX[name] % RING)[:, 0:c * n].rearrange("p (c n) -> p c n", c=c)

        def e_unit(name):
            c = 4 if name[0] == "d" else 8
            return slot(EUIDX[name] % XRING).rearrange("p (c n) -> p c n", c=c)

        def e_source(name, e):
            f = slice(512 * name[1], 512 * name[1] + 512)
            if name[0] == "d":
                return a["moe_w_down"][0, e, f, :].rearrange("(c p) n -> p c n", p=P)
            return a["moe_w_gate" if name[0] == "g" else "moe_w_up"][0, e, :, f].rearrange("(c p) n -> p c n", p=P)

        @block.sync
        def _(sp):
            for i, name in enumerate(UNITS):
                if i >= RING:
                    before = UNITS[i - RING]
                    if before[0] == "wd" and before[1] < DOWN:
                        sp.wait_ge(down_used, before[1] + 1)
                    elif before[0] == "mod" and before[2] < 11:
                        sp.wait_ge(mod_used, 11 * before[1] + before[2] + 1)
                    else:
                        await_product(sp, *LAST[before])
                sp.dma_start(unit(name), unit_source(name)).then_inc(w_loaded[i % RING], 16)

            def experts(passes):
                with sp.Fori(0, EXPERTS) as e:
                    E = e + EXPERTS * passes
                    for i, name in enumerate(EUNITS):
                        if i >= XRING:
                            b = EUNITS[i - XRING]
                            if b[0] == "d":
                                sp.wait_ge(down_used, E * (EC - 1) + (DOWN + b[1] + 1))
                            else:
                                e_await_product(sp, E, *{"g": ("G", b[1]), "u": ("U", b[1])}[b[0]])
                        else:
                            b = EUNITS[i + len(EUNITS) - XRING]
                            if b[1] < EC - 1:
                                sp.wait_ge(down_used, E * (EC - 1) + (DOWN + b[1] + 1 - (EC - 1)))
                            else:
                                j = EPIDX[("D", 1)]
                                sp.wait_ge(bank_full[j % NB], E * EPER[j % NB] + (PBASE[j % NB] + j // NB + 1 - EPER[j % NB]))
                        sp.dma_start(e_unit(name), e_source(name, e)).then_inc(w_loaded[i % XRING], 16)

            await_product(sp, "h2T", DEPTH - 1, 1, 1)
            sp.wait_ge(kv_stored, 32 * DEPTH)
            experts(0)
            sp.wait_ge(flag_ready, 1)
            over = sp.value_load(flag[0:1, 0:1], min_val=0, max_val=T)
            with sp.If(over > P):
                experts(1)

        @block.gpsimd
        def _(pool):
            pool.dma_start(cst[:, :], a["const_tables"]).then_inc(consts_in, 16)
            cr = rows[:, P:2 * P]
            pool.dma_start(cr[0:KD, :], a["c_ctx"].rearrange("(c p) -> c p", p=P)).then_inc(vecs_in, 16)
            pool.dma_start(cr[KD:2 * KD, :], a["c"].rearrange("b (c p) -> (b c) p", p=P)).then_inc(vecs_in, 16)
            for l in range(DEPTH):
                b = 64 * l
                for name, n in (("b_mod", 48), ("cv_b", 4), ("cv_ln_g", 4), ("cv_ln_b", 4)):
                    pool.dma_start(rows[b:b + n, 0:P], a[name][l].rearrange("(c p) -> c p", p=P)).then_inc(vecs_in, 16)
                    b += n
                pool.dma_start(rows[b:b + 4, 0:P], a["gla_norm"][l]).then_inc(vecs_in, 16)
                pool.dma_start(rows[0:TAPS * CC, (2 + l) * P:(3 + l) * P],
                               a["cv_w"][l].rearrange("t (c p) -> (t c) p", p=P)).then_inc(vecs_in, 16)
            pool.dma_start(x[:, 0:D], a["x_prompt"][0]).then_inc(x_in, 16)
            pool.dma_start(x[:, D:2 * D], a["x_sample"][0]).then_inc(x_in, 16)
            pool.memset(gup[:, :], 0.0).then_inc(pool_step, 1)
            pool.memset(gdaT[:, :], 0.0).then_inc(pool_step, 1)
            pool.memset(z[:, :], 0.0).then_inc(zeroed, 1)
            pool.memset(A[:, :], 0.0).then_inc(zeroed, 1)
            pool.wait_ge(zeroed, 2)
            pool.wait_ge(pool_step, 2)
            pool.memset(gdaT[32:33, :], 1.0).then_inc(zeroed, 1)

            def last_layer_done_with(l, *name):
                if l:
                    await_product(pool, name[0], l - 1, *name[1:])

            def load_mixer(l):
                last_layer_done_with(l, "gda")
                pool.dma_start(wgda[:, :].rearrange("p (c n) -> p c n", c=KD),
                               a["w_in"][l, :, 1536:1568].rearrange("(c p) n -> p c n", p=P)).then_inc(wgda_in, 16)
                last_layer_done_with(l, "glog", 1)
                for n in range(2):
                    pool.dma_start(gup[RANK * n:RANK * n + RANK, 256 * n:256 * n + 256],
                                   a["gla_w_gup"][l, n]).then_inc(gup_in, 16)
                pool.dma_start(gup[32:33, :], a["gla_b_g"][l:l + 1].rearrange("o n k -> o (n k)")).then_inc(gup_in, 16)

            def load_state(l):
                if l:
                    pool.wait_ge(x_ready, 2 * G * l)
                for n in range(2):
                    pool.dma_start(S0[:, 256 * n:256 * n + 256].rearrange("p (h v) -> p h v", h=HP),
                                   a["state_gla"][0, l, n].rearrange("(h a) k v -> (a k) h v", a=2))\
                        .then_inc(state_in, 16)

            def na_loads(l):
                await_product(pool, "o", l, 1)
                pool.dma_start(kctx, a["cache_na_k"][0, l].rearrange("t h d -> t (h d)")).then_inc(ctx_in, 16)
                pool.dma_start(vctx, a["cache_na_v"][0, l].rearrange("t h d -> t (h d)")).then_inc(vctx_in, 16)
                w = a["na_rpb"][l]
                for rq in range(2):
                    for rk in range(2):
                        start = l * NA_H * 15 * 31 + (rk - rq + WIN_R - 1) * 31 + WIN_C - GRID_W
                        toeplitz = bass.AP(w.tensor, start, [[1, GRID_W], [15 * 31, NA_H], [1, GRID_W]])
                        pool.dma_start(bias[64 * rq:64 * rq + 64, :].rearrange("p (h k) -> p h k", h=NA_H)[
                            :, :, 64 * rk:64 * rk + 64], toeplitz).then_inc(bias_in, 16)

            def load_ln(dst, l, j):
                for i, name in enumerate(("ln_g", "ln_b")):
                    w = a[name][l, j]
                    pool.dma_start(dst[:, i * D:(i + 1) * D],
                                   bass.AP(w.tensor, (l * 2 + j) * D, [[0, P], [1, D]])).then_inc(ln_in, 16)

            def load_router():
                await_product(pool, "gda", DEPTH - 1)
                pool.dma_start(wgda[:, 0:KD * EXPERTS].rearrange("p (c n) -> p c n", c=KD),
                               a["moe_w_router"][0].rearrange("(c p) n -> p c n", p=P)).then_inc(router_in, 16)

            for l in range(DEPTH):
                load_mixer(l)
                load_state(l)
                await_copied(pool, "vb", l, 0)
                pool.dma_start(new_v[0, l].rearrange("t h d -> t (h d)"), vb[:, 0:512]).then_inc(kv_stored, 16)
                await_copied(pool, "kv", l, 0, 0)
                await_copied(pool, "kv", l, 0, 1)
                for n in range(2):
                    pool.dma_start(new_state[0, l, n].rearrange("(h a) k v -> (a k) h v", a=2),
                                   qarg[:, 256 * n:256 * n + 256].rearrange("p (h v) -> p h v", h=HP))\
                        .then_inc(state_stored, 16)
                na_loads(l)
                await_product(pool, "oT", l, 1)
                load_ln(ln1, l, 0)
                await_copied(pool, "kbtok", l)
                pool.dma_start(new_k[0, l].rearrange("t h d -> t (h d)"), kbtok).then_inc(kv_stored, 16)
                if l == DEPTH - 1:
                    load_router()
                await_product(pool, "h2T", l, 1, 1)
                pool.wait_ge(kv_stored, 32 * (l + 1))
                load_ln(ln2, l, 1)
            for g, out in enumerate((y_prompt, y_sample)):
                pool.wait_ge(y_ready, g + 1)
                pool.dma_start(out[0], x[:, g * D:(g + 1) * D]).then_inc(stored, 16)
            pool.wait_ge(stored, 32)
            pool.wait_ge(state_stored, 32 * DEPTH)
            pool.wait_ge(kv_stored, 32 * DEPTH)

        @block.tensor
        def _(pe):
            st = Steps(pe, None)

            def claim(*name):
                i = PIDX[name]
                if i >= NB:
                    pe.wait_ge(bank_free[i % NB], i // NB)
                return bank(name)

            def full(ins, *name):
                ins.then_inc(bank_full[PIDX[name] % NB], 1)

            def arrived(name):
                i = UIDX[name]
                pe.wait_ge(w_loaded[i % RING], 16 * (i // RING + 1))
                return unit(name)

            mm = nc.tensor.matmul
            tr = nc.tensor.transpose

            def tokens_times(name, lhs, w, n=512, ks=KD, n0=0):
                o_ = claim(*name)
                for k in range(ks):
                    ins = mm(o_[:, 0:n], lhs(k), w[:, k, n0:n0 + n], start=(k == 0), stop=(k == ks - 1))
                full(ins, *name)

            def hTk(g):
                return lambda k: hT[:, k * T + g * P:k * T + g * P + P]

            def features(name, w, chunks):
                o_ = claim(*name)
                for j, c in enumerate(chunks):
                    for k in range(KD):
                        ins = mm(o_[:, j * T:(j + 1) * T], w[:, k, c * P:(c + 1) * P], hT[:, k * T:(k + 1) * T],
                                 start=(k == 0), stop=(k == KD - 1))
                full(ins, *name)

            def turned(name, sources, rows_=P):
                o_ = claim(*name)
                for j, s in enumerate(sources):
                    ins = tr(o_[:, j * P:j * P + rows_], s, ident[0:rows_, 0:rows_])
                full(ins, *name)

            def copied(*name):
                await_copied(pe, *name)

            pe.wait_ge(consts_in, 16)
            pe.wait_ge(vecs_in, 16 * 14)
            o_ = claim("vecs")
            tr(o_[:, 0:128], rows[:, 0:P], ident)
            tr(o_[:, 128:144], rows[0:16, P:2 * P], ident[0:16, 0:16])
            tr(o_[:, 144:268], rows[0:124, 2 * P:3 * P], ident[0:124, 0:124])
            full(tr(o_[:, 268:392], rows[0:124, 3 * P:4 * P], ident[0:124, 0:124]), "vecs")

            for l in range(DEPTH):
                pe.wait_ge(cond_ready, 1)
                o_ = claim("mod", l)
                for i in range(12):
                    w = arrived(("mod", l, i))
                    for j in range(4):
                        c = 4 * i + j
                        for k in range(KD):
                            ins = mm(o_[:, 2 * c:2 * c + 2], w[:, k, j * P:(j + 1) * P], condT[:, k:16:KD],
                                     start=(k == 0), stop=(k == KD - 1))
                    if i < 11:
                        ins.then_inc(mod_used, 1)
                full(ins, "mod", l)

                for g in range(G):
                    if l == 0:
                        pe.wait_ge(x_in, 32)
                    else:
                        pe.wait_ge(x_ready, 2 * G * l - G + g + 1)
                    for h in range(2):
                        turned(("hT", l, g, h), [x[:, g * D + (4 * h + j) * P:g * D + (4 * h + j + 1) * P] for j in range(4)])
                for g in range(G):
                    copied("hT", l, g, 0), copied("hT", l, g, 1)
                w = arrived(("cva", l))
                features(("cva", l, 0), w, (0, 1)), features(("cva", l, 1), w, (2, 3))
                w = arrived(("cvg", l))
                features(("cvg", l, 0), w, (0, 1)), features(("cvg", l, 1), w, (2, 3))
                pe.wait_ge(wgda_in, 16 * (l + 1))
                o_ = claim("gda", l)
                for k in range(KD):
                    ins = mm(o_[0:32, 0:T], wgda[:, k * 32:(k + 1) * 32], hT[:, k * T:(k + 1) * T],
                             start=(k == 0), stop=(k == KD - 1))
                full(ins, "gda", l)
                w = arrived(("qk", l))
                features(("q", l), w, (0, 1)), features(("k", l), w, (2, 3))
                copied("gda", l)
                pe.wait_ge(zeroed, 3)
                pe.wait_ge(gup_in, 48 * (l + 1))
                for g in range(G):
                    o_ = claim("glog", l, g)
                    full(mm(o_, gdaT[:, g * P:(g + 1) * P], gup[:, :], start=True, stop=True), "glog", l, g)
                w = arrived(("v", l))
                tokens_times(("v", l, 0), hTk(0), w), tokens_times(("v", l, 1), hTk(1), w)
                o_ = claim("rope", l)
                copied("q", l), copied("k", l)
                for j in range(4):
                    s = (qT, kT)[j // 2][:, (j % 2) * T + P:(j % 2) * T + T]
                    ins = mm(o_[:, j * P:(j + 1) * P], C("rot"), s, start=True, stop=True)
                full(ins, "rope", l)
                for g in range(G):
                    o_ = claim("cum", l, g)
                    pe.wait_ge(glog_ready, G * l + g + 1)
                    for dr in range(2):
                        for hp in range(HP):
                            j = dr * HP + hp
                            ins = mm(o_[:, j * P:(j + 1) * P], glog[:, g * 512 + j * P:g * 512 + (j + 1) * P],
                                     C("tri_f" if dr == 0 else "tri_b"), start=True, stop=True)
                    full(ins, "cum", l, g)
                for n in ("qb", "kb"):
                    w = arrived((n, l))
                    features((n, l, 0), w, (0, 1)), features((n, l, 1), w, (2, 3))

                def gla_scores(g):
                    pe.wait_ge(gla_ready, G * l + g + 1)
                    turned(("keT", l, g), [klarg[:, j * P:(j + 1) * P] for j in range(4)])
                    k5 = karg.rearrange("p (n h b s) -> p n h b s", n=2, h=HP, b=8)
                    q5 = qpad.rearrange("p (n h a t) -> p n h a t", n=2, h=HP, a=2)
                    for dr in range(2):
                        o4 = claim("att", l, g, dr).rearrange("s (h a t) -> s h a t", h=HP, a=2)
                        for hp in range(HP):
                            for b in range(8):
                                c = b // 4
                                ins = mm(o4[64 * c:64 * c + 64, hp, :, b * SUB:(b + 1) * SUB], k5[:, dr, hp, b, :],
                                         q5[:, dr, hp, :, b * SUB:(b + 1) * SUB], start=True, stop=True)
                        full(ins, "att", l, g, dr)

                def gla_states(g):
                    copied("keT", l, g)
                    copied("v", l, g)
                    for dr in range(2):
                        o_ = claim("kv", l, g, dr)
                        for c in range(2):
                            for hp in range(HP):
                                for s in range(2):
                                    j = c * HP + hp
                                    k0 = c * 512 + (dr * HP + hp) * P + 64 * s
                                    ins = mm(o_[64 * s:64 * s + 64, j * P:(j + 1) * P], ke[:, k0:k0 + 64],
                                             v[:, g * 512 + (2 * hp + s) * P:g * 512 + (2 * hp + s + 1) * P],
                                             start=True, stop=True)
                        full(ins, "kv", l, g, dr)

                def gla_out(g):
                    pe.wait_ge(A_ready, G * l + g + 1)
                    copied("kv", l, g, 0), copied("kv", l, g, 1)
                    o_ = claim("o", l, g)
                    qe = qepad.rearrange("p (n h a t) -> p n h a t", n=2, h=HP, a=2)
                    for h in range(GLA_H):
                        hp, s = h // 2, h % 2
                        terms = [(0, 1, S1), (1, 0, S1)] + ([(0, 0, S0), (1, 1, S0)] if g == 1 else [])
                        mm(o_[:, h * P:(h + 1) * P], A[:, h * P:(h + 1) * P],
                           v[:, g * 512 + h * P:g * 512 + (h + 1) * P], start=True, stop=False, skip_group_check=True)
                        for n, (dr, c, state) in enumerate(terms):
                            ins = mm(o_[64 * c:64 * c + 64, h * P:(h + 1) * P], qe[:, dr, hp, s, 64 * c:64 * c + 64],
                                     state[:, (dr * HP + hp) * P:(dr * HP + hp + 1) * P],
                                     start=False, stop=(n == len(terms) - 1), skip_group_check=True)
                    full(ins, "o", l, g)

                def gla_turn(g):
                    pe.wait_ge(o_ready, G * l + g + 1)
                    turned(("oT", l, g), [o[:, g * 512 + j * P:g * 512 + (j + 1) * P] for j in range(4)])

                def mgate(n):
                    w = arrived((MG[n], l))
                    tokens_times(("mg", l, 0, n), hTk(0), w), tokens_times(("mg", l, 1, n), hTk(1), w)

                gla_scores(0)
                w = arrived(("vb", l))
                tokens_times(("vb", l, 0), hTk(0), w), tokens_times(("vb", l, 1), hTk(1), w)
                gla_states(0)
                w = arrived(("r", l))
                tokens_times(("r", l, 0), hTk(0), w), tokens_times(("r", l, 1), hTk(1), w)
                gla_out(0)
                mgate(0)
                gla_turn(0)
                mgate(1)
                gla_scores(1)
                mgate(2)
                gla_states(1)
                mgate(3)
                gla_out(1)
                mgate(4)
                gla_turn(1)
                mgate(5)
                turned(("kbtok", l), [kbT[:, j * T:j * T + P] for j in range(4)])
                pe.wait_ge(ctx_in, 16 * (l + 1))
                turned(("kctxT", l), [kctx[:, j * P:(j + 1) * P] for j in range(4)])
                pe.wait_ge(bias_in, 64 * (l + 1))
                for i in range(2):
                    full(mm(claim("bias", l, i), C("flip"), bias[:, i * 512:(i + 1) * 512], start=True, stop=True),
                         "bias", l, i)
                for i in range(2):
                    o_ = claim("sc", l, 0, i)
                    for j in range(4):
                        h = 4 * i + j
                        ins = mm(o_[:, j * P:(j + 1) * P], qbT[:, h * T:h * T + P],
                                 kbT[:, (h // 2) * T:(h // 2) * T + P], start=True, stop=True)
                    full(ins, "sc", l, 0, i)
                for g in range(G):
                    pe.wait_ge(conv_summed, l + 1)
                    turned(("cvtok", l, g), [acc[:, g * 512 + j * P:g * 512 + (j + 1) * P] for j in range(4)])
                for g in range(G):
                    copied("cvtok", l, g)
                    turned(("cvT", l, g), [acc[:, g * 512 + j * P:g * 512 + (j + 1) * P] for j in range(4)])
                pe.wait_ge(P_ready, G * l + 1)
                for i in range(2):
                    turned(("PT", l, 0, i), [Pm[:, (4 * i + j) * P:(4 * i + j + 1) * P] for j in range(4)])
                copied("kctxT", l)
                for i in range(4):
                    o_ = claim("sc", l, 1, i)
                    for j in range(2):
                        h = 2 * i + j
                        q = qbT[:, h * T + P:h * T + T]
                        mm(o_[:, j * T:j * T + P], q, kbT[:, (h // 2) * T + P:(h // 2) * T + T], start=True, stop=True)
                        ins = mm(o_[:, j * T + P:(j + 1) * T], q, kctxT[:, (h // 2) * P:(h // 2 + 1) * P],
                                 start=True, stop=True)
                    full(ins, "sc", l, 1, i)

                def branch(b, src):
                    w = arrived(("br", l, b))
                    for g in range(G):
                        for n in range(2):
                            tokens_times(("y", l, b, g, n), (lambda k, g=g: src(g, k)), w, ks=4, n0=512 * n)

                copied("oT", l, 0), copied("oT", l, 1)
                branch(0, lambda g, k: o[:, g * 512 + k * P:g * 512 + (k + 1) * P])
                copied("cvT", l, 0), copied("cvT", l, 1)
                branch(2, lambda g, k: acc[:, g * 512 + k * P:g * 512 + (k + 1) * P])

                def na_values(g):
                    o_ = claim("attT", l, g)
                    if g:
                        pe.wait_ge(vctx_in, 16 * (l + 1))
                    kinds = 1 + g
                    for i in range(4 if g else 2):
                        copied("PT", l, g, i)
                    for h in range(NA_H):
                        for n in range(kinds):
                            val = (vb[:, g * 512:(g + 1) * 512] if n == 0 else vctx)[:, h * NA_DH:(h + 1) * NA_DH]
                            ins = mm(o_[64 * (h % 2):64 * (h % 2) + 64, (h // 2) * P:(h // 2 + 1) * P], val,
                                     PT[:, (h * kinds + n) * P:(h * kinds + n + 1) * P],
                                     start=(n == 0), stop=(n == kinds - 1))
                    full(ins, "attT", l, g)

                na_values(0)
                pe.wait_ge(P_ready, G * l + 2)
                for i in range(4):
                    turned(("PT", l, 1, i), [Pm[:, (4 * i + j) * P:(4 * i + j + 1) * P] for j in range(4)])
                na_values(1)
                copied("attT", l, 0), copied("attT", l, 1)
                branch(1, lambda g, k: attT[:, g * 512 + k * P:g * 512 + (k + 1) * P])

                def gate_rows(j, d):
                    pe.wait_ge(diag_ready, 2 * l + j + 1)
                    for g in range(G):
                        for n in range(2):
                            o_ = claim("gbc", l, j, g, n)
                            full(mm(o_, C("ones"), d[:, g * D + 512 * n:g * D + 512 * n + 512],
                                    start=True, stop=True), "gbc", l, j, g, n)

                gate_rows(0, diag1)
                for g in range(G):
                    pe.wait_ge(m_ready, G * l + g + 1)
                    for h in range(2):
                        turned(("mT", l, g, h), [gates[:, g * 3 * D + (4 * h + j) * P:g * 3 * D + (4 * h + j + 1) * P]
                                                 for j in range(4)])
                for g in range(G):
                    copied("mT", l, g, 0), copied("mT", l, g, 1)
                for n in range(2):
                    w = arrived(("out", l, n))
                    for g in range(G):
                        tokens_times(("mix", l, g, n), hTk(g), w)
                for g in range(G):
                    pe.wait_ge(x_ready, 2 * G * l + g + 1)
                    for h in range(2):
                        turned(("h2T", l, g, h), [x[:, g * D + (4 * h + j) * P:g * D + (4 * h + j + 1) * P] for j in range(4)])
                gate_rows(1, diag2)
                for g in range(G):
                    copied("h2T", l, g, 0), copied("h2T", l, g, 1)

                if l == 0:
                    def dense_turn(i):
                        for g in range(G):
                            copied("U", i, g)
                            b = act[:, g * 512:(g + 1) * 512]
                            turned(("aT", i, g), [b[:, j * P:(j + 1) * P] for j in range(FCHUNKS[i][1] // P)])

                    for i, (f0, fn) in enumerate(FCHUNKS):
                        w = arrived(("wg", i))
                        for g in range(G):
                            tokens_times(("G", i, g), hTk(g), w, n=fn)
                        w = arrived(("wu", i))
                        for g in range(G):
                            o_ = claim("U", i, g)
                            for k in range(KD):
                                ins = mm(o_[:, 0:fn], hTk(g)(k), w[:, k, :], start=(k == 0), stop=(k == KD - 1))
                            full(ins, "U", i, g)
                        if i:
                            dense_turn(i - 1)
                    dense_turn(len(FCHUNKS) - 1)
                    ys = {(g, n): claim("Y", g, n) for g in range(G) for n in range(2)}
                    for i, (f0, fn) in enumerate(FCHUNKS):
                        w = arrived(("wd", i))
                        for g in range(G):
                            copied("aT", i, g)
                        for c in range(fn // P):
                            f = f0 // P + c
                            end = f == FF_D // P - 1
                            for g in range(G):
                                for n in range(2):
                                    ins = mm(ys[g, n], dT[:, f * T + g * P:f * T + (g + 1) * P],
                                             w[:, c, 512 * n:512 * n + 512], start=(f == 0), stop=end)
                                    if end:
                                        full(ins, "Y", g, n)
                        if not end:
                            ins.then_inc(down_used, 1)
                else:
                    for g in range(G):
                        for h in range(2):
                            turned(("htok", g, h), [hTk(g)(4 * h + j) for j in range(4)])
                    pe.wait_ge(router_in, 16)
                    o_ = claim("logits")
                    for g in range(G):
                        for k in range(KD):
                            ins = mm(o_[:, 8 * g:8 * g + 8], hTk(g)(k), wgda[:, 8 * k:8 * k + 8],
                                     start=(k == 0), stop=(k == KD - 1))
                    full(ins, "logits")
                    o_ = claim("rank")
                    pe.wait_ge(mask_ready, 1)
                    m0, m1 = route[:, 64:72], route[:, 72:80]
                    mm(o_[:, 0:8], C("before"), m0, start=True, stop=True)
                    mm(o_[:, 8:16], C("before"), m1, start=True, stop=False)
                    mm(o_[:, 8:16], C("ones"), m0, start=False, stop=True)
                    mm(o_[:, 16:24], C("ones"), m0, start=True, stop=False)
                    full(mm(o_[:, 16:24], C("ones"), m1, start=False, stop=True), "rank")

            def e_claim(E, *name):
                i = EPIDX[name]
                pe.wait_ge(bank_free[i % NB], E * EPER[i % NB] + (PBASE[i % NB] + i // NB))
                return ebank(name)

            def e_full(ins, *name):
                ins.then_inc(bank_full[EPIDX[name] % NB], 1)

            def e_arrived(E, *name):
                i = EUIDX[name]
                s = i % XRING
                pe.wait_ge(w_loaded[s], E * (16 * EUPER[s]) + 16 * (UBASE[s] + i // XRING + 1))
                return e_unit(name)

            def experts(passes):
                with pe.Fori(0, EXPERTS) as e:
                    E = e + EXPERTS * passes
                    pe.wait_ge(sel_ready, E + 1)
                    for h in range(2):
                        o_ = e_claim(E, "hg", h)
                        for j in range(4):
                            for g in range(G):
                                ins = mm(o_[:, j * P:(j + 1) * P], htok[:, g * D + (4 * h + j) * P:g * D + (4 * h + j + 1) * P],
                                         S[:, g * P:(g + 1) * P], start=(g == 0), stop=(g == 1))
                        e_full(ins, "hg", h)
                    o_ = e_claim(E, "ST")
                    for g in range(G):
                        ins = tr(o_[:, g * P:(g + 1) * P], S2[:, g * P:(g + 1) * P], ident)
                    e_full(ins, "ST")
                    e_await_copied(pe, E, "hg", 0)
                    e_await_copied(pe, E, "hg", 1)

                    def turn(i):
                        o_ = e_claim(E, "T", i)
                        e_await_copied(pe, E, "U", i)
                        for j in range(4):
                            ins = tr(o_[:, j * P:(j + 1) * P], act[:, (i % 2) * 512 + j * P:(i % 2) * 512 + (j + 1) * P], ident)
                        e_full(ins, "T", i)

                    for i in range(EC):
                        for kind, pn in (("g", "G"), ("u", "U")):
                            w = e_arrived(E, kind, i)
                            o_ = e_claim(E, pn, i)
                            for k in range(KD):
                                ins = mm(o_, hg[:, k * P:(k + 1) * P], w[:, k, :], start=(k == 0), stop=(k == KD - 1))
                            e_full(ins, pn, i)
                        if i:
                            turn(i - 1)
                    ds = [e_claim(E, "D", 0), e_claim(E, "D", 1)]
                    for i in range(EC):
                        if i == EC - 1:
                            turn(i)
                        w = e_arrived(E, "d", i)
                        e_await_copied(pe, E, "T", i)
                        for c in range(4):
                            f = 4 * i + c
                            end = f == 4 * EC - 1
                            for n in range(2):
                                ins = mm(ds[n], eT[:, f * P:(f + 1) * P], w[:, c, 512 * n:512 * n + 512],
                                         start=(f == 0), stop=end)
                                if end:
                                    e_full(ins, "D", n)
                        if not end:
                            ins.then_inc(down_used, 1)
                    e_await_copied(pe, E, "ST")
                    e_await_copied(pe, E, "D", 0)
                    e_await_copied(pe, E, "D", 1)
                    for g in range(G):
                        for n in range(2):
                            o_ = e_claim(E, "SC", g, n)
                            e_full(mm(o_, S2T[:, g * P:(g + 1) * P], yd[:, 512 * n:512 * n + 512],
                                      start=True, stop=True), "SC", g, n)

            for h in range(2):
                for g in range(G):
                    copied("htok", g, h)
            experts(0)
            pe.wait_ge(flag_ready, 1)
            over = pe.value_load(flag[0:1, 0:1], min_val=0, max_val=T)
            with pe.If(over > P):
                experts(1)

        @block.scalar
        def _(sc):
            st = Steps(sc, act_step)
            act_ = nc.scalar.activation

            def take(out, name, func=ACT.Copy, src=None, **kw):
                await_product(sc, *name)
                free(act_(out, bank(name) if src is None else src, func, **kw), *name)

            await_copied(sc, "vecs")
            act_(condT[:, :], vecs[:, 128:144], ACT.Silu).then_inc(cond_ready, 1)

            for l in range(DEPTH):
                def modulated(kind, sh, scl):
                    for g in range(G):
                        await_product(sc, kind, l, g, 1)
                        for j in range(4):
                            k = 4 + j
                            ins = act_(hT[:, k * T + g * P:k * T + (g + 1) * P], bank((kind, l, g, 1))[:, j * P:(j + 1) * P],
                                       ACT.Identity, bias=modcol(sh + k, g), scale=modcol(scl + k, g))
                        free(ins, kind, l, g, 1)

                def norm_sqrt(n):
                    for _ in range(n):
                        st.next(var_ready)
                        act_(stat[:, 40:41], stat[:, 39:40], ACT.Sqrt).then_inc(std_ready, 1)

                st.next(mod_ready)
                modulated("hT", 0, 8)
                for i in range(2):
                    take(gtmp[:, i * 512:(i + 1) * 512], ("cvg", l, i), ACT.Sigmoid)
                take(kT, ("k", l))
                for g in range(G):
                    s = gtmp[:, g * 512:(g + 1) * 512]
                    st.next(glog_part)
                    st.done(act_(s, s, ACT.Exp))
                    act_(s, s, ACT.Ln, bias=1.0).then_inc(glog_soft, 1)
                for g in range(G):
                    take(v[:, g * 512:(g + 1) * 512], ("v", l, g))
                for i in range(2):
                    await_product(sc, "qb", l, i)
                    for j in range(2):
                        for s in range(2):
                            h = 2 * (2 * i + j) + s
                            ins = act_(qbT[:, h * T:(h + 1) * T], bank(("qb", l, i))[:, j * T:(j + 1) * T], ACT.Copy,
                                       scale=half[s])
                    free(ins, "qb", l, i)
                for i in range(2):
                    take(kbT[:, i * 512:(i + 1) * 512], ("kb", l, i))

                def gla_exps(g):
                    st.next(args_ready)
                    act_(qarg, qarg, ACT.Exp)
                    act_(ecum, cum[:, g * 512:(g + 1) * 512], ACT.Exp)
                    act_(klarg, klarg, ACT.Exp)
                    act_(karg, karg, ACT.Exp).then_inc(exps_ready, 1)

                def gla_keys(g):
                    await_product(sc, "keT", l, g)
                    for c in range(2):
                        ins = act_(ke[:, c * 512:(c + 1) * 512], bank(("keT", l, g)), ACT.Copy, scale=half[c])
                    free(ins, "keT", l, g)

                def gla_turned(g):
                    await_product(sc, "oT", l, g)
                    for j in range(4):
                        ins = act_(o[:, g * 512 + j * P:g * 512 + (j + 1) * P], bank(("oT", l, g))[:, j * P:(j + 1) * P],
                                   ACT.Copy, scale=vecs[:, 64 * l + 60 + j:64 * l + 61 + j])
                    free(ins, "oT", l, g)

                def mgate(n):
                    for g in range(G):
                        take(gates[:, g * 3 * D + n * 512:g * 3 * D + (n + 1) * 512], ("mg", l, g, n), ACT.Sigmoid)

                def gla_sqrt():
                    st.next(gla_var)
                    act_(stat[:, 50:54], stat[:, 42:46], ACT.Sqrt).then_inc(gla_std, 1)

                gla_exps(0)
                gla_keys(0)
                for g in range(G):
                    take(vb[:, g * 512:(g + 1) * 512], ("vb", l, g))
                for g in range(G):
                    take(r[:, g * 512:(g + 1) * 512], ("r", l, g), ACT.Silu)
                gla_sqrt()
                mgate(0)
                gla_turned(0)
                mgate(1)
                gla_exps(1)
                gla_keys(1)
                mgate(2)
                mgate(3)
                gla_sqrt()
                mgate(4)
                gla_turned(1)
                mgate(5)
                take(kbtok, ("kbtok", l))
                take(kctxT, ("kctxT", l))
                norm_sqrt(2)

                def softmax_exp(n):
                    st.next(P_arg)
                    act_(Pm[:, 0:n], Pm[:, 0:n], ACT.Exp).then_inc(P_exp, 1)

                for g in range(G):
                    await_product(sc, "cvT", l, g)
                    for j in range(4):
                        ins = act_(acc[:, g * 512 + j * P:g * 512 + (j + 1) * P], bank(("cvT", l, g))[:, j * P:(j + 1) * P],
                                   ACT.Silu, scale=vecs[:, 64 * l + 52 + j:64 * l + 53 + j],
                                   bias=vecs[:, 64 * l + 56 + j:64 * l + 57 + j])
                    free(ins, "cvT", l, g)
                softmax_exp(1024)
                for i in range(2):
                    take(PT[:, i * 512:(i + 1) * 512], ("PT", l, 0, i))
                softmax_exp(2048)
                take(attT[:, 0:512], ("attT", l, 0))
                for i in range(4):
                    take(PT[:, i * 512:(i + 1) * 512], ("PT", l, 1, i))
                take(attT[:, 512:1024], ("attT", l, 1))
                for g in range(G):
                    for n in range(2):
                        take(gbc1[:, g * D + n * 512:g * D + (n + 1) * 512], ("gbc", l, 0, g, n))
                for g in range(G):
                    for h in range(2):
                        await_product(sc, "mT", l, g, h)
                        for j in range(4):
                            k = 4 * h + j
                            ins = act_(hT[:, k * T + g * P:k * T + (g + 1) * P], bank(("mT", l, g, h))[:, j * P:(j + 1) * P],
                                       ACT.Copy)
                        free(ins, "mT", l, g, h)
                norm_sqrt(2)
                modulated("h2T", 24, 32)
                sc.wait_ge(kv_stored, 32 * (l + 1))
                for g in range(G):
                    for n in range(2):
                        take(gbc2[:, g * D + n * 512:g * D + (n + 1) * 512], ("gbc", l, 1, g, n))
                if l == 0:
                    def dense_turned(i):
                        for g in range(G):
                            await_product(sc, "aT", i, g)
                            for j in range(FCHUNKS[i][1] // P):
                                f = FCHUNKS[i][0] // P + j
                                ins = act_(dT[:, f * T + g * P:f * T + (g + 1) * P], bank(("aT", i, g))[:, j * P:(j + 1) * P],
                                           ACT.Copy)
                            free(ins, "aT", i, g)

                    for i, (f0, fn) in enumerate(FCHUNKS):
                        for g in range(G):
                            if i:
                                await_copied(sc, "U", i - 1, g)
                            take(sil[:, g * 512:g * 512 + fn], ("G", i, g), ACT.Silu, src=bank(("G", i, g))[:, 0:fn])
                        if i:
                            dense_turned(i - 1)
                    dense_turned(len(FCHUNKS) - 1)
                    norm_sqrt(2)
                else:
                    for g in range(G):
                        for h in range(2):
                            take(htok[:, g * D + h * 512:g * D + (h + 1) * 512], ("htok", g, h))
                    st.next(gate_arg)
                    act_(route[:, 100:102], route[:, 98:100], ACT.Exp).then_inc(gate_exp, 1)

            def experts(passes):
                with sc.Fori(0, EXPERTS) as e:
                    E = e + EXPERTS * passes

                    def e_take(out, *name, func=ACT.Copy, src=None):
                        e_await_product(sc, E, *name)
                        e_free(act_(out, ebank(name) if src is None else src, func), *name)

                    for h in range(2):
                        e_take(hg[:, h * 512:(h + 1) * 512], "hg", h)
                    e_take(S2T, "ST", src=ebank(("ST",))[:, 0:256])

                    def gated(i):
                        if i >= 2:
                            e_await_copied(sc, E, "U", i - 2)
                        else:
                            e_await_copied(sc, E, "U", EC - 1 if i == 0 else EC - 2, back=1)
                        e_take(sil[:, (i % 2) * 512:(i % 2 + 1) * 512], "G", i, func=ACT.Silu)

                    def turned(i):
                        e_take(eT[:, i * 512:(i + 1) * 512], "T", i)

                    for i in range(EC):
                        gated(i)
                        if i:
                            turned(i - 1)
                    turned(EC - 1)
                    e_take(yd[:, 512:1024], "D", 1)

            experts(0)
            sc.wait_ge(flag_ready, 1)
            over = sc.value_load(flag[0:1, 0:1], min_val=0, max_val=T)
            with sc.If(over > P):
                experts(1)
            for _ in range(G):
                st.next(var_ready)
                act_(stat[:, 40:41], stat[:, 39:40], ACT.Sqrt).then_inc(std_ready, 1)

        @block.vector
        def _(dv):
            st = Steps(dv, dve_step)
            V = nc.vector

            def lag(ins, n):
                ins.then_inc(dve_step, 1)
                st.made[dve_step.name] += 1
                if st.made[dve_step.name] > n:
                    dv.wait_ge(dve_step, st.made[dve_step.name] - n)

            def settle():
                dv.wait_ge(dve_step, st.made[dve_step.name])

            def rstd(src_var, out):
                st.done(V.tensor_scalar(stat[:, 39:40], src_var, EPS, None, ALU.add), var_ready)
                st.next(std_ready)
                st.done(V.reciprocal(out, stat[:, 40:41]))

            def moments(halves):
                for i, h in enumerate(halves):
                    st.done(V.bn_stats(stat[:, 6 * i:6 * i + 6], h))
                st.done(V.bn_aggr(stat[:, 36:38], stat[:, 0:6 * len(halves)]))

            def layer_norm(xg, gain, bias_, sig):
                moments([xg[:, 0:512], xg[:, 512:1024]])
                rstd(stat[:, 37:38], stat[:, 38:39])
                st.done(V.tensor_scalar(xg, xg, stat[:, 36:37], stat[:, 38:39], ALU.subtract, ALU.mult))
                st.done(V.tensor_tensor(xg, xg, gain, ALU.mult))
                st.done(V.tensor_tensor(xg, xg, bias_, ALU.add), sig)

            await_product(dv, "vecs")
            freed(dv, V.tensor_copy(vecs[:, :], bank(("vecs",))[:, 0:392]), "vecs")

            for l in range(DEPTH):
                vl = 64 * l
                await_product(dv, "mod", l)
                mod3 = modT[:, :].rearrange("p (c g) -> p c g", g=G)
                freed(dv, V.tensor_tensor(mod3, bank(("mod", l))[:, 0:96].rearrange("p (c g) -> p c g", g=G),
                                          vecs[:, vl:vl + 48].unsqueeze(2).to_broadcast([P, 48, G]), ALU.add), "mod", l)
                st.done(V.tensor_scalar(modT[:, 16:32], modT[:, 16:32], 1.0, None, ALU.add))
                st.done(V.tensor_scalar(modT[:, 64:80], modT[:, 64:80], 1.0, None, ALU.add), mod_ready)

                def modulated(kind, sh, scl):
                    for g in range(G):
                        await_product(dv, kind, l, g, 0)
                        for k in range(4):
                            ins = V.tensor_scalar(hT[:, k * T + g * P:k * T + (g + 1) * P],
                                                  bank((kind, l, g, 0))[:, k * P:(k + 1) * P],
                                                  modcol(scl + k, g), modcol(sh + k, g), ALU.mult, ALU.add)
                        free(ins, kind, l, g, 0)

                modulated("hT", 0, 8)
                dv.wait_ge(zeroed, 3)
                z4 = z[:, :].rearrange("p (c g w) -> p c g w", c=CC, g=G)
                for i in range(2):
                    await_copied(dv, "cvg", l, i)
                    await_product(dv, "cva", l, i)
                    for j in range(2):
                        ins = V.tensor_tensor(z4[:, 2 * i + j, :, TAPS // 2:TAPS // 2 + P],
                                              bank(("cva", l, i))[:, j * T:(j + 1) * T].rearrange("p (g t) -> p g t", g=G),
                                              gtmp[:, i * 512 + j * T:i * 512 + (j + 1) * T].rearrange("p (g t) -> p g t", g=G),
                                              ALU.mult)
                    freed(dv, ins, "cva", l, i)
                await_product(dv, "gda", l)
                free(V.tensor_copy(gdaT[0:32, :], bank(("gda", l))[0:32, 0:T]), "gda", l)
                await_product(dv, "q", l)
                if l:
                    dv.wait_ge(kv_stored, 32 * l)
                freed(dv, V.tensor_scalar(qT, bank(("q", l)), GLA_DK ** -0.5, None, ALU.mult), "q", l)
                for g in range(G):
                    lg, tmp = glog[:, g * 512:(g + 1) * 512], gtmp[:, g * 512:(g + 1) * 512]
                    await_product(dv, "glog", l, g)
                    freed(dv, V.tensor_copy(lg, bank(("glog", l, g))), "glog", l, g)
                    st.done(V.scalar_tensor_tensor(out=tmp, in0=lg, scalar=-1.0, in1=lg, op0=ALU.mult, op1=ALU.min),
                            glog_part)
                for g in range(G):
                    lg, tmp = glog[:, g * 512:(g + 1) * 512], gtmp[:, g * 512:(g + 1) * 512]
                    st.next(glog_soft)
                    st.done(V.scalar_tensor_tensor(out=lg, in0=lg, scalar=0.0, in1=tmp, op0=ALU.min, op1=ALU.subtract),
                            glog_ready)
                await_copied(dv, "k", l)
                await_product(dv, "rope", l)
                o4 = bank(("rope", l)).rearrange("p (w h t) -> p w h t", w=2, h=HP)
                tmp = gtmp[:, 0:512].rearrange("p (w h t) -> p w h t", w=2, h=HP)
                sin_b = C("sin").unsqueeze(1).to_broadcast([P, 4, P])
                cos_b = C("cos").unsqueeze(1).to_broadcast([P, HP, P])
                freed(dv, V.tensor_tensor(gtmp[:, 0:512].rearrange("p (w t) -> p w t", w=4),
                                          bank(("rope", l)).rearrange("p (w t) -> p w t", w=4), sin_b, ALU.mult), "rope", l)
                for n, w in enumerate((qT, kT)):
                    s = w.rearrange("p (h t) -> p h t", h=HP)[:, :, P:T]
                    st.done(V.tensor_tensor(s, s, cos_b, ALU.mult))
                    st.done(V.tensor_tensor(s, s, tmp[:, n], ALU.add))
                for g in range(G):
                    await_product(dv, "cum", l, g)
                    freed(dv, V.tensor_copy(cum[:, g * 512:(g + 1) * 512], bank(("cum", l, g))), "cum", l, g)

                def gla_prepare(g):
                    if g:
                        await_product(dv, "o", l, 0)
                        dv.wait_ge(state_stored, 32 * (l + 1))
                    cg = cum[:, g * 512:(g + 1) * 512]
                    for dr in range(2):
                        cd = cg[:, dr * 256:(dr + 1) * 256]
                        first = 0 if dr == 0 else SUB - 1
                        end = CHUNK - 1 if dr == 0 else 0
                        V.tensor_tensor(qarg[:, dr * 256:(dr + 1) * 256].rearrange("p (b s) -> p b s", s=SUB),
                                        cd.rearrange("p (b s) -> p b s", s=SUB),
                                        cd[:, first:256:SUB].unsqueeze(2).to_broadcast([P, 16, SUB]), ALU.subtract)
                        V.tensor_tensor(klarg[:, dr * 256:(dr + 1) * 256].rearrange("p (c s) -> p c s", s=CHUNK),
                                        cd[:, end:256:CHUNK].unsqueeze(2).to_broadcast([P, 4, CHUNK]),
                                        cd.rearrange("p (c s) -> p c s", s=CHUNK), ALU.subtract)
                        for hp in range(HP):
                            ch = cd[:, hp * P:(hp + 1) * P]
                            kd = karg[:, (dr * HP + hp) * 512:(dr * HP + hp + 1) * 512]
                            for c in range(2):
                                kc = kd[:, c * 256:(c + 1) * 256].rearrange("p (b s) -> p b s", s=CHUNK)
                                lag(V.tensor_tensor(kc, ch[:, c * CHUNK + first:(c + 1) * CHUNK:SUB].unsqueeze(2)
                                                    .to_broadcast([P, 4, CHUNK]),
                                                    ch[:, c * CHUNK:(c + 1) * CHUNK].unsqueeze(1)
                                                    .to_broadcast([P, 4, CHUNK]), ALU.subtract), 99999)
                    settle()
                    st.done(V.tensor_scalar(karg, karg, EXP_CAP, None, ALU.min), args_ready)
                    st.next(exps_ready)
                    qg = [w.rearrange("p (h t) -> p h t", h=HP)[:, :, g * P:(g + 1) * P] for w in (qT, kT)]
                    for dr in range(2):
                        for dst, e_ in ((qpad, qarg), (qepad, ecum)):
                            d4 = dst[:, dr * 512:(dr + 1) * 512].rearrange("p (h a t) -> p h a t", h=HP, a=2)
                            e3 = e_[:, dr * 256:(dr + 1) * 256].rearrange("p (h t) -> p h t", h=HP)
                            for s in range(2):
                                V.scalar_tensor_tensor(out=d4[:, :, s, :], in0=qg[0], scalar=half[s], in1=e3,
                                                       op0=ALU.mult, op1=ALU.mult)
                        kl = klarg[:, dr * 256:(dr + 1) * 256].rearrange("p (h t) -> p h t", h=HP)
                        V.tensor_tensor(kl, kl, qg[1], ALU.mult)
                        for hp in range(HP):
                            kd = karg[:, (dr * HP + hp) * 512:(dr * HP + hp + 1) * 512].rearrange(
                                "p (c b s) -> p c b s", c=2, b=4)
                            kk = qg[1][:, hp, :].rearrange("p (c s) -> p c s", c=2).unsqueeze(2)\
                                .to_broadcast([P, 2, 4, CHUNK])
                            ins = V.tensor_tensor(kd, kd, kk, ALU.mult)
                    st.done(ins, gla_ready)

                def gla_mask(g):
                    A3 = A[:, :].rearrange("p (h t) -> p h t", h=GLA_H)
                    T3 = gtmp[:, 0:512].rearrange("p (h t) -> p h t", h=GLA_H)
                    if g:
                        await_product(dv, "o", l, 0)
                    elif l:
                        await_product(dv, "o", l - 1, 1)
                    for dr, dst in ((0, A3), (1, T3)):
                        await_product(dv, "att", l, g, dr)
                        src = bank(("att", l, g, dr)).rearrange("p (h t) -> p h t", h=GLA_H)
                        for c in range(2):
                            q = slice(64 * c, 64 * c + 64)
                            m = C("mask_f" if dr == 0 else "mask_b")[q, q].unsqueeze(1).to_broadcast([64, GLA_H, 64])
                            ins = V.tensor_tensor(dst[q, :, q], src[q, :, q], m, ALU.mult)
                        freed(dv, ins, "att", l, g, dr)
                    for c in range(2):
                        q = slice(64 * c, 64 * c + 64)
                        ins = V.tensor_tensor(A3[q, :, q], A3[q, :, q], T3[q, :, q], ALU.add)
                    st.done(ins, A_ready)

                def gla_carry(g):
                    if g:
                        dv.wait_ge(state_in, 32 * (l + 1))
                        await_product(dv, "o", l, 0)
                    for dr in range(2):
                        await_product(dv, "kv", l, g, dr)
                        kv = bank(("kv", l, g, dr))
                        c0 = 0 if dr == 0 else 1
                        end = CHUNK - 1 if dr == 0 else 0
                        for hp in range(HP):
                            j = dr * HP + hp
                            s1 = S1[:, j * P:(j + 1) * P]
                            first = kv[:, (c0 * HP + hp) * P:(c0 * HP + hp + 1) * P]
                            second = kv[:, ((1 - c0) * HP + hp) * P:((1 - c0) * HP + hp + 1) * P]

                            def decay(c):
                                t = j * P + c * CHUNK + end
                                return ecum[:, t:t + 1]

                            if g == 0:
                                st.done(V.tensor_copy(s1, first))
                                ins = V.scalar_tensor_tensor(out=qarg[:, j * P:(j + 1) * P], in0=s1, scalar=decay(1 - c0),
                                                             in1=second, op0=ALU.mult, op1=ALU.add)
                            else:
                                ins = V.scalar_tensor_tensor(out=s1, in0=S0[:, j * P:(j + 1) * P], scalar=decay(c0),
                                                             in1=first, op0=ALU.mult, op1=ALU.add)
                        freed(dv, ins, "kv", l, g, dr)

                def gla_norm(g):
                    og = o[:, g * 512:(g + 1) * 512]
                    o3 = og.rearrange("p (h v) -> p h v", h=GLA_H)
                    sq = gtmp[:, 512:1024]
                    await_product(dv, "o", l, g)
                    freed(dv, V.tensor_copy(og, bank(("o", l, g))), "o", l, g)
                    st.done(V.tensor_tensor(sq, og, og, ALU.mult))
                    st.done(V.tensor_reduce(stat[:, 42:46], sq.rearrange("p (h v) -> p h v", h=GLA_H), X, ALU.add))
                    st.done(V.tensor_scalar(stat[:, 42:46], stat[:, 42:46], 1.0 / GLA_DV, EPS, ALU.mult, ALU.add), gla_var)
                    st.next(gla_std)
                    st.done(V.reciprocal(stat[:, 46:50], stat[:, 50:54]))
                    st.done(V.tensor_tensor(o3, o3, stat[:, 46:50].unsqueeze(2).to_broadcast([P, GLA_H, GLA_DV]), ALU.mult))
                    await_copied(dv, "r", l, g)
                    st.done(V.tensor_tensor(og, og, r[:, g * 512:(g + 1) * 512], ALU.mult), o_ready)

                def conv_taps(t0, t1):
                    if t0 == 0 and l:
                        await_product(dv, "y", l - 1, 2, 1, 1)
                    a4 = acc.rearrange("p (g c t) -> p c g t", g=G, c=CC)
                    for t in range(t0, t1):
                        for c in range(CC):
                            src = z4[:, c, :, t:t + P]
                            w = vecs[:, 144 + 124 * l + t * CC + c:145 + 124 * l + t * CC + c]
                            if t == 0:
                                ins = V.tensor_scalar(a4[:, c], src, w, vecs[:, vl + 48 + c:vl + 49 + c], ALU.mult, ALU.add)
                            else:
                                ins = V.scalar_tensor_tensor(out=a4[:, c], in0=src, scalar=w, in1=a4[:, c],
                                                             op0=ALU.mult, op1=ALU.add)
                            if t == TAPS - 1 and c == CC - 1:
                                ins.then_inc(conv_summed, 1)
                            else:
                                lag(ins, CC - 1)

                def conv_norm():
                    for g in range(G):
                        await_product(dv, "cvtok", l, g)
                        b = bank(("cvtok", l, g))
                        moments([b])
                        rstd(stat[:, 37:38], stat[:, 38:39])
                        freed(dv, V.tensor_scalar(acc[:, g * 512:(g + 1) * 512], b, stat[:, 36:37], stat[:, 38:39],
                                                  ALU.subtract, ALU.mult), "cvtok", l, g)

                def softmax(g):
                    keys = P * (1 + g)
                    n = NA_H * keys
                    Pn = Pm[:, 0:n]
                    P4 = Pn.rearrange("p (h k) -> p h k", h=NA_H)
                    if g:
                        await_product(dv, "PT", l, 0, 1)
                        b3 = bias.rearrange("p (h k) -> p h k", h=NA_H)
                    for i in range(2 * (1 + g)):
                        await_product(dv, "sc", l, g, i)
                        s = bank(("sc", l, g, i))
                        if g == 0:
                            free(V.tensor_scalar(Pn[:, i * 512:(i + 1) * 512], s, NA_DH ** -0.5, None, ALU.mult), "sc", l, g, i)
                        else:
                            s3 = s.rearrange("p (h k) -> p h k", h=2)
                            d3 = P4[:, 2 * i:2 * i + 2, :]
                            V.scalar_tensor_tensor(out=d3[:, :, 0:P], in0=s3[:, :, 0:P], scalar=NA_DH ** -0.5,
                                                   in1=b3[:, 2 * i:2 * i + 2, :], op0=ALU.mult, op1=ALU.add)
                            free(V.tensor_scalar(d3[:, :, P:2 * P], s3[:, :, P:2 * P], NA_DH ** -0.5, None, ALU.mult),
                                 "sc", l, g, i)
                    await_copied(dv, "sc", l, g, 2 * (1 + g) - 1)
                    st.done(V.tensor_reduce(stat[:, 12:20], P4, X, ALU.max))
                    st.done(V.tensor_tensor(P4, P4, stat[:, 12:20].unsqueeze(2).to_broadcast([P, NA_H, keys]),
                                            ALU.subtract), P_arg)
                    st.next(P_exp)
                    st.done(V.tensor_reduce(stat[:, 20:28], P4, X, ALU.add))
                    st.done(V.reciprocal(stat[:, 28:36], stat[:, 20:28]))
                    st.done(V.tensor_tensor(P4, P4, stat[:, 28:36].unsqueeze(2).to_broadcast([P, NA_H, keys]),
                                            ALU.mult), P_ready)

                gla_prepare(0)
                gla_mask(0)
                gla_carry(0)
                gla_norm(0)
                conv_taps(0, 12)
                gla_prepare(1)
                gla_mask(1)
                gla_carry(1)
                gla_norm(1)
                conv_taps(12, TAPS)
                await_product(dv, "bias", l, 1)
                for i in range(2):
                    freed(dv, V.tensor_tensor(bias[:, i * 512:(i + 1) * 512].rearrange("p (h k) -> p h k", h=4),
                                              bank(("bias", l, i)).rearrange("p (h k) -> p h k", h=4),
                                              C("window").unsqueeze(1).to_broadcast([P, 4, P]), ALU.add), "bias", l, i)
                conv_norm()
                softmax(0)
                softmax(1)

                def diagonal(dst, c0, j):
                    for g in range(G):
                        ins = V.tensor_tensor(dst[:, g * D:(g + 1) * D].rearrange("p (c n) -> p c n", c=KD),
                                              ident.unsqueeze(1).to_broadcast([P, KD, P]),
                                              mod3[:, c0:c0 + KD, g:g + 1].to_broadcast([P, KD, P]), ALU.mult)
                    st.done(ins, diag_ready)

                def gated(b):
                    for g in range(G):
                        for n in range(2):
                            await_copied(dv, "mg", l, g, 2 * b + n)
                            await_product(dv, "y", l, b, g, n)
                            s = gates[:, g * 3 * D + b * D + 512 * n:g * 3 * D + b * D + 512 * n + 512]
                            free(V.tensor_tensor(s, s, bank(("y", l, b, g, n)), ALU.mult), "y", l, b, g, n)

                gated(0)
                gated(2)
                diagonal(diag1, 16, 0)
                gated(1)
                await_copied(dv, "y", l, 1, 1, 1)
                for g in range(G):
                    m = [gates[:, g * 3 * D + b * D:g * 3 * D + (b + 1) * D] for b in range(3)]
                    st.done(V.tensor_tensor(m[0], m[0], m[1], ALU.add))
                    st.done(V.tensor_tensor(m[0], m[0], m[2], ALU.add), m_ready)

                def block_norm(j, lnw, gbc, name, sig):
                    dv.wait_ge(ln_in, 32 * (2 * l + j + 1))
                    for g in range(G):
                        for n in range(2):
                            xs = x[:, g * D + 512 * n:g * D + 512 * n + 512]
                            tmp = mtmp[:, 0:512] if j == 0 else ftmp[:, 0:512]
                            await_copied(dv, "gbc", l, j, g, n)
                            await_product(dv, *name(g, n))
                            freed(dv, V.tensor_tensor(tmp, gbc[:, g * D + 512 * n:g * D + 512 * n + 512],
                                                      bank(name(g, n)), ALU.mult), *name(g, n))
                            st.done(V.scalar_tensor_tensor(out=xs, in0=xs, scalar=ALPHA, in1=tmp, op0=ALU.mult,
                                                           op1=ALU.add))
                        layer_norm(x[:, g * D:(g + 1) * D], lnw[:, 0:D], lnw[:, D:2 * D], sig)

                block_norm(0, ln1, gbc1, lambda g, n: ("mix", l, g, n), x_ready)
                modulated("h2T", 24, 32)
                await_product(dv, "h2T", l, 1, 1)
                diagonal(diag2, 40, 1)
                if l == 0:
                    for i, (f0, fn) in enumerate(FCHUNKS):
                        for g in range(G):
                            if i:
                                await_product(dv, "aT", i - 1, g)
                            await_copied(dv, "G", i, g)
                            await_product(dv, "U", i, g)
                            free(V.tensor_tensor(act[:, g * 512:g * 512 + fn], sil[:, g * 512:g * 512 + fn],
                                                 bank(("U", i, g))[:, 0:fn], ALU.mult), "U", i, g)
                    block_norm(1, ln2, gbc2, lambda g, n: ("Y", g, n), x_ready)

            def R(i, n):
                return route[:, i:i + n]

            def GE(i):
                return R(i, 16).rearrange("p (g e) -> p g e", g=G)

            def EG(i):
                return R(i, 16).rearrange("p (e g) -> p g e", g=G)

            def over_e(i):
                return R(i, G).unsqueeze(2).to_broadcast([P, G, EXPERTS])

            LOG, TMP, TOP1, TOP2, MASK, V1, V2, AT, DIFF, GATE1, GATE2, NUM = 0, 16, 32, 48, 64, 80, 82, 84, 98, 102, 104, 106
            nums = R(NUM, EXPERTS).unsqueeze(1).to_broadcast([P, G, EXPERTS])
            st.done(V.memset(route[:, 128:256], -BIG))
            st.done(V.memset(moe_y, 0.0))
            st.done(V.tensor_scalar(R(NUM, EXPERTS), C("slots")[:, 0:EXPERTS], -1.0 * EXPERTS, None, ALU.add))
            await_product(dv, "logits")
            freed(dv, V.tensor_copy(R(LOG, 16), bank(("logits",))[:, 0:16]), "logits")

            def pick(src, top, onehot):
                st.done(V.tensor_reduce(R(top, G), GE(src), X, ALU.max))
                st.done(V.tensor_tensor(GE(onehot), GE(src), over_e(top), ALU.is_equal))
                st.done(V.tensor_tensor(GE(onehot), GE(onehot), nums, ALU.mult))
                st.done(V.tensor_reduce(R(AT, G), GE(onehot), X, ALU.min))
                st.done(V.tensor_tensor(GE(onehot), nums, over_e(AT), ALU.is_equal))

            pick(LOG, V1, TOP1)
            st.done(V.scalar_tensor_tensor(out=R(TMP, 16), in0=R(TOP1, 16), scalar=-1e30, in1=R(LOG, 16),
                                           op0=ALU.mult, op1=ALU.add))
            pick(TMP, V2, TOP2)
            st.done(V.tensor_tensor(R(MASK, 16), R(TOP1, 16), R(TOP2, 16), ALU.add), mask_ready)
            st.done(V.tensor_tensor(R(DIFF, 2), R(V2, 2), R(V1, 2), ALU.subtract), gate_arg)
            st.next(gate_exp)
            st.done(V.tensor_scalar(R(GATE1, 2), R(100, 2), 1.0, None, ALU.add))
            st.done(V.reciprocal(R(GATE1, 2), R(GATE1, 2)))
            st.done(V.tensor_tensor(R(GATE2, 2), R(100, 2), R(GATE1, 2), ALU.mult))
            st.done(V.tensor_tensor(GE(TOP1), GE(TOP1), over_e(GATE1), ALU.mult))
            st.done(V.tensor_tensor(GE(TOP2), GE(TOP2), over_e(GATE2), ALU.mult))
            POS, WT = 128, 192
            for n in range(2):
                st.done(V.tensor_tensor(EG(WT + 16 * n), GE(TOP1), GE(TOP2), ALU.add))
            await_product(dv, "rank")
            rank = bank(("rank",))
            st.done(V.tensor_scalar(R(TMP, 16), rank[:, 0:16], BIG, None, ALU.add))
            st.done(V.tensor_tensor(R(TMP, 16), R(TMP, 16), R(MASK, 16), ALU.mult))
            st.done(V.tensor_scalar(EG(POS), GE(TMP), -BIG, None, ALU.add))
            st.done(V.tensor_scalar(EG(POS + 16), GE(TMP), -BIG - P, None, ALU.add))
            freed(dv, V.tensor_reduce(R(DIFF, 1), rank[:, 16:24], X, ALU.max), "rank")
            st.done(V.tensor_copy(flag[:, :], R(DIFF, 1)), flag_ready)

            def select(E, ins_first=None):
                for g in range(G):
                    pos = route[:, bass.ds(POS + 2 * E + g, 1)]
                    wt = route[:, bass.ds(WT + 2 * E + g, 1)]
                    V.tensor_scalar(S[:, g * P:(g + 1) * P], C("slots"), pos, None, ALU.is_equal)
                    ins = V.tensor_scalar(S2[:, g * P:(g + 1) * P], C("slots"), pos, wt, ALU.is_equal, ALU.mult)
                ins.then_inc(sel_ready, 1)

            def experts(passes):
                with dv.Fori(0, EXPERTS) as e:
                    E = e + EXPERTS * passes
                    for i in range(EC):
                        if i >= 2:
                            e_await_product(dv, E, "T", i - 2)
                        e_await_copied(dv, E, "G", i)
                        e_await_product(dv, E, "U", i)
                        b = slice((i % 2) * 512, (i % 2 + 1) * 512)
                        e_free(V.tensor_tensor(act[:, b], sil[:, b], ebank(("U", i)), ALU.mult), "U", i)
                    e_await_product(dv, E, "ST")
                    select(E + 1)
                    e_await_product(dv, E, "D", 0)
                    e_free(V.tensor_copy(yd[:, 0:512], ebank(("D", 0))), "D", 0)
                    for g in range(G):
                        for n in range(2):
                            e_await_product(dv, E, "SC", g, n)
                            y = moe_y[:, g * D + 512 * n:g * D + 512 * n + 512]
                            e_free(V.tensor_tensor(y, y, ebank(("SC", g, n)), ALU.add), "SC", g, n)
                    e_await_copied(dv, E, "SC", 1, 1)

            select(0)
            experts(0)
            over = dv.value_load(flag[0:1, 0:1], min_val=0, max_val=T)
            with dv.If(over > P):
                experts(1)
            dv.wait_ge(ln_in, 32 * 2 * DEPTH)
            await_copied(dv, "gbc", DEPTH - 1, 1, 1, 1)
            for g in range(G):
                xg, yg = x[:, g * D:(g + 1) * D], moe_y[:, g * D:(g + 1) * D]
                st.done(V.tensor_tensor(yg, yg, gbc2[:, g * D:(g + 1) * D], ALU.mult))
                st.done(V.scalar_tensor_tensor(out=xg, in0=xg, scalar=ALPHA, in1=yg, op0=ALU.mult, op1=ALU.add))
                layer_norm(xg, ln2[:, 0:D], ln2[:, D:2 * D], y_ready)


_INS = ["x_prompt", "x_sample", "cache_na_k", "cache_na_v", "state_gla", "c", "c_ctx", "w_mod", "b_mod", "w_in",
        "gla_w_gup", "gla_b_g", "gla_norm", "w_br_gla", "na_rpb", "w_br_na", "cv_w", "cv_b", "cv_ln_g", "cv_ln_b",
        "w_br_cv", "w_out", "ln_g", "ln_b", "ffd_w_gate", "ffd_w_up", "ffd_w_down",
        "moe_w_router", "moe_w_gate", "moe_w_up", "moe_w_down"]
_OUTS = [(1, P, D), (1, P, D), (1, DEPTH, P, NA_H, NA_DH), (1, DEPTH, P, NA_H, NA_DH),
         (1, DEPTH, 2, GLA_H, GLA_DK, GLA_DV)]


def kernel(**inputs):
    import numpy as _np
    import concourse.bacc as _bacc
    from concourse.bass_utils import run_bass_kernel_spmd as _run

    nc = _bacc.Bacc("TRN2", target_bir_lowering=False, num_devices=1)
    arrays, args = {}, {}
    for name in _INS:
        arrays[f"in_{name}"] = _np.ascontiguousarray(inputs[name])
        args[name] = nc.dram_tensor(f"in_{name}", arrays[f"in_{name}"].shape, F32, kind="ExternalInput").ap()
    arrays["const_tables"] = shape_constants()
    args["const_tables"] = nc.dram_tensor("const_tables", arrays["const_tables"].shape, F32, kind="ExternalInput").ap()
    outs = [nc.dram_tensor(f"out_{i}", shape, F32, kind="ExternalOutput").ap() for i, shape in enumerate(_OUTS)]
    build(nc, args, outs)
    r = _run(nc, [arrays], core_ids=[0])
    return tuple(r.results[0][f"out_{i}"] for i in range(len(_OUTS)))
```

```python
from collections import Counter
from contextlib import ExitStack

import numpy as np

import concourse.bass as bass
from concourse import mybir

F32 = mybir.dt.float32
F32R = mybir.dt.float32r
I32 = mybir.dt.int32
ALU = mybir.AluOpType
ACT = mybir.ActivationFunctionType
X = mybir.AxisListType.X

P = 128
G = 2
T = G * P
D = 1024
KD = D // P
DEPTH = 2
GLA_H, GLA_DK, GLA_DV, RANK, CHUNK, SUB = 4, 64, 128, 16, 64, 16
HP = GLA_H * GLA_DK // P
NA_H, NA_DH = 8, 64
PAIRS = NA_H // 2
CONV, TAPS = 512, 31
CC = CONV // P
ZW = P + TAPS - 1
FF_D, FF_E, EXPERTS = 2816, 3584, 8
GRID_W, WIN_R, WIN_C = 64, 8, 16
EPS = 1e-5
ALPHA = (2 * DEPTH) ** 0.25
TAU = 16.0
BIG = 1000.0
EXP_CAP = 80.0
RING = 4
XRING = 3
W = 4096
PART = W // 4
PARTS = 6

SPLIT = dict(qk=0, v=512, r=1024, gda=1536, qb=1568, kb=2080, vb=2592, cva=3104, cvg=3616, mg=4128)
MG = [f"mg{n}" for n in range(6)]
SPLIT.update({m: 4128 + 512 * n for n, m in enumerate(MG)})

CONSTS = ["ident", "mask_f", "mask_b", "rot", "cos", "sin", "window", "slots", "before", "ones", "flip"]


def shape_constants():
    i = np.arange(P)
    r, c = i[:, None], i[None, :]
    same = r // CHUNK == c // CHUNK
    t = {"ident": r == c, "ones": np.ones((P, P)), "before": r < c}
    t["flip"] = (r // GRID_W == c // GRID_W) & (r % GRID_W + c % GRID_W == GRID_W - 1)
    t["mask_f"] = same & (r <= c)
    t["mask_b"] = same & (r >= c)
    rot = np.zeros((P, P))
    n = GLA_DK // 4
    for m in range(P):
        rot[m + n if m % (2 * n) < n else m - n, m] = -1.0 if m % (2 * n) < n else 1.0
    t["rot"] = rot
    inv = np.float32(10000.0) ** (-np.arange(n, dtype=np.float32) / np.float32(n))
    d = i % GLA_DK
    pos = np.where((d < GLA_DK // 2)[:, None], c // GRID_W, c % GRID_W).astype(np.float32)
    ang = pos * inv[d % n][:, None].astype(np.float32)
    t["cos"], t["sin"] = np.cos(ang), np.sin(ang)
    start = np.clip(r % GRID_W - WIN_C // 2, 0, GRID_W - WIN_C)
    t["window"] = np.where((c % GRID_W >= start) & (c % GRID_W < start + WIN_C), 0.0, -1e30)
    t["slots"] = np.broadcast_to(c, (P, P))
    half = np.stack([i < 64, i >= 64], 1)
    return np.concatenate([np.asarray(t[k], np.float32) for k in CONSTS] + [half.astype(np.float32)], 1)


FCHUNKS = [(a, min(512, FF_D - a)) for a in range(0, FF_D, 512)]


EARLY = range(4)
FIRST3 = ("v", "vb", "r")


def plan():
    prods, units = [("vecs",)], []
    last = {}

    def p(*name):
        prods.append(name)

    def u(name, *users):
        units.append(name)
        last[name] = users[-1]

    def mod(l, i):
        p("mod", l, i), p("modT", l, i)
        u(("mod", l, i), ("mod", l, i))

    def w_token(l, name):
        for g in range(G):
            p(name, l, g)
        u((name, l), (name, l, G - 1))

    def mg(l, n):
        p("mg", l, 0, n), p("mg", l, 1, n)
        u((MG[n], l), ("mg", l, 1, n))

    for i in EARLY:
        mod(0, i)
    for l in range(DEPTH):
        for g in range(G):
            p("hT", l, g, 0), p("hT", l, g, 1)
            for n in FIRST3:
                p(n, l, g)
        for n in FIRST3:
            u((n, l), (n, l, G - 1))
        for i in range(2):
            p("cva", l, i)
        for i in range(2):
            p("cvg", l, i)
        u(("cva", l), ("cva", l, 1)), u(("cvg", l), ("cvg", l, 1))
        mod(l, 4)
        p("gda", l), p("q", l), p("k", l)
        u(("qk", l), ("k", l))
        mod(l, 5)
        p("glog", l, 0), p("glog", l, 1)
        p("kb", l, 0), p("kb", l, 1), u(("kb", l), ("kb", l, 1))
        p("rope", l)
        mod(l, 6)
        p("cum", l, 0), p("cum", l, 1)
        p("qb", l, 0), p("qb", l, 1), u(("qb", l), ("qb", l, 1))
        mod(l, 7)
        mg(l, 0)
        mod(l, 8)
        p("keT", l, 0), p("att", l, 0, 0), p("att", l, 0, 1)
        mg(l, 1)
        mod(l, 9)
        p("kv", l, 0, 0), p("kv", l, 0, 1)
        mg(l, 2)
        mod(l, 10)
        p("o", l, 0)
        mg(l, 3)
        mod(l, 11)
        p("oT", l, 0)
        mg(l, 4)
        p("keT", l, 1), p("att", l, 1, 0), p("att", l, 1, 1)
        mg(l, 5)
        p("kv", l, 1, 0), p("kv", l, 1, 1)
        p("o", l, 1), p("oT", l, 1)
        p("kbtok", l), p("kctxT", l), p("bias", l, 0), p("bias", l, 1)
        p("sc", l, 0, 0), p("sc", l, 0, 1)
        p("cvtok", l, 0), p("cvtok", l, 1)
        p("cvT", l, 0), p("cvT", l, 1)
        p("PT", l, 0, 0), p("PT", l, 0, 1)
        for i in range(4):
            p("sc", l, 1, i)
        for b in (0, 2):
            for g in range(G):
                p("y", l, b, g, 0), p("y", l, b, g, 1)
            u(("br", l, b), ("y", l, b, 1, 1))
        p("attT", l, 0)
        for i in range(4):
            p("PT", l, 1, i)
        p("attT", l, 1)
        for g in range(G):
            p("y", l, 1, g, 0), p("y", l, 1, g, 1)
        u(("br", l, 1), ("y", l, 1, 1, 1))
        for g in range(G):
            p("gbc", l, 0, g, 0), p("gbc", l, 0, g, 1)
        for g in range(G):
            p("mT", l, g, 0), p("mT", l, g, 1)
        for g in range(G):
            p("mix", l, g, 0), p("mix", l, g, 1)
        u(("out", l, 0), ("mix", l, 1, 0)), u(("out", l, 1), ("mix", l, 1, 1))
        for g in range(G):
            p("h2T", l, g, 0), p("h2T", l, g, 1)
            if l == 0:
                p("G", 0, g), p("U", 0, g)
        if l == 0:
            u(("wg", 0), ("G", 0, 1)), u(("wu", 0), ("U", 0, 1))
        for g in range(G):
            p("gbc", l, 1, g, 0), p("gbc", l, 1, g, 1)
        if l == 0:
            for i in range(len(FCHUNKS)):
                if i:
                    for g in range(G):
                        p("G", i, g), p("U", i, g)
                    u(("wg", i), ("G", i, 1)), u(("wu", i), ("U", i, 1))
                    p("aT", i - 1, 0), p("aT", i - 1, 1)
                if i in EARLY:
                    mod(1, i)
            p("aT", len(FCHUNKS) - 1, 0), p("aT", len(FCHUNKS) - 1, 1)
            for g in range(G):
                p("Y", g, 0), p("Y", g, 1)
            for i in range(len(FCHUNKS)):
                u(("wd", i), ("Y", 1, 1))
        else:
            for g in range(G):
                p("htok", g, 0), p("htok", g, 1)
            p("logits",), p("rank",)
    return prods, units, last


DOWN = len(FCHUNKS) - 1
PRODS, UNITS, LAST = plan()
PIDX = {n: i for i, n in enumerate(PRODS)}
UIDX = {n: i for i, n in enumerate(UNITS)}
NB = 8
PBASE = [len([i for i in range(len(PRODS)) if i % NB == b]) for b in range(NB)]
UBASE = [len([i for i in range(len(UNITS)) if i % RING == s]) for s in range(XRING)]

EC = FF_E // 512
EPRODS = [("hg", 0), ("hg", 1), ("ST",)]
EUNITS = []
for _i in range(EC):
    EPRODS += [("G", _i), ("U", _i)] + ([("T", _i - 1)] if _i else [])
    EUNITS += [("g", _i), ("u", _i)]
TAIL = 2
EPRODS += [("D", 0), ("D", 1), ("T", EC - 1)] + [("SC", g, n) for g in range(G) for n in range(2)]
EUNITS += [("d", _i) for _i in range(EC)]
EPIDX = {n: i for i, n in enumerate(EPRODS)}
EUIDX = {n: i for i, n in enumerate(EUNITS)}
EPER = [len([i for i in range(len(EPRODS)) if i % NB == b]) for b in range(NB)]
EUPER = [len([i for i in range(len(EUNITS)) if i % XRING == s]) for s in range(XRING)]
EQ = 4 * len(EUNITS)
EUSED, USED_PER = [], 0
for _u in EUNITS:
    for _q in range(4):
        if _q == 3 and _u[0] != "d":
            EUSED.append(("G" if _u[0] == "g" else "U", _u[1]))
        elif _q == 3 and _u[1] == EC - 1:
            EUSED.append(("D", 1))
        else:
            USED_PER += 1
            EUSED.append(USED_PER)
LO_BASE = 4 * XRING
HI_PER = 2 + EC
LAST_TURN = 4 * (2 * EC + TAIL) + PARTS


def build(nc, a, outs):
    y_prompt, y_sample, new_k, new_v, new_state = outs
    with ExitStack() as ctx:
        def sb(name, n, parts=P):
            return ctx.enter_context(nc.sbuf_tensor(name, [parts, n], F32))

        def sem(name):
            return ctx.enter_context(nc.semaphore(name))

        ring = sb("ring", RING * W)
        x = sb("x", G * D)
        hT = sb("hT", KD * T)
        cst = sb("cst", len(CONSTS) * P + 2)
        vecs = sb("vecs", 392)
        condT = sb("condT", 48)
        modraw = sb("modraw", 48 * 8)
        modT = sb("modT", DEPTH * 48 * G)
        wgda = sb("wgda", KD * 32)
        gdaT = sb("gdaT", T)
        gup = sb("gup", 512)
        z = sb("z", CC * G * ZW)
        A = sb("A", GLA_H * P)
        stat = sb("stat", 64)
        route = sb("route", 256)
        flag = ctx.enter_context(nc.sbuf_tensor("flag", [P, 1], I32))
        arena = sb("arena", 27136)
        at = [0]

        def carve(n):
            at[0] += n
            assert at[0] <= 27136
            return arena[:, at[0] - n:at[0]]

        gates = carve(6 * T * 4)
        rows = gates[:, 0:4 * P]
        acc = carve(G * CONV)
        qT, kT = carve(512), carve(512)
        v = carve(G * 512)
        r = carve(G * 512)
        glog = carve(G * 512)
        gtmp = carve(G * 512)
        cum = carve(G * 512)
        pg = carve(6656)
        qarg, karg, klarg, ecum = pg[:, 0:512], pg[:, 512:2560], pg[:, 2560:3072], pg[:, 3072:3584]
        qpad, qepad, ke = pg[:, 3584:4608], pg[:, 4608:5632], pg[:, 5632:6656]
        S0, S1 = carve(512), carve(512)
        o = carve(G * 512)
        qbT = carve(NA_H * T)
        kbT = carve(PAIRS * T)
        vb = carve(G * 512)
        kctxT = carve(512)
        mrow = carve(512)
        Pm, PT = pg[:, 0:2048], pg[:, 2048:4096]
        bias, kctx = pg[:, 4096:5120], pg[:, 5120:5632]
        kbtok, vctx = qT, kT
        attT = cum
        diag1 = arena[:, 10240:12288]
        gbc1 = pg[:, 0:2048]
        ln1 = arena[:, 8192:10240]
        mtmp = pg[:, 2048:4096]
        at[0] = 0
        xslots = carve(3 * W)
        diag2 = arena[:, 16384:18432]
        at[0] = 17408
        htok = carve(G * D)
        sil, act = carve(512), carve(1024)
        moe_y = carve(G * D)
        ln2 = carve(2 * D)
        gbc2 = carve(G * D)
        dT = xslots[:, 0:22 * T]
        ftmp = xslots[:, 8192:8192 + 2048]
        mrow2 = xslots[:, 6144:6656]
        sil_d, act_d = xslots[:, 10240:11264], xslots[:, 11264:12288]
        yd, S, S2, S2T = hT[:, 0:1024], hT[:, 1024:1280], hT[:, 1280:1536], hT[:, 1536:1792]
        ring_r = nc.alloc_sbuf_tensor_at("ring_r", [P, W], F32R, offset=nc.lookup_mloc(ring).addr + 4 * 3 * W)
        arena_r = nc.alloc_sbuf_tensor_at("arena_r", [P, 17408], F32R, offset=nc.lookup_mloc(arena).addr)
        hg_hi, hg_lo = arena_r[:, 8192:9216], arena_r[:, 9216:10240]
        eT_hi, eT_lo = arena_r[:, 10240:13824], arena_r[:, 13824:17408]

        def split_part(j):
            s = j % PARTS
            b = ring_r[:, s * 2 * PART:(s + 1) * 2 * PART] if s < 2 else arena_r[:, (s - 2) * 2 * PART:(s - 1) * 2 * PART]
            return b[:, 0:PART], b[:, PART:2 * PART]

        ps = ctx.enter_context(nc.psum_tensor("ps", [P, NB, 512], F32))

        def C(name):
            i = CONSTS.index(name)
            return cst[:, i * P:(i + 1) * P]

        half = [cst[:, len(CONSTS) * P + i:len(CONSTS) * P + i + 1] for i in range(2)]
        ident = C("ident")

        def slot(s):
            return ring[:, s * W:(s + 1) * W]

        bank_full = [sem(f"bank_full{b}") for b in range(NB)]
        bank_free = [sem(f"bank_free{b}") for b in range(NB)]
        w_loaded = [sem(f"w_loaded{s}") for s in range(RING)]
        down_used = sem("down_used")
        part_hi, part_lo, part_used, act_hi = (sem(n) for n in ("part_hi", "part_lo", "part_used", "act_hi"))
        consts_in, x_in, vecs_in, wgda_in, gup_in = (sem(n) for n in ("consts_in", "x_in", "vecs_in", "wgda_in", "gup_in"))
        state_in, bias_in, ctx_in, vctx_in, ln_in, router_in = (
            sem(n) for n in ("state_in", "bias_in", "ctx_in", "vctx_in", "ln_in", "router_in"))
        zeroed, stored, kv_stored, state_stored = (sem(n) for n in ("zeroed", "stored", "kv_stored", "state_stored"))
        cond_ready, mod_ready, x_ready, glog_part, glog_soft, glog_ready = (
            sem(n) for n in ("cond_ready", "mod_ready", "x_ready", "glog_part", "glog_soft", "glog_ready"))
        args_ready, exps_ready, gla_ready, A_ready, o_ready, gla_var, gla_std = (
            sem(n) for n in ("args_ready", "exps_ready", "gla_ready", "A_ready", "o_ready", "gla_var", "gla_std"))
        conv_summed, P_arg, P_exp, P_ready, m_ready, var_ready, std_ready = (
            sem(n) for n in ("conv_summed", "P_arg", "P_exp", "P_ready", "m_ready", "var_ready", "std_ready"))
        diag_ready, gate_arg, gate_exp, mask_ready, sel_ready, flag_ready, y_ready = (
            sem(n) for n in ("diag_ready", "gate_arg", "gate_exp", "mask_ready", "sel_ready", "flag_ready", "y_ready"))
        dve_step, act_step, pool_step = sem("dve_step"), sem("act_step"), sem("pool_step")

        def bank(name):
            return ps[:, PIDX[name] % NB, :]

        def await_product(eng, *name):
            i = PIDX[name]
            eng.wait_ge(bank_full[i % NB], i // NB + 1)

        def await_copied(eng, *name):
            i = PIDX[name]
            eng.wait_ge(bank_free[i % NB], i // NB + 1)

        def free(ins, *name):
            ins.then_inc(bank_free[PIDX[name] % NB], 1)

        def ebank(name):
            return ps[:, EPIDX[name] % NB, :]

        def e_await_product(eng, E, *name, back=0):
            i = EPIDX[name]
            eng.wait_ge(bank_full[i % NB], E * EPER[i % NB] + (PBASE[i % NB] + i // NB + 1 - back * EPER[i % NB]))

        def e_await_copied(eng, E, *name, back=0):
            i = EPIDX[name]
            eng.wait_ge(bank_free[i % NB], E * EPER[i % NB] + (PBASE[i % NB] + i // NB + 1 - back * EPER[i % NB]))

        def e_free(ins, *name):
            ins.then_inc(bank_free[EPIDX[name] % NB], 1)

        class Steps:

            def __init__(self, eng, own):
                self.eng, self.own, self.seen, self.made = eng, own, Counter(), Counter()

            def next(self, s, by=1):
                self.seen[s.name] += by
                self.eng.wait_ge(s, self.seen[s.name])

            def done(self, ins, s=None):
                s = s or self.own
                ins.then_inc(s, 1)
                self.made[s.name] += 1
                self.eng.wait_ge(s, self.made[s.name])

        def freed(eng, ins, *name):
            free(ins, *name)
            await_copied(eng, *name)

        def modcol(l, c, g):
            return modT[:, (48 * l + c) * G + g:(48 * l + c) * G + g + 1]

        block = ctx.enter_context(nc.Block())

        def unit_source(name):
            kind = name[0]
            if kind == "mod":
                return a["w_mod"][name[1], :, 512 * name[2]:512 * name[2] + 512].rearrange("(c p) n -> p c n", p=P)
            if kind in SPLIT:
                return a["w_in"][name[1], :, SPLIT[kind]:SPLIT[kind] + 512].rearrange("(c p) n -> p c n", p=P)
            if kind == "br":
                w = a[("w_br_gla", "w_br_na", "w_br_cv")[name[2]]]
                return w[name[1]].rearrange("(c p) n -> p c n", p=P)
            if kind == "out":
                return a["w_out"][name[1], :, 512 * name[2]:512 * name[2] + 512].rearrange("(c p) n -> p c n", p=P)
            f0, fn = FCHUNKS[name[1]]
            if kind == "wd":
                return a["ffd_w_down"][0, f0:f0 + fn, :].rearrange("(c p) n -> p c n", p=P)
            w = a["ffd_w_gate" if kind == "wg" else "ffd_w_up"]
            return w[0, :, f0:f0 + fn].rearrange("(c p) n -> p c n", p=P)

        def unit_shape(name):
            src = unit_source(name)
            return src.shape[1], src.shape[2]

        def unit(name):
            c, n = unit_shape(name)
            return slot(UIDX[name] % RING)[:, 0:c * n].rearrange("p (c n) -> p c n", c=c)

        def raw_part(j):
            return slot((j // 4) % XRING)[:, (j % 4) * PART:(j % 4 + 1) * PART]

        def await_part_free(eng, E, j):
            if j < PARTS:
                e_await_product(eng, E, "D", 1, back=1)
            elif isinstance(EUSED[j - PARTS], tuple):
                e_await_product(eng, E, *EUSED[j - PARTS])
            else:
                eng.wait_ge(part_used, E * USED_PER + EUSED[j - PARTS])

        def e_source(name, e):
            f = slice(512 * name[1], 512 * name[1] + 512)
            if name[0] == "d":
                return a["moe_w_down"][0, e, f, :].rearrange("(c p) n -> p c n", p=P)
            return a["moe_w_gate" if name[0] == "g" else "moe_w_up"][0, e, :, f].rearrange("(c p) n -> p c n", p=P)

        @block.sync
        def _(sp):
            for i, name in enumerate(UNITS):
                if i >= RING:
                    before = UNITS[i - RING]
                    if before[0] == "wd" and before[1] < DOWN:
                        sp.wait_ge(down_used, before[1] + 1)
                    else:
                        await_product(sp, *LAST[before])
                sp.dma_start(unit(name), unit_source(name)).then_inc(w_loaded[i % RING], 16)

            def experts(passes):
                with sp.Fori(0, EXPERTS) as e:
                    for i, name in enumerate(EUNITS):
                        sp.wait_ge(part_lo, (e + EXPERTS * passes) * EQ + (LO_BASE + 4 * (i - XRING + 1)))
                        dst = slot(i % XRING).rearrange("p (c n) -> p c n", c=4 if name[0] == "d" else 8)
                        sp.dma_start(dst, e_source(name, e)).then_inc(w_loaded[i % XRING], 16)

            await_product(sp, "h2T", DEPTH - 1, 1, 1)
            sp.wait_ge(kv_stored, 32 * DEPTH)
            experts(0)
            sp.wait_ge(flag_ready, 1)
            over = sp.value_load(flag[0:1, 0:1], min_val=0, max_val=T)
            with sp.If(over > P):
                experts(1)

        @block.gpsimd
        def _(pool):
            pool.memset(condT[:, :], 0.0).then_inc(zeroed, 1)
            pool.memset(gup[:, :], 0.0).then_inc(pool_step, 1)
            pool.memset(gdaT[:, :], 0.0).then_inc(pool_step, 1)
            pool.memset(z[:, :], 0.0).then_inc(zeroed, 1)
            pool.memset(A[:, :], 0.0).then_inc(zeroed, 1)
            pool.wait_ge(zeroed, 3)
            pool.wait_ge(pool_step, 2)
            pool.memset(gdaT[32:33, :], 1.0).then_inc(zeroed, 1)

            def last_layer_done_with(l, *name):
                if l:
                    await_product(pool, name[0], l - 1, *name[1:])

            def load_mixer(l):
                last_layer_done_with(l, "gda")
                pool.dma_start(wgda[:, :].rearrange("p (c n) -> p c n", c=KD),
                               a["w_in"][l, :, 1536:1568].rearrange("(c p) n -> p c n", p=P)).then_inc(wgda_in, 16)
                last_layer_done_with(l, "glog", 1)
                for n in range(2):
                    pool.dma_start(gup[RANK * n:RANK * n + RANK, 256 * n:256 * n + 256],
                                   a["gla_w_gup"][l, n]).then_inc(gup_in, 16)
                pool.dma_start(gup[32:33, :], a["gla_b_g"][l:l + 1].rearrange("o n k -> o (n k)")).then_inc(gup_in, 16)

            def load_state(l):
                if l:
                    pool.wait_ge(x_ready, 2 * G * l)
                for n in range(2):
                    pool.dma_start(S0[:, 256 * n:256 * n + 256].rearrange("p (h v) -> p h v", h=HP),
                                   a["state_gla"][0, l, n].rearrange("(h a) k v -> (a k) h v", a=2))\
                        .then_inc(state_in, 16)

            def na_loads(l):
                await_product(pool, "o", l, 1)
                pool.dma_start(kctx, a["cache_na_k"][0, l].rearrange("t h d -> t (h d)")).then_inc(ctx_in, 16)
                pool.dma_start(vctx, a["cache_na_v"][0, l].rearrange("t h d -> t (h d)")).then_inc(vctx_in, 16)
                w = a["na_rpb"][l]
                for rq in range(2):
                    for rk in range(2):
                        start = l * NA_H * 15 * 31 + (rk - rq + WIN_R - 1) * 31 + WIN_C - GRID_W
                        toeplitz = bass.AP(w.tensor, start, [[1, GRID_W], [15 * 31, NA_H], [1, GRID_W]])
                        pool.dma_start(bias[64 * rq:64 * rq + 64, :].rearrange("p (h k) -> p h k", h=NA_H)[
                            :, :, 64 * rk:64 * rk + 64], toeplitz).then_inc(bias_in, 16)

            def load_ln(dst, l, j):
                for i, name in enumerate(("ln_g", "ln_b")):
                    w = a[name][l, j]
                    pool.dma_start(dst[:, i * D:(i + 1) * D],
                                   bass.AP(w.tensor, (l * 2 + j) * D, [[0, P], [1, D]])).then_inc(ln_in, 16)

            def load_router():
                await_product(pool, "gda", DEPTH - 1)
                pool.dma_start(wgda[:, 0:KD * EXPERTS].rearrange("p (c n) -> p c n", c=KD),
                               a["moe_w_router"][0].rearrange("(c p) n -> p c n", p=P)).then_inc(router_in, 16)

            for l in range(DEPTH):
                load_mixer(l)
                load_state(l)
                await_copied(pool, "vb", l, 0)
                pool.dma_start(new_v[0, l].rearrange("t h d -> t (h d)"), vb[:, 0:512]).then_inc(kv_stored, 16)
                await_copied(pool, "kv", l, 0, 0)
                await_copied(pool, "kv", l, 0, 1)
                for n in range(2):
                    pool.dma_start(new_state[0, l, n].rearrange("(h a) k v -> (a k) h v", a=2),
                                   qarg[:, 256 * n:256 * n + 256].rearrange("p (h v) -> p h v", h=HP))\
                        .then_inc(state_stored, 16)
                na_loads(l)
                await_product(pool, "oT", l, 1)
                load_ln(ln1, l, 0)
                await_copied(pool, "kbtok", l)
                pool.dma_start(new_k[0, l].rearrange("t h d -> t (h d)"), kbtok).then_inc(kv_stored, 16)
                if l == DEPTH - 1:
                    load_router()
                await_product(pool, "h2T", l, 1, 1)
                pool.wait_ge(kv_stored, 32 * (l + 1))
                load_ln(ln2, l, 1)
            for g, out in enumerate((y_prompt, y_sample)):
                pool.wait_ge(y_ready, g + 1)
                pool.dma_start(out[0], x[:, g * D:(g + 1) * D]).then_inc(stored, 16)
            pool.wait_ge(stored, 32)
            pool.wait_ge(state_stored, 32 * DEPTH)
            pool.wait_ge(kv_stored, 32 * DEPTH)

        @block.tensor
        def _(pe):
            st = Steps(pe, None)

            def claim(*name):
                i = PIDX[name]
                if i >= NB:
                    pe.wait_ge(bank_free[i % NB], i // NB)
                return bank(name)

            def full(ins, *name):
                ins.then_inc(bank_full[PIDX[name] % NB], 1)

            def arrived(name):
                i = UIDX[name]
                pe.wait_ge(w_loaded[i % RING], 16 * (i // RING + 1))
                return unit(name)

            mm = nc.tensor.matmul
            tr = nc.tensor.transpose

            def tokens_times(name, lhs, w, n=512, ks=KD, n0=0):
                o_ = claim(*name)
                for k in range(ks):
                    ins = mm(o_[:, 0:n], lhs(k), w[:, k, n0:n0 + n], start=(k == 0), stop=(k == ks - 1))
                full(ins, *name)

            def hTk(g):
                return lambda k: hT[:, k * T + g * P:k * T + g * P + P]

            def features(name, w, chunks):
                o_ = claim(*name)
                for j, c in enumerate(chunks):
                    for k in range(KD):
                        ins = mm(o_[:, j * T:(j + 1) * T], w[:, k, c * P:(c + 1) * P], hT[:, k * T:(k + 1) * T],
                                 start=(k == 0), stop=(k == KD - 1))
                full(ins, *name)

            def turned(name, sources, rows_=P):
                o_ = claim(*name)
                for j, s in enumerate(sources):
                    ins = tr(o_[:, j * P:j * P + rows_], s, ident[0:rows_, 0:rows_])
                full(ins, *name)

            def copied(*name):
                await_copied(pe, *name)

            pe.wait_ge(consts_in, 16)
            pe.wait_ge(vecs_in, 16 * 14)
            o_ = claim("vecs")
            tr(o_[:, 0:128], rows[:, 0:P], ident)
            tr(o_[:, 128:144], rows[0:16, P:2 * P], ident[0:16, 0:16])
            tr(o_[:, 144:268], rows[0:124, 2 * P:3 * P], ident[0:124, 0:124])
            full(tr(o_[:, 268:392], rows[0:124, 3 * P:4 * P], ident[0:124, 0:124]), "vecs")

            def mod_unit(l, i, buf):
                w = arrived(("mod", l, i))
                pe.wait_ge(cond_ready, 1)
                o_ = claim("mod", l, i)
                for k in range(KD):
                    j = k % 4
                    ins = mm(o_[32 * j:32 * j + 32, :], condT[:, G * k:G * k + 32], w[:, k, :],
                             start=(k < 4), stop=(k >= 4))
                full(ins, "mod", l, i)
                copied("mod", l, i)
                turned(("modT", l, i), [buf[:, j * P:(j + 1) * P] for j in range(4)])

            for i in EARLY:
                mod_unit(0, i, mrow)
            for l in range(DEPTH):
                first = {}
                for g in range(G):
                    if l == 0:
                        pe.wait_ge(x_in, 32)
                    else:
                        pe.wait_ge(x_ready, 2 * G * l - G + g + 1)
                    for h in range(2):
                        turned(("hT", l, g, h), [x[:, g * D + (4 * h + j) * P:g * D + (4 * h + j + 1) * P] for j in range(4)])
                    copied("hT", l, g, 0), copied("hT", l, g, 1)
                    for n in FIRST3:
                        if g == 0:
                            first[n] = arrived((n, l))
                        tokens_times((n, l, g), hTk(g), first[n])
                w = arrived(("cva", l))
                features(("cva", l, 0), w, (0, 1)), features(("cva", l, 1), w, (2, 3))
                w = arrived(("cvg", l))
                features(("cvg", l, 0), w, (0, 1)), features(("cvg", l, 1), w, (2, 3))
                mod_unit(l, 4, mrow)
                pe.wait_ge(wgda_in, 16 * (l + 1))
                o_ = claim("gda", l)
                for k in range(KD):
                    ins = mm(o_[0:32, 0:T], wgda[:, k * 32:(k + 1) * 32], hT[:, k * T:(k + 1) * T],
                             start=(k == 0), stop=(k == KD - 1))
                full(ins, "gda", l)
                w = arrived(("qk", l))
                features(("q", l), w, (0, 1)), features(("k", l), w, (2, 3))
                mod_unit(l, 5, mrow)
                copied("gda", l)
                pe.wait_ge(zeroed, 4)
                pe.wait_ge(gup_in, 48 * (l + 1))
                for g in range(G):
                    o_ = claim("glog", l, g)
                    full(mm(o_, gdaT[:, g * P:(g + 1) * P], gup[:, :], start=True, stop=True), "glog", l, g)
                w = arrived(("kb", l))
                features(("kb", l, 0), w, (0, 1)), features(("kb", l, 1), w, (2, 3))
                o_ = claim("rope", l)
                copied("q", l), copied("k", l)
                for j in range(4):
                    s = (qT, kT)[j // 2][:, (j % 2) * T + P:(j % 2) * T + T]
                    ins = mm(o_[:, j * P:(j + 1) * P], C("rot"), s, start=True, stop=True)
                full(ins, "rope", l)
                mod_unit(l, 6, mrow)
                for g in range(G):
                    o_ = claim("cum", l, g)
                    pe.wait_ge(glog_ready, G * l + g + 1)
                    for dr in range(2):
                        for hp in range(HP):
                            j = dr * HP + hp
                            ins = mm(o_[:, j * P:(j + 1) * P], glog[:, g * 512 + j * P:g * 512 + (j + 1) * P],
                                     C("mask_f" if dr == 0 else "mask_b"), start=True, stop=True)
                    full(ins, "cum", l, g)
                w = arrived(("qb", l))
                features(("qb", l, 0), w, (0, 1)), features(("qb", l, 1), w, (2, 3))
                mod_unit(l, 7, mrow)

                def gla_scores(g):
                    pe.wait_ge(gla_ready, G * l + g + 1)
                    turned(("keT", l, g), [klarg[:, j * P:(j + 1) * P] for j in range(4)])
                    k5 = karg.rearrange("p (n h b s) -> p n h b s", n=2, h=HP, b=8)
                    q5 = qpad.rearrange("p (n h a t) -> p n h a t", n=2, h=HP, a=2)
                    for dr in range(2):
                        o4 = claim("att", l, g, dr).rearrange("s (h a t) -> s h a t", h=HP, a=2)
                        for hp in range(HP):
                            for b in range(8):
                                c = b // 4
                                ins = mm(o4[64 * c:64 * c + 64, hp, :, b * SUB:(b + 1) * SUB], k5[:, dr, hp, b, :],
                                         q5[:, dr, hp, :, b * SUB:(b + 1) * SUB], start=True, stop=True)
                        full(ins, "att", l, g, dr)

                def gla_states(g):
                    copied("keT", l, g)
                    copied("v", l, g)
                    for dr in range(2):
                        o_ = claim("kv", l, g, dr)
                        for c in range(2):
                            for hp in range(HP):
                                for s in range(2):
                                    j = c * HP + hp
                                    k0 = c * 512 + (dr * HP + hp) * P + 64 * s
                                    ins = mm(o_[64 * s:64 * s + 64, j * P:(j + 1) * P], ke[:, k0:k0 + 64],
                                             v[:, g * 512 + (2 * hp + s) * P:g * 512 + (2 * hp + s + 1) * P],
                                             start=True, stop=True)
                        full(ins, "kv", l, g, dr)

                def gla_out(g):
                    pe.wait_ge(A_ready, G * l + g + 1)
                    copied("kv", l, g, 0), copied("kv", l, g, 1)
                    o_ = claim("o", l, g)
                    qe = qepad.rearrange("p (n h a t) -> p n h a t", n=2, h=HP, a=2)
                    for h in range(GLA_H):
                        hp, s = h // 2, h % 2
                        terms = [(0, 1, S1), (1, 0, S1)] + ([(0, 0, S0), (1, 1, S0)] if g == 1 else [])
                        mm(o_[:, h * P:(h + 1) * P], A[:, h * P:(h + 1) * P],
                           v[:, g * 512 + h * P:g * 512 + (h + 1) * P], start=True, stop=False, skip_group_check=True)
                        for n, (dr, c, state) in enumerate(terms):
                            ins = mm(o_[64 * c:64 * c + 64, h * P:(h + 1) * P], qe[:, dr, hp, s, 64 * c:64 * c + 64],
                                     state[:, (dr * HP + hp) * P:(dr * HP + hp + 1) * P],
                                     start=False, stop=(n == len(terms) - 1), skip_group_check=True)
                    full(ins, "o", l, g)

                def gla_turn(g):
                    pe.wait_ge(o_ready, G * l + g + 1)
                    turned(("oT", l, g), [o[:, g * 512 + j * P:g * 512 + (j + 1) * P] for j in range(4)])

                def mgate(n):
                    w = arrived((MG[n], l))
                    tokens_times(("mg", l, 0, n), hTk(0), w), tokens_times(("mg", l, 1, n), hTk(1), w)

                mgate(0)
                mod_unit(l, 8, mrow)
                gla_scores(0)
                mgate(1)
                mod_unit(l, 9, mrow)
                gla_states(0)
                mgate(2)
                mod_unit(l, 10, mrow)
                gla_out(0)
                mgate(3)
                mod_unit(l, 11, mrow)
                gla_turn(0)
                mgate(4)
                gla_scores(1)
                mgate(5)
                gla_states(1)
                gla_out(1)
                gla_turn(1)
                turned(("kbtok", l), [kbT[:, j * T:j * T + P] for j in range(4)])
                pe.wait_ge(ctx_in, 16 * (l + 1))
                turned(("kctxT", l), [kctx[:, j * P:(j + 1) * P] for j in range(4)])
                pe.wait_ge(bias_in, 64 * (l + 1))
                for i in range(2):
                    full(mm(claim("bias", l, i), C("flip"), bias[:, i * 512:(i + 1) * 512], start=True, stop=True),
                         "bias", l, i)
                for i in range(2):
                    o_ = claim("sc", l, 0, i)
                    for j in range(4):
                        h = 4 * i + j
                        ins = mm(o_[:, j * P:(j + 1) * P], qbT[:, h * T:h * T + P],
                                 kbT[:, (h // 2) * T:(h // 2) * T + P], start=True, stop=True)
                    full(ins, "sc", l, 0, i)
                for g in range(G):
                    pe.wait_ge(conv_summed, l + 1)
                    turned(("cvtok", l, g), [acc[:, g * 512 + j * P:g * 512 + (j + 1) * P] for j in range(4)])
                for g in range(G):
                    copied("cvtok", l, g)
                    turned(("cvT", l, g), [acc[:, g * 512 + j * P:g * 512 + (j + 1) * P] for j in range(4)])
                pe.wait_ge(P_ready, G * l + 1)
                for i in range(2):
                    turned(("PT", l, 0, i), [Pm[:, (4 * i + j) * P:(4 * i + j + 1) * P] for j in range(4)])
                copied("kctxT", l)
                for i in range(4):
                    o_ = claim("sc", l, 1, i)
                    for j in range(2):
                        h = 2 * i + j
                        q = qbT[:, h * T + P:h * T + T]
                        mm(o_[:, j * T:j * T + P], q, kbT[:, (h // 2) * T + P:(h // 2) * T + T], start=True, stop=True)
                        ins = mm(o_[:, j * T + P:(j + 1) * T], q, kctxT[:, (h // 2) * P:(h // 2 + 1) * P],
                                 start=True, stop=True)
                    full(ins, "sc", l, 1, i)

                def branch(b, src):
                    w = arrived(("br", l, b))
                    for g in range(G):
                        for n in range(2):
                            tokens_times(("y", l, b, g, n), (lambda k, g=g: src(g, k)), w, ks=4, n0=512 * n)

                copied("oT", l, 0), copied("oT", l, 1)
                branch(0, lambda g, k: o[:, g * 512 + k * P:g * 512 + (k + 1) * P])
                copied("cvT", l, 0), copied("cvT", l, 1)
                branch(2, lambda g, k: acc[:, g * 512 + k * P:g * 512 + (k + 1) * P])

                def na_values(g):
                    o_ = claim("attT", l, g)
                    if g:
                        pe.wait_ge(vctx_in, 16 * (l + 1))
                    kinds = 1 + g
                    for i in range(4 if g else 2):
                        copied("PT", l, g, i)
                    for h in range(NA_H):
                        for n in range(kinds):
                            val = (vb[:, g * 512:(g + 1) * 512] if n == 0 else vctx)[:, h * NA_DH:(h + 1) * NA_DH]
                            ins = mm(o_[64 * (h % 2):64 * (h % 2) + 64, (h // 2) * P:(h // 2 + 1) * P], val,
                                     PT[:, (h * kinds + n) * P:(h * kinds + n + 1) * P],
                                     start=(n == 0), stop=(n == kinds - 1))
                    full(ins, "attT", l, g)

                na_values(0)
                pe.wait_ge(P_ready, G * l + 2)
                for i in range(4):
                    turned(("PT", l, 1, i), [Pm[:, (4 * i + j) * P:(4 * i + j + 1) * P] for j in range(4)])
                na_values(1)
                copied("attT", l, 0), copied("attT", l, 1)
                branch(1, lambda g, k: attT[:, g * 512 + k * P:g * 512 + (k + 1) * P])

                def gate_rows(j, d):
                    pe.wait_ge(diag_ready, 2 * l + j + 1)
                    for g in range(G):
                        for n in range(2):
                            o_ = claim("gbc", l, j, g, n)
                            full(mm(o_, C("ones"), d[:, g * D + 512 * n:g * D + 512 * n + 512],
                                    start=True, stop=True), "gbc", l, j, g, n)

                gate_rows(0, diag1)
                for g in range(G):
                    pe.wait_ge(m_ready, G * l + g + 1)
                    for h in range(2):
                        turned(("mT", l, g, h), [gates[:, g * 3 * D + (4 * h + j) * P:g * 3 * D + (4 * h + j + 1) * P]
                                                 for j in range(4)])
                for g in range(G):
                    copied("mT", l, g, 0), copied("mT", l, g, 1)
                for g in range(G):
                    for n in range(2):
                        tokens_times(("mix", l, g, n), hTk(g), arrived(("out", l, n)))

                def dense_pair(i, g):
                    for kind, pn in (("wg", "G"), ("wu", "U")):
                        tokens_times((pn, i, g), hTk(g), arrived((kind, i)), n=FCHUNKS[i][1])

                for g in range(G):
                    pe.wait_ge(x_ready, 2 * G * l + g + 1)
                    for h in range(2):
                        turned(("h2T", l, g, h), [x[:, g * D + (4 * h + j) * P:g * D + (4 * h + j + 1) * P] for j in range(4)])
                    copied("h2T", l, g, 0), copied("h2T", l, g, 1)
                    if l == 0:
                        dense_pair(0, g)
                gate_rows(1, diag2)

                if l == 0:
                    def dense_turn(i):
                        for g in range(G):
                            copied("U", i, g)
                            b = act_d[:, g * 512:(g + 1) * 512]
                            turned(("aT", i, g), [b[:, j * P:(j + 1) * P] for j in range(FCHUNKS[i][1] // P)])

                    for i in range(len(FCHUNKS)):
                        if i:
                            for g in range(G):
                                dense_pair(i, g)
                            dense_turn(i - 1)
                        if i in EARLY:
                            mod_unit(1, i, mrow2)
                    dense_turn(len(FCHUNKS) - 1)
                    ys = {(g, n): claim("Y", g, n) for g in range(G) for n in range(2)}
                    for i, (f0, fn) in enumerate(FCHUNKS):
                        w = arrived(("wd", i))
                        for g in range(G):
                            copied("aT", i, g)
                        for c in range(fn // P):
                            f = f0 // P + c
                            end = f == FF_D // P - 1
                            for g in range(G):
                                for n in range(2):
                                    ins = mm(ys[g, n], dT[:, f * T + g * P:f * T + (g + 1) * P],
                                             w[:, c, 512 * n:512 * n + 512], start=(f == 0), stop=end)
                                    if end:
                                        full(ins, "Y", g, n)
                        if not end:
                            ins.then_inc(down_used, 1)
                else:
                    for g in range(G):
                        for h in range(2):
                            turned(("htok", g, h), [hTk(g)(4 * h + j) for j in range(4)])
                    pe.wait_ge(router_in, 16)
                    o_ = claim("logits")
                    for g in range(G):
                        for k in range(KD):
                            ins = mm(o_[:, 8 * g:8 * g + 8], hTk(g)(k), wgda[:, 8 * k:8 * k + 8],
                                     start=(k == 0), stop=(k == KD - 1))
                    full(ins, "logits")
                    o_ = claim("rank")
                    pe.wait_ge(mask_ready, 1)
                    m0, m1 = route[:, 64:72], route[:, 72:80]
                    mm(o_[:, 0:8], C("before"), m0, start=True, stop=True)
                    mm(o_[:, 8:16], C("before"), m1, start=True, stop=False)
                    mm(o_[:, 8:16], C("ones"), m0, start=False, stop=True)
                    mm(o_[:, 16:24], C("ones"), m0, start=True, stop=False)
                    full(mm(o_[:, 16:24], C("ones"), m1, start=False, stop=True), "rank")

            def e_claim(E, *name):
                i = EPIDX[name]
                pe.wait_ge(bank_free[i % NB], E * EPER[i % NB] + (PBASE[i % NB] + i // NB))
                return ebank(name)

            def e_full(ins, *name):
                ins.then_inc(bank_full[EPIDX[name] % NB], 1)

            def split_mm(pairs, hi, lo, w_hi, w_lo, start, stop):
                for o_, n in pairs:
                    mm(o_, hi, w_hi[:, n], start=start, stop=False)
                    mm(o_, hi, w_lo[:, n], start=False, stop=False)
                return [mm(o_, lo, w_hi[:, n], start=False, stop=stop) for o_, n in pairs]

            def experts(passes):
                with pe.Fori(0, EXPERTS) as e:
                    E = e + EXPERTS * passes
                    pe.wait_ge(sel_ready, E + 1)
                    for h in range(2):
                        o_ = e_claim(E, "hg", h)
                        for j in range(4):
                            for g in range(G):
                                ins = mm(o_[:, j * P:(j + 1) * P], htok[:, g * D + (4 * h + j) * P:g * D + (4 * h + j + 1) * P],
                                         S[:, g * P:(g + 1) * P], start=(g == 0), stop=(g == 1))
                        e_full(ins, "hg", h)
                    o_ = e_claim(E, "ST")
                    for g in range(G):
                        ins = tr(o_[:, g * P:(g + 1) * P], S2[:, g * P:(g + 1) * P], ident)
                    e_full(ins, "ST")
                    e_await_copied(pe, E, "hg", 0)
                    e_await_copied(pe, E, "hg", 1)

                    def turn(i):
                        o_ = e_claim(E, "T", i)
                        e_await_copied(pe, E, "U", i)
                        for j in range(4):
                            ins = tr(o_[:, j * P:(j + 1) * P], act[:, (i % 2) * 512 + j * P:(i % 2) * 512 + (j + 1) * P], ident)
                        e_full(ins, "T", i)

                    for i in range(EC):
                        for kind, pn in (("g", "G"), ("u", "U")):
                            o_ = e_claim(E, pn, i)
                            for q in range(4):
                                j = 4 * EUIDX[kind, i] + q
                                pe.wait_ge(part_lo, E * EQ + (LO_BASE + j + 1))
                                w_hi, w_lo = split_part(j)
                                for c in range(2):
                                    k = 2 * q + c
                                    ks = slice(k * P, (k + 1) * P)
                                    ins = split_mm([(o_, slice(512 * c, 512 * c + 512))], hg_hi[:, ks], hg_lo[:, ks],
                                                   w_hi, w_lo, k == 0, k == KD - 1)[0]
                                if q < 3:
                                    ins.then_inc(part_used, 1)
                            e_full(ins, pn, i)
                        if i:
                            turn(i - 1)
                    ds = [(e_claim(E, "D", 0), slice(0, 512)), (e_claim(E, "D", 1), slice(512, 1024))]
                    for i in range(EC):
                        if i == TAIL:
                            turn(EC - 1)
                        e_await_copied(pe, E, "T", i)
                        for q in range(4):
                            j = 4 * EUIDX["d", i] + q
                            pe.wait_ge(part_lo, E * EQ + (LO_BASE + j + 1))
                            f = 4 * i + q
                            fs = slice(f * P, (f + 1) * P)
                            inss = split_mm(ds, eT_hi[:, fs], eT_lo[:, fs], *split_part(j), f == 0, f == 4 * EC - 1)
                            if f < 4 * EC - 1:
                                inss[1].then_inc(part_used, 1)
                    for n in range(2):
                        e_full(inss[n], "D", n)
                    e_await_copied(pe, E, "ST")
                    e_await_copied(pe, E, "D", 0)
                    e_await_copied(pe, E, "D", 1)
                    for g in range(G):
                        for n in range(2):
                            o_ = e_claim(E, "SC", g, n)
                            e_full(mm(o_, S2T[:, g * P:(g + 1) * P], yd[:, 512 * n:512 * n + 512],
                                      start=True, stop=True), "SC", g, n)

            for h in range(2):
                for g in range(G):
                    copied("htok", g, h)
            experts(0)
            pe.wait_ge(flag_ready, 1)
            over = pe.value_load(flag[0:1, 0:1], min_val=0, max_val=T)
            with pe.If(over > P):
                experts(1)

        @block.scalar
        def _(sc):
            st = Steps(sc, act_step)
            act_ = nc.scalar.activation

            def take(out, name, func=ACT.Copy, src=None, **kw):
                await_product(sc, *name)
                free(act_(out, bank(name) if src is None else src, func, **kw), *name)

            sc.dma_start(cst[:, :], a["const_tables"]).then_inc(consts_in, 16)
            cr = rows[:, P:2 * P]
            sc.dma_start(cr[0:KD, :], a["c_ctx"].rearrange("(c p) -> c p", p=P)).then_inc(vecs_in, 16)
            sc.dma_start(cr[KD:2 * KD, :], a["c"].rearrange("b (c p) -> (b c) p", p=P)).then_inc(vecs_in, 16)
            for l in range(DEPTH):
                b = 64 * l
                for name, n in (("b_mod", 48), ("cv_b", 4), ("cv_ln_g", 4), ("cv_ln_b", 4)):
                    sc.dma_start(rows[b:b + n, 0:P], a[name][l].rearrange("(c p) -> c p", p=P)).then_inc(vecs_in, 16)
                    b += n
                sc.dma_start(rows[b:b + 4, 0:P], a["gla_norm"][l]).then_inc(vecs_in, 16)
                sc.dma_start(rows[0:TAPS * CC, (2 + l) * P:(3 + l) * P],
                               a["cv_w"][l].rearrange("t (c p) -> (t c) p", p=P)).then_inc(vecs_in, 16)
            sc.dma_start(x[:, 0:D], a["x_prompt"][0]).then_inc(x_in, 16)
            sc.dma_start(x[:, D:2 * D], a["x_sample"][0]).then_inc(x_in, 16)
            sc.wait_ge(zeroed, 4)
            await_copied(sc, "vecs")
            act_(condT[:, 0:16].rearrange("p (k g) -> p g k", g=G), vecs[:, 128:144].rearrange("p (g k) -> p g k", g=G),
                 ACT.Silu).then_inc(cond_ready, 1)

            def mod_rows(l, i, buf):
                take(buf, ("mod", l, i))
                take(modraw[:, 32 * i:32 * i + 32].rearrange("p (c j g) -> p c j g", c=4, j=4), ("modT", l, i),
                     src=bank(("modT", l, i)).rearrange("p (c j r) -> p c j r", c=4, j=4)[:, :, :, 0:G])

            for i in EARLY:
                mod_rows(0, i, mrow)

            for l in range(DEPTH):
                def modulated(kind, sh, scl, g):
                    await_product(sc, kind, l, g, 1)
                    for j in range(4):
                        k = 4 + j
                        ins = act_(hT[:, k * T + g * P:k * T + (g + 1) * P], bank((kind, l, g, 1))[:, j * P:(j + 1) * P],
                                   ACT.Identity, bias=modcol(l, sh + k, g), scale=modcol(l, scl + k, g))
                    free(ins, kind, l, g, 1)

                def norm_sqrt(n):
                    for _ in range(n):
                        st.next(var_ready)
                        act_(stat[:, 40:41], stat[:, 39:40], ACT.Sqrt).then_inc(std_ready, 1)

                sc.wait_ge(mod_ready, 2 * l + 1)
                for g in range(G):
                    modulated("hT", 0, 8, g)
                    take(v[:, g * 512:(g + 1) * 512], ("v", l, g))
                    take(vb[:, g * 512:(g + 1) * 512], ("vb", l, g))
                    take(r[:, g * 512:(g + 1) * 512], ("r", l, g), ACT.Silu)
                for i in range(2):
                    take(gtmp[:, i * 512:(i + 1) * 512], ("cvg", l, i), ACT.Sigmoid)
                mod_rows(l, 4, mrow)
                take(kT, ("k", l))
                mod_rows(l, 5, mrow)
                for g in range(G):
                    s = gtmp[:, g * 512:(g + 1) * 512]
                    st.next(glog_part)
                    st.done(act_(s, s, ACT.Exp))
                    act_(s, s, ACT.Ln, bias=1.0).then_inc(glog_soft, 1)
                for i in range(2):
                    take(kbT[:, i * 512:(i + 1) * 512], ("kb", l, i))
                mod_rows(l, 6, mrow)
                for i in range(2):
                    await_product(sc, "qb", l, i)
                    for j in range(2):
                        for s in range(2):
                            h = 2 * (2 * i + j) + s
                            ins = act_(qbT[:, h * T:(h + 1) * T], bank(("qb", l, i))[:, j * T:(j + 1) * T], ACT.Copy,
                                       scale=half[s])
                    free(ins, "qb", l, i)
                mod_rows(l, 7, mrow)

                def gla_exps(g):
                    st.next(args_ready)
                    act_(qarg, qarg, ACT.Exp)
                    act_(ecum, cum[:, g * 512:(g + 1) * 512], ACT.Exp)
                    act_(klarg, klarg, ACT.Exp)
                    act_(karg, karg, ACT.Exp).then_inc(exps_ready, 1)

                def gla_keys(g):
                    await_product(sc, "keT", l, g)
                    for c in range(2):
                        ins = act_(ke[:, c * 512:(c + 1) * 512], bank(("keT", l, g)), ACT.Copy, scale=half[c])
                    free(ins, "keT", l, g)

                def gla_turned(g):
                    await_product(sc, "oT", l, g)
                    for j in range(4):
                        ins = act_(o[:, g * 512 + j * P:g * 512 + (j + 1) * P], bank(("oT", l, g))[:, j * P:(j + 1) * P],
                                   ACT.Copy, scale=vecs[:, 64 * l + 60 + j:64 * l + 61 + j])
                    free(ins, "oT", l, g)

                def mgate(n):
                    for g in range(G):
                        take(gates[:, g * 3 * D + n * 512:g * 3 * D + (n + 1) * 512], ("mg", l, g, n), ACT.Sigmoid)

                def gla_sqrt():
                    st.next(gla_var)
                    act_(stat[:, 50:54], stat[:, 42:46], ACT.Sqrt).then_inc(gla_std, 1)

                gla_exps(0)
                mgate(0)
                mod_rows(l, 8, mrow)
                gla_keys(0)
                mgate(1)
                mod_rows(l, 9, mrow)
                mgate(2)
                mod_rows(l, 10, mrow)
                gla_sqrt()
                mgate(3)
                mod_rows(l, 11, mrow)
                gla_turned(0)
                gla_exps(1)
                mgate(4)
                gla_keys(1)
                mgate(5)
                gla_sqrt()
                gla_turned(1)
                take(kbtok, ("kbtok", l))
                take(kctxT, ("kctxT", l))
                norm_sqrt(2)

                def softmax_exp(n):
                    st.next(P_arg)
                    act_(Pm[:, 0:n], Pm[:, 0:n], ACT.Exp).then_inc(P_exp, 1)

                for g in range(G):
                    await_product(sc, "cvT", l, g)
                    for j in range(4):
                        ins = act_(acc[:, g * 512 + j * P:g * 512 + (j + 1) * P], bank(("cvT", l, g))[:, j * P:(j + 1) * P],
                                   ACT.Silu, scale=vecs[:, 64 * l + 52 + j:64 * l + 53 + j],
                                   bias=vecs[:, 64 * l + 56 + j:64 * l + 57 + j])
                    free(ins, "cvT", l, g)
                softmax_exp(1024)
                for i in range(2):
                    take(PT[:, i * 512:(i + 1) * 512], ("PT", l, 0, i))
                softmax_exp(2048)
                take(attT[:, 0:512], ("attT", l, 0))
                for i in range(4):
                    take(PT[:, i * 512:(i + 1) * 512], ("PT", l, 1, i))
                take(attT[:, 512:1024], ("attT", l, 1))
                for g in range(G):
                    for n in range(2):
                        take(gbc1[:, g * D + n * 512:g * D + (n + 1) * 512], ("gbc", l, 0, g, n))
                for g in range(G):
                    for h in range(2):
                        await_product(sc, "mT", l, g, h)
                        for j in range(4):
                            k = 4 * h + j
                            ins = act_(hT[:, k * T + g * P:k * T + (g + 1) * P], bank(("mT", l, g, h))[:, j * P:(j + 1) * P],
                                       ACT.Copy)
                        free(ins, "mT", l, g, h)
                norm_sqrt(1)
                sc.wait_ge(mod_ready, 2 * l + 2)
                modulated("h2T", 24, 32, 0)
                if l == 0:
                    take(sil_d[:, 0:FCHUNKS[0][1]], ("G", 0, 0), ACT.Silu)
                norm_sqrt(1)
                modulated("h2T", 24, 32, 1)
                if l == 0:
                    take(sil_d[:, 512:512 + FCHUNKS[0][1]], ("G", 0, 1), ACT.Silu)
                sc.wait_ge(kv_stored, 32 * (l + 1))
                for g in range(G):
                    for n in range(2):
                        take(gbc2[:, g * D + n * 512:g * D + (n + 1) * 512], ("gbc", l, 1, g, n))
                if l == 0:
                    def dense_turned(i):
                        for g in range(G):
                            await_product(sc, "aT", i, g)
                            for j in range(FCHUNKS[i][1] // P):
                                f = FCHUNKS[i][0] // P + j
                                ins = act_(dT[:, f * T + g * P:f * T + (g + 1) * P], bank(("aT", i, g))[:, j * P:(j + 1) * P],
                                           ACT.Copy)
                            free(ins, "aT", i, g)

                    for i, (f0, fn) in enumerate(FCHUNKS):
                        if i:
                            for g in range(G):
                                await_copied(sc, "U", i - 1, g)
                                take(sil_d[:, g * 512:g * 512 + fn], ("G", i, g), ACT.Silu, src=bank(("G", i, g))[:, 0:fn])
                            dense_turned(i - 1)
                        if i in EARLY:
                            mod_rows(1, i, mrow2)
                    dense_turned(len(FCHUNKS) - 1)
                    norm_sqrt(2)
                else:
                    for g in range(G):
                        for h in range(2):
                            take(htok[:, g * D + h * 512:g * D + (h + 1) * 512], ("htok", g, h))
                    st.next(gate_arg)
                    act_(route[:, 100:102], route[:, 98:100], ACT.Exp).then_inc(gate_exp, 1)

            def experts(passes):
                with sc.Fori(0, EXPERTS) as e:
                    E = e + EXPERTS * passes

                    def e_take(out, *name, func=ACT.Copy, src=None):
                        e_await_product(sc, E, *name)
                        e_free(act_(out, ebank(name) if src is None else src, func), *name)

                    def high(out, *name):
                        e_await_product(sc, E, *name)
                        act_(out, ebank(name), ACT.Copy).then_inc(act_hi, 1)

                    for j in range(EQ):
                        if j == 3:
                            for h in range(2):
                                high(hg_hi[:, h * 512:(h + 1) * 512], "hg", h)
                            e_take(S2T, "ST", src=ebank(("ST",))[:, 0:256])
                        i = (j - 10) // 8
                        if j % 8 == 2 and 0 <= i < EC:
                            if i:
                                e_await_copied(sc, E, "U", i - 1)
                            else:
                                e_await_copied(sc, E, "U", EC - 1, back=1)
                            e_take(sil, "G", i, func=ACT.Silu)
                        if j % 8 == 6 and 0 < i < EC:
                            high(eT_hi[:, (i - 1) * 512:i * 512], "T", i - 1)
                        if j == LAST_TURN:
                            high(eT_hi[:, (EC - 1) * 512:EC * 512], "T", EC - 1)
                        s_ = (j // 4) % XRING
                        if j % 4 == 0:
                            sc.wait_ge(w_loaded[s_], E * (16 * EUPER[s_]) + 16 * (UBASE[s_] + j // 4 // XRING + 1))
                        await_part_free(sc, E, j)
                        act_(split_part(j)[0], raw_part(j), ACT.Copy).then_inc(part_hi, 1)
                    e_take(yd[:, 512:1024], "D", 1)

            experts(0)
            sc.wait_ge(flag_ready, 1)
            over = sc.value_load(flag[0:1, 0:1], min_val=0, max_val=T)
            with sc.If(over > P):
                experts(1)
            for _ in range(G):
                st.next(var_ready)
                act_(stat[:, 40:41], stat[:, 39:40], ACT.Sqrt).then_inc(std_ready, 1)

        @block.vector
        def _(dv):
            st = Steps(dv, dve_step)
            V = nc.vector

            def lag(ins, n):
                ins.then_inc(dve_step, 1)
                st.made[dve_step.name] += 1
                if st.made[dve_step.name] > n:
                    dv.wait_ge(dve_step, st.made[dve_step.name] - n)

            def settle():
                dv.wait_ge(dve_step, st.made[dve_step.name])

            def rstd(src_var, out):
                st.done(V.tensor_scalar(stat[:, 39:40], src_var, EPS, None, ALU.add), var_ready)
                st.next(std_ready)
                st.done(V.reciprocal(out, stat[:, 40:41]))

            def moments(halves):
                for i, h in enumerate(halves):
                    st.done(V.bn_stats(stat[:, 6 * i:6 * i + 6], h))
                st.done(V.bn_aggr(stat[:, 36:38], stat[:, 0:6 * len(halves)]))

            def layer_norm(xg, gain, bias_, sig):
                moments([xg[:, 0:512], xg[:, 512:1024]])
                rstd(stat[:, 37:38], stat[:, 38:39])
                st.done(V.tensor_scalar(xg, xg, stat[:, 36:37], stat[:, 38:39], ALU.subtract, ALU.mult))
                st.done(V.tensor_tensor(xg, xg, gain, ALU.mult))
                st.done(V.tensor_tensor(xg, xg, bias_, ALU.add), sig)

            await_product(dv, "vecs")
            freed(dv, V.tensor_copy(vecs[:, :], bank(("vecs",))[:, 0:392]), "vecs")

            for l in range(DEPTH):
                vl = 64 * l
                mod3 = modT[:, 96 * l:96 * (l + 1)].rearrange("p (c g) -> p c g", g=G)

                def mod_columns(u0, u1, scales):
                    for i in range(u0, u1):
                        await_copied(dv, "modT", l, i)
                    c0, c1 = 4 * u0, 4 * u1
                    st.done(V.tensor_reduce(mod3[:, c0:c1], modraw[:, 8 * c0:8 * c1].rearrange(
                        "p (c j g) -> p c g j", j=4, g=G), X, ALU.add))
                    st.done(V.tensor_tensor(mod3[:, c0:c1], mod3[:, c0:c1],
                                            vecs[:, vl + c0:vl + c1].unsqueeze(2).to_broadcast([P, c1 - c0, G]), ALU.add))
                    sc_ = modT[:, 96 * l + G * scales:96 * l + G * (scales + KD)]
                    st.done(V.tensor_scalar(sc_, sc_, 1.0, None, ALU.add), mod_ready)

                mod_columns(0, 4, 8)

                def modulated(kind, sh, scl, g):
                    await_product(dv, kind, l, g, 0)
                    for k in range(4):
                        ins = V.tensor_scalar(hT[:, k * T + g * P:k * T + (g + 1) * P],
                                              bank((kind, l, g, 0))[:, k * P:(k + 1) * P],
                                              modcol(l, scl + k, g), modcol(l, sh + k, g), ALU.mult, ALU.add)
                    free(ins, kind, l, g, 0)

                modulated("hT", 0, 8, 0)
                modulated("hT", 0, 8, 1)
                dv.wait_ge(zeroed, 4)
                z4 = z[:, :].rearrange("p (c g w) -> p c g w", c=CC, g=G)
                for i in range(2):
                    await_copied(dv, "cvg", l, i)
                    await_product(dv, "cva", l, i)
                    for j in range(2):
                        ins = V.tensor_tensor(z4[:, 2 * i + j, :, TAPS // 2:TAPS // 2 + P],
                                              bank(("cva", l, i))[:, j * T:(j + 1) * T].rearrange("p (g t) -> p g t", g=G),
                                              gtmp[:, i * 512 + j * T:i * 512 + (j + 1) * T].rearrange("p (g t) -> p g t", g=G),
                                              ALU.mult)
                    freed(dv, ins, "cva", l, i)
                await_product(dv, "gda", l)
                free(V.tensor_copy(gdaT[0:32, :], bank(("gda", l))[0:32, 0:T]), "gda", l)
                await_product(dv, "q", l)
                if l:
                    dv.wait_ge(kv_stored, 32 * l)
                freed(dv, V.tensor_scalar(qT, bank(("q", l)), GLA_DK ** -0.5, None, ALU.mult), "q", l)
                for g in range(G):
                    lg, tmp = glog[:, g * 512:(g + 1) * 512], gtmp[:, g * 512:(g + 1) * 512]
                    await_product(dv, "glog", l, g)
                    freed(dv, V.tensor_copy(lg, bank(("glog", l, g))), "glog", l, g)
                    st.done(V.scalar_tensor_tensor(out=tmp, in0=lg, scalar=-1.0, in1=lg, op0=ALU.mult, op1=ALU.min),
                            glog_part)
                for g in range(G):
                    lg, tmp = glog[:, g * 512:(g + 1) * 512], gtmp[:, g * 512:(g + 1) * 512]
                    st.next(glog_soft)
                    st.done(V.scalar_tensor_tensor(out=lg, in0=lg, scalar=0.0, in1=tmp, op0=ALU.min, op1=ALU.subtract),
                            glog_ready)
                await_copied(dv, "k", l)
                await_product(dv, "rope", l)
                o4 = bank(("rope", l)).rearrange("p (w h t) -> p w h t", w=2, h=HP)
                tmp = gtmp[:, 0:512].rearrange("p (w h t) -> p w h t", w=2, h=HP)
                sin_b = C("sin").unsqueeze(1).to_broadcast([P, 4, P])
                cos_b = C("cos").unsqueeze(1).to_broadcast([P, HP, P])
                freed(dv, V.tensor_tensor(gtmp[:, 0:512].rearrange("p (w t) -> p w t", w=4),
                                          bank(("rope", l)).rearrange("p (w t) -> p w t", w=4), sin_b, ALU.mult), "rope", l)
                for n, w in enumerate((qT, kT)):
                    s = w.rearrange("p (h t) -> p h t", h=HP)[:, :, P:T]
                    st.done(V.tensor_tensor(s, s, cos_b, ALU.mult))
                    st.done(V.tensor_tensor(s, s, tmp[:, n], ALU.add))
                for g in range(G):
                    await_product(dv, "cum", l, g)
                    freed(dv, V.tensor_scalar(cum[:, g * 512:(g + 1) * 512], bank(("cum", l, g)), 1.0 / TAU, None,
                                              ALU.mult), "cum", l, g)

                def gla_prepare(g):
                    if g:
                        await_product(dv, "o", l, 0)
                        dv.wait_ge(state_stored, 32 * (l + 1))
                    cg = cum[:, g * 512:(g + 1) * 512]
                    for dr in range(2):
                        cd = cg[:, dr * 256:(dr + 1) * 256]
                        first = 0 if dr == 0 else SUB - 1
                        end = CHUNK - 1 if dr == 0 else 0
                        V.tensor_tensor(qarg[:, dr * 256:(dr + 1) * 256].rearrange("p (b s) -> p b s", s=SUB),
                                        cd.rearrange("p (b s) -> p b s", s=SUB),
                                        cd[:, first:256:SUB].unsqueeze(2).to_broadcast([P, 16, SUB]), ALU.subtract)
                        V.tensor_tensor(klarg[:, dr * 256:(dr + 1) * 256].rearrange("p (c s) -> p c s", s=CHUNK),
                                        cd[:, end:256:CHUNK].unsqueeze(2).to_broadcast([P, 4, CHUNK]),
                                        cd.rearrange("p (c s) -> p c s", s=CHUNK), ALU.subtract)
                        for hp in range(HP):
                            ch = cd[:, hp * P:(hp + 1) * P]
                            kd = karg[:, (dr * HP + hp) * 512:(dr * HP + hp + 1) * 512]
                            for c in range(2):
                                kc = kd[:, c * 256:(c + 1) * 256].rearrange("p (b s) -> p b s", s=CHUNK)
                                lag(V.tensor_tensor(kc, ch[:, c * CHUNK + first:(c + 1) * CHUNK:SUB].unsqueeze(2)
                                                    .to_broadcast([P, 4, CHUNK]),
                                                    ch[:, c * CHUNK:(c + 1) * CHUNK].unsqueeze(1)
                                                    .to_broadcast([P, 4, CHUNK]), ALU.subtract), 99999)
                    settle()
                    st.done(V.tensor_scalar(karg, karg, EXP_CAP, None, ALU.min), args_ready)
                    st.next(exps_ready)
                    qg = [w.rearrange("p (h t) -> p h t", h=HP)[:, :, g * P:(g + 1) * P] for w in (qT, kT)]
                    for dr in range(2):
                        for dst, e_ in ((qpad, qarg), (qepad, ecum)):
                            d4 = dst[:, dr * 512:(dr + 1) * 512].rearrange("p (h a t) -> p h a t", h=HP, a=2)
                            e3 = e_[:, dr * 256:(dr + 1) * 256].rearrange("p (h t) -> p h t", h=HP)
                            for s in range(2):
                                V.scalar_tensor_tensor(out=d4[:, :, s, :], in0=qg[0], scalar=half[s], in1=e3,
                                                       op0=ALU.mult, op1=ALU.mult)
                        kl = klarg[:, dr * 256:(dr + 1) * 256].rearrange("p (h t) -> p h t", h=HP)
                        V.tensor_tensor(kl, kl, qg[1], ALU.mult)
                        for hp in range(HP):
                            kd = karg[:, (dr * HP + hp) * 512:(dr * HP + hp + 1) * 512].rearrange(
                                "p (c b s) -> p c b s", c=2, b=4)
                            kk = qg[1][:, hp, :].rearrange("p (c s) -> p c s", c=2).unsqueeze(2)\
                                .to_broadcast([P, 2, 4, CHUNK])
                            ins = V.tensor_tensor(kd, kd, kk, ALU.mult)
                    st.done(ins, gla_ready)

                def gla_mask(g):
                    A3 = A[:, :].rearrange("p (h t) -> p h t", h=GLA_H)
                    T3 = gtmp[:, 0:512].rearrange("p (h t) -> p h t", h=GLA_H)
                    if g:
                        await_product(dv, "o", l, 0)
                    elif l:
                        await_product(dv, "o", l - 1, 1)
                    for dr, dst in ((0, A3), (1, T3)):
                        await_product(dv, "att", l, g, dr)
                        src = bank(("att", l, g, dr)).rearrange("p (h t) -> p h t", h=GLA_H)
                        for c in range(2):
                            q = slice(64 * c, 64 * c + 64)
                            m = C("mask_f" if dr == 0 else "mask_b")[q, q].unsqueeze(1).to_broadcast([64, GLA_H, 64])
                            ins = V.tensor_tensor(dst[q, :, q], src[q, :, q], m, ALU.mult)
                        freed(dv, ins, "att", l, g, dr)
                    for c in range(2):
                        q = slice(64 * c, 64 * c + 64)
                        ins = V.tensor_tensor(A3[q, :, q], A3[q, :, q], T3[q, :, q], ALU.add)
                    st.done(ins, A_ready)

                def gla_carry(g):
                    if g:
                        dv.wait_ge(state_in, 32 * (l + 1))
                        await_product(dv, "o", l, 0)
                    for dr in range(2):
                        await_product(dv, "kv", l, g, dr)
                        kv = bank(("kv", l, g, dr))
                        c0 = 0 if dr == 0 else 1
                        end = CHUNK - 1 if dr == 0 else 0
                        for hp in range(HP):
                            j = dr * HP + hp
                            s1 = S1[:, j * P:(j + 1) * P]
                            first = kv[:, (c0 * HP + hp) * P:(c0 * HP + hp + 1) * P]
                            second = kv[:, ((1 - c0) * HP + hp) * P:((1 - c0) * HP + hp + 1) * P]

                            def decay(c):
                                t = j * P + c * CHUNK + end
                                return ecum[:, t:t + 1]

                            if g == 0:
                                st.done(V.tensor_copy(s1, first))
                                ins = V.scalar_tensor_tensor(out=qarg[:, j * P:(j + 1) * P], in0=s1, scalar=decay(1 - c0),
                                                             in1=second, op0=ALU.mult, op1=ALU.add)
                            else:
                                ins = V.scalar_tensor_tensor(out=s1, in0=S0[:, j * P:(j + 1) * P], scalar=decay(c0),
                                                             in1=first, op0=ALU.mult, op1=ALU.add)
                        freed(dv, ins, "kv", l, g, dr)

                def gla_norm(g):
                    og = o[:, g * 512:(g + 1) * 512]
                    o3 = og.rearrange("p (h v) -> p h v", h=GLA_H)
                    sq = gtmp[:, 512:1024]
                    await_product(dv, "o", l, g)
                    freed(dv, V.tensor_copy(og, bank(("o", l, g))), "o", l, g)
                    st.done(V.tensor_tensor(sq, og, og, ALU.mult))
                    st.done(V.tensor_reduce(stat[:, 42:46], sq.rearrange("p (h v) -> p h v", h=GLA_H), X, ALU.add))
                    st.done(V.tensor_scalar(stat[:, 42:46], stat[:, 42:46], 1.0 / GLA_DV, EPS, ALU.mult, ALU.add), gla_var)
                    st.next(gla_std)
                    st.done(V.reciprocal(stat[:, 46:50], stat[:, 50:54]))
                    st.done(V.tensor_tensor(o3, o3, stat[:, 46:50].unsqueeze(2).to_broadcast([P, GLA_H, GLA_DV]), ALU.mult))
                    await_copied(dv, "r", l, g)
                    st.done(V.tensor_tensor(og, og, r[:, g * 512:(g + 1) * 512], ALU.mult), o_ready)

                def conv_taps(t0, t1):
                    if t0 == 0 and l:
                        await_product(dv, "y", l - 1, 2, 1, 1)
                    a4 = acc.rearrange("p (g c t) -> p c g t", g=G, c=CC)
                    for t in range(t0, t1):
                        for c in range(CC):
                            src = z4[:, c, :, t:t + P]
                            w = vecs[:, 144 + 124 * l + t * CC + c:145 + 124 * l + t * CC + c]
                            if t == 0:
                                ins = V.tensor_scalar(a4[:, c], src, w, vecs[:, vl + 48 + c:vl + 49 + c], ALU.mult, ALU.add)
                            else:
                                ins = V.scalar_tensor_tensor(out=a4[:, c], in0=src, scalar=w, in1=a4[:, c],
                                                             op0=ALU.mult, op1=ALU.add)
                            if t == TAPS - 1 and c == CC - 1:
                                ins.then_inc(conv_summed, 1)
                            else:
                                lag(ins, CC - 1)

                def conv_norm():
                    for g in range(G):
                        await_product(dv, "cvtok", l, g)
                        b = bank(("cvtok", l, g))
                        moments([b])
                        rstd(stat[:, 37:38], stat[:, 38:39])
                        freed(dv, V.tensor_scalar(acc[:, g * 512:(g + 1) * 512], b, stat[:, 36:37], stat[:, 38:39],
                                                  ALU.subtract, ALU.mult), "cvtok", l, g)

                def softmax(g):
                    keys = P * (1 + g)
                    n = NA_H * keys
                    Pn = Pm[:, 0:n]
                    P4 = Pn.rearrange("p (h k) -> p h k", h=NA_H)
                    if g:
                        await_product(dv, "PT", l, 0, 1)
                        b3 = bias.rearrange("p (h k) -> p h k", h=NA_H)
                    for i in range(2 * (1 + g)):
                        await_product(dv, "sc", l, g, i)
                        s = bank(("sc", l, g, i))
                        if g == 0:
                            free(V.tensor_scalar(Pn[:, i * 512:(i + 1) * 512], s, NA_DH ** -0.5, None, ALU.mult), "sc", l, g, i)
                        else:
                            s3 = s.rearrange("p (h k) -> p h k", h=2)
                            d3 = P4[:, 2 * i:2 * i + 2, :]
                            V.scalar_tensor_tensor(out=d3[:, :, 0:P], in0=s3[:, :, 0:P], scalar=NA_DH ** -0.5,
                                                   in1=b3[:, 2 * i:2 * i + 2, :], op0=ALU.mult, op1=ALU.add)
                            free(V.tensor_scalar(d3[:, :, P:2 * P], s3[:, :, P:2 * P], NA_DH ** -0.5, None, ALU.mult),
                                 "sc", l, g, i)
                    await_copied(dv, "sc", l, g, 2 * (1 + g) - 1)
                    st.done(V.tensor_reduce(stat[:, 12:20], P4, X, ALU.max))
                    st.done(V.tensor_tensor(P4, P4, stat[:, 12:20].unsqueeze(2).to_broadcast([P, NA_H, keys]),
                                            ALU.subtract), P_arg)
                    st.next(P_exp)
                    st.done(V.tensor_reduce(stat[:, 20:28], P4, X, ALU.add))
                    st.done(V.reciprocal(stat[:, 28:36], stat[:, 20:28]))
                    st.done(V.tensor_tensor(P4, P4, stat[:, 28:36].unsqueeze(2).to_broadcast([P, NA_H, keys]),
                                            ALU.mult), P_ready)

                gla_prepare(0)
                conv_taps(0, 12)
                gla_mask(0)
                gla_carry(0)
                gla_norm(0)
                gla_prepare(1)
                conv_taps(12, 22)
                gla_mask(1)
                gla_carry(1)
                gla_norm(1)
                conv_taps(22, TAPS)
                mod_columns(4, 12, 32)
                await_product(dv, "bias", l, 1)
                for i in range(2):
                    freed(dv, V.tensor_tensor(bias[:, i * 512:(i + 1) * 512].rearrange("p (h k) -> p h k", h=4),
                                              bank(("bias", l, i)).rearrange("p (h k) -> p h k", h=4),
                                              C("window").unsqueeze(1).to_broadcast([P, 4, P]), ALU.add), "bias", l, i)
                conv_norm()
                softmax(0)
                softmax(1)

                def diagonal(dst, c0, j):
                    for g in range(G):
                        ins = V.tensor_tensor(dst[:, g * D:(g + 1) * D].rearrange("p (c n) -> p c n", c=KD),
                                              ident.unsqueeze(1).to_broadcast([P, KD, P]),
                                              mod3[:, c0:c0 + KD, g:g + 1].to_broadcast([P, KD, P]), ALU.mult)
                    st.done(ins, diag_ready)

                def gated(b):
                    for g in range(G):
                        for n in range(2):
                            await_copied(dv, "mg", l, g, 2 * b + n)
                            await_product(dv, "y", l, b, g, n)
                            s = gates[:, g * 3 * D + b * D + 512 * n:g * 3 * D + b * D + 512 * n + 512]
                            free(V.tensor_tensor(s, s, bank(("y", l, b, g, n)), ALU.mult), "y", l, b, g, n)

                gated(0)
                gated(2)
                diagonal(diag1, 16, 0)
                gated(1)
                await_copied(dv, "y", l, 1, 1, 1)
                for g in range(G):
                    m = [gates[:, g * 3 * D + b * D:g * 3 * D + (b + 1) * D] for b in range(3)]
                    st.done(V.tensor_tensor(m[0], m[0], m[1], ALU.add))
                    st.done(V.tensor_tensor(m[0], m[0], m[2], ALU.add), m_ready)

                def block_norm(j, lnw, gbc, name, sig, g):
                    dv.wait_ge(ln_in, 32 * (2 * l + j + 1))
                    for n in range(2):
                        xs = x[:, g * D + 512 * n:g * D + 512 * n + 512]
                        tmp = mtmp[:, 0:512] if j == 0 else ftmp[:, 0:512]
                        await_copied(dv, "gbc", l, j, g, n)
                        await_product(dv, *name(g, n))
                        freed(dv, V.tensor_tensor(tmp, gbc[:, g * D + 512 * n:g * D + 512 * n + 512],
                                                  bank(name(g, n)), ALU.mult), *name(g, n))
                        st.done(V.scalar_tensor_tensor(out=xs, in0=xs, scalar=ALPHA, in1=tmp, op0=ALU.mult,
                                                       op1=ALU.add))
                    layer_norm(x[:, g * D:(g + 1) * D], lnw[:, 0:D], lnw[:, D:2 * D], sig)

                def dense_act(i, g):
                    fn = FCHUNKS[i][1]
                    if i:
                        await_product(dv, "aT", i - 1, g)
                    await_copied(dv, "G", i, g)
                    await_product(dv, "U", i, g)
                    free(V.tensor_tensor(act_d[:, g * 512:g * 512 + fn], sil_d[:, g * 512:g * 512 + fn],
                                         bank(("U", i, g))[:, 0:fn], ALU.mult), "U", i, g)

                for g in range(G):
                    block_norm(0, ln1, gbc1, lambda g, n: ("mix", l, g, n), x_ready, g)
                    modulated("h2T", 24, 32, g)
                    if l == 0:
                        dense_act(0, g)
                await_product(dv, "h2T", l, 1, 1)
                diagonal(diag2, 40, 1)
                if l == 0:
                    for i in range(1, len(FCHUNKS)):
                        for g in range(G):
                            dense_act(i, g)
                    for g in range(G):
                        block_norm(1, ln2, gbc2, lambda g, n: ("Y", g, n), x_ready, g)

            def R(i, n):
                return route[:, i:i + n]

            def GE(i):
                return R(i, 16).rearrange("p (g e) -> p g e", g=G)

            def EG(i):
                return R(i, 16).rearrange("p (e g) -> p g e", g=G)

            def over_e(i):
                return R(i, G).unsqueeze(2).to_broadcast([P, G, EXPERTS])

            LOG, TMP, TOP1, TOP2, MASK, V1, V2, AT, DIFF, GATE1, GATE2, NUM = 0, 16, 32, 48, 64, 80, 82, 84, 98, 102, 104, 106
            nums = R(NUM, EXPERTS).unsqueeze(1).to_broadcast([P, G, EXPERTS])
            st.done(V.memset(route[:, 128:256], -BIG))
            V.memset(moe_y, 0.0).then_inc(part_lo, LO_BASE)
            st.done(V.tensor_scalar(R(NUM, EXPERTS), C("slots")[:, 0:EXPERTS], -1.0 * EXPERTS, None, ALU.add))
            await_product(dv, "logits")
            freed(dv, V.tensor_copy(R(LOG, 16), bank(("logits",))[:, 0:16]), "logits")

            def pick(src, top, onehot):
                st.done(V.tensor_reduce(R(top, G), GE(src), X, ALU.max))
                st.done(V.tensor_tensor(GE(onehot), GE(src), over_e(top), ALU.is_equal))
                st.done(V.tensor_tensor(GE(onehot), GE(onehot), nums, ALU.mult))
                st.done(V.tensor_reduce(R(AT, G), GE(onehot), X, ALU.min))
                st.done(V.tensor_tensor(GE(onehot), nums, over_e(AT), ALU.is_equal))

            pick(LOG, V1, TOP1)
            st.done(V.scalar_tensor_tensor(out=R(TMP, 16), in0=R(TOP1, 16), scalar=-1e30, in1=R(LOG, 16),
                                           op0=ALU.mult, op1=ALU.add))
            pick(TMP, V2, TOP2)
            st.done(V.tensor_tensor(R(MASK, 16), R(TOP1, 16), R(TOP2, 16), ALU.add), mask_ready)
            st.done(V.tensor_tensor(R(DIFF, 2), R(V2, 2), R(V1, 2), ALU.subtract), gate_arg)
            st.next(gate_exp)
            st.done(V.tensor_scalar(R(GATE1, 2), R(100, 2), 1.0, None, ALU.add))
            st.done(V.reciprocal(R(GATE1, 2), R(GATE1, 2)))
            st.done(V.tensor_tensor(R(GATE2, 2), R(100, 2), R(GATE1, 2), ALU.mult))
            st.done(V.tensor_tensor(GE(TOP1), GE(TOP1), over_e(GATE1), ALU.mult))
            st.done(V.tensor_tensor(GE(TOP2), GE(TOP2), over_e(GATE2), ALU.mult))
            POS, WT = 128, 192
            for n in range(2):
                st.done(V.tensor_tensor(EG(WT + 16 * n), GE(TOP1), GE(TOP2), ALU.add))
            await_product(dv, "rank")
            rank = bank(("rank",))
            st.done(V.tensor_scalar(R(TMP, 16), rank[:, 0:16], BIG, None, ALU.add))
            st.done(V.tensor_tensor(R(TMP, 16), R(TMP, 16), R(MASK, 16), ALU.mult))
            st.done(V.tensor_scalar(EG(POS), GE(TMP), -BIG, None, ALU.add))
            st.done(V.tensor_scalar(EG(POS + 16), GE(TMP), -BIG - P, None, ALU.add))
            freed(dv, V.tensor_reduce(R(DIFF, 1), rank[:, 16:24], X, ALU.max), "rank")
            st.done(V.tensor_copy(flag[:, :], R(DIFF, 1)), flag_ready)

            def select(E):
                for g in range(G):
                    pos = route[:, bass.ds(POS + 2 * E + g, 1)]
                    wt = route[:, bass.ds(WT + 2 * E + g, 1)]
                    V.tensor_scalar(S[:, g * P:(g + 1) * P], C("slots"), pos, None, ALU.is_equal)
                    ins = V.tensor_scalar(S2[:, g * P:(g + 1) * P], C("slots"), pos, wt, ALU.is_equal, ALU.mult)
                ins.then_inc(sel_ready, 1)

            def experts(passes):
                with dv.Fori(0, EXPERTS) as e:
                    E = e + EXPERTS * passes
                    def low(hi, lo, n, *name):
                        dv.wait_ge(act_hi, E * HI_PER + n)
                        e_free(V.tensor_tensor(lo, ebank(name), hi.bitcast(F32), ALU.subtract), *name)

                    for j in range(EQ):
                        if j == 3:
                            for h in range(2):
                                hs = slice(h * 512, (h + 1) * 512)
                                low(hg_hi[:, hs], hg_lo[:, hs], h + 1, "hg", h)
                            e_await_product(dv, E, "ST")
                            select(E + 1)
                        i = (j - 14) // 8
                        if j % 8 == 6 and 0 <= i < EC:
                            if i >= 2:
                                e_await_product(dv, E, "T", i - 2)
                            e_await_copied(dv, E, "G", i)
                            e_await_product(dv, E, "U", i)
                            b = slice((i % 2) * 512, (i % 2 + 1) * 512)
                            e_free(V.tensor_tensor(act[:, b], sil, ebank(("U", i)), ALU.mult), "U", i)
                            if i:
                                fs = slice((i - 1) * 512, i * 512)
                                low(eT_hi[:, fs], eT_lo[:, fs], 2 + i, "T", i - 1)
                        if j == LAST_TURN:
                            fs = slice((EC - 1) * 512, EC * 512)
                            low(eT_hi[:, fs], eT_lo[:, fs], 2 + EC, "T", EC - 1)
                        dv.wait_ge(part_hi, E * EQ + j + 1)
                        w_hi, w_lo = split_part(j)
                        V.tensor_tensor(w_lo, raw_part(j), w_hi.bitcast(F32), ALU.subtract).then_inc(part_lo, 1)
                    e_await_product(dv, E, "D", 0)
                    e_free(V.tensor_copy(yd[:, 0:512], ebank(("D", 0))), "D", 0)
                    for g in range(G):
                        for n in range(2):
                            e_await_product(dv, E, "SC", g, n)
                            y = moe_y[:, g * D + 512 * n:g * D + 512 * n + 512]
                            e_free(V.tensor_tensor(y, y, ebank(("SC", g, n)), ALU.add), "SC", g, n)
                    e_await_copied(dv, E, "SC", 1, 1)

            select(0)
            dv.wait_ge(part_lo, LO_BASE)
            experts(0)
            over = dv.value_load(flag[0:1, 0:1], min_val=0, max_val=T)
            with dv.If(over > P):
                experts(1)
            dv.wait_ge(ln_in, 32 * 2 * DEPTH)
            await_copied(dv, "gbc", DEPTH - 1, 1, 1, 1)
            for g in range(G):
                xg, yg = x[:, g * D:(g + 1) * D], moe_y[:, g * D:(g + 1) * D]
                st.done(V.tensor_tensor(yg, yg, gbc2[:, g * D:(g + 1) * D], ALU.mult))
                st.done(V.scalar_tensor_tensor(out=xg, in0=xg, scalar=ALPHA, in1=yg, op0=ALU.mult, op1=ALU.add))
                layer_norm(xg, ln2[:, 0:D], ln2[:, D:2 * D], y_ready)


_INS = ["x_prompt", "x_sample", "cache_na_k", "cache_na_v", "state_gla", "c", "c_ctx", "w_mod", "b_mod", "w_in",
        "gla_w_gup", "gla_b_g", "gla_norm", "w_br_gla", "na_rpb", "w_br_na", "cv_w", "cv_b", "cv_ln_g", "cv_ln_b",
        "w_br_cv", "w_out", "ln_g", "ln_b", "ffd_w_gate", "ffd_w_up", "ffd_w_down",
        "moe_w_router", "moe_w_gate", "moe_w_up", "moe_w_down"]
_OUTS = [(1, P, D), (1, P, D), (1, DEPTH, P, NA_H, NA_DH), (1, DEPTH, P, NA_H, NA_DH),
         (1, DEPTH, 2, GLA_H, GLA_DK, GLA_DV)]


def kernel(**inputs):
    import numpy as _np
    import concourse.bacc as _bacc
    from concourse.bass_utils import run_bass_kernel_spmd as _run

    nc = _bacc.Bacc("TRN2", target_bir_lowering=False, num_devices=1)
    arrays, args = {}, {}
    for name in _INS:
        arrays[f"in_{name}"] = _np.ascontiguousarray(inputs[name])
        args[name] = nc.dram_tensor(f"in_{name}", arrays[f"in_{name}"].shape, F32, kind="ExternalInput").ap()
    arrays["const_tables"] = shape_constants()
    args["const_tables"] = nc.dram_tensor("const_tables", arrays["const_tables"].shape, F32, kind="ExternalInput").ap()
    outs = [nc.dram_tensor(f"out_{i}", shape, F32, kind="ExternalOutput").ap() for i, shape in enumerate(_OUTS)]
    build(nc, args, outs)
    r = _run(nc, [arrays], core_ids=[0])
    return tuple(r.results[0][f"out_{i}"] for i in range(len(_OUTS)))
```

```python
from collections import Counter
from contextlib import ExitStack

import numpy as np

import concourse.bass as bass
from concourse import mybir

F32 = mybir.dt.float32
F32R = mybir.dt.float32r
I32 = mybir.dt.int32
ALU = mybir.AluOpType
ACT = mybir.ActivationFunctionType
X = mybir.AxisListType.X

P = 128
G = 2
T = G * P
D = 1024
KD = D // P
DEPTH = 2
GLA_H, GLA_DK, GLA_DV, RANK, CHUNK, SUB = 4, 64, 128, 16, 64, 16
HP = GLA_H * GLA_DK // P
NA_H, NA_DH = 8, 64
PAIRS = NA_H // 2
CONV, TAPS = 512, 31
CC = CONV // P
ZW = P + TAPS - 1
FF_D, FF_E, EXPERTS = 2816, 3584, 8
GRID_W, WIN_R, WIN_C = 64, 8, 16
EPS = 1e-5
ALPHA = (2 * DEPTH) ** 0.25
TAU = 16.0
BIG = 1000.0
EXP_CAP = 80.0
RING = 4
XRING = 3
W = 4096
PART = W // 4
PARTS = 6

SPLIT = dict(qk=0, v=512, r=1024, gda=1536, qb=1568, kb=2080, vb=2592, cva=3104, cvg=3616, mg=4128)
MG = [f"mg{n}" for n in range(6)]
SPLIT.update({m: 4128 + 512 * n for n, m in enumerate(MG)})

CONSTS = ["ident", "mask_f", "mask_b", "rot", "cos", "sin", "window", "slots", "before", "ones", "flip"]


def shape_constants():
    i = np.arange(P)
    r, c = i[:, None], i[None, :]
    same = r // CHUNK == c // CHUNK
    t = {"ident": r == c, "ones": np.ones((P, P)), "before": r < c}
    t["flip"] = (r // GRID_W == c // GRID_W) & (r % GRID_W + c % GRID_W == GRID_W - 1)
    t["mask_f"] = same & (r <= c)
    t["mask_b"] = same & (r >= c)
    rot = np.zeros((P, P))
    n = GLA_DK // 4
    for m in range(P):
        rot[m + n if m % (2 * n) < n else m - n, m] = -1.0 if m % (2 * n) < n else 1.0
    t["rot"] = rot
    inv = np.float32(10000.0) ** (-np.arange(n, dtype=np.float32) / np.float32(n))
    d = i % GLA_DK
    pos = np.where((d < GLA_DK // 2)[:, None], c // GRID_W, c % GRID_W).astype(np.float32)
    ang = pos * inv[d % n][:, None].astype(np.float32)
    t["cos"], t["sin"] = np.cos(ang), np.sin(ang)
    start = np.clip(r % GRID_W - WIN_C // 2, 0, GRID_W - WIN_C)
    t["window"] = np.where((c % GRID_W >= start) & (c % GRID_W < start + WIN_C), 0.0, -1e30)
    t["slots"] = np.broadcast_to(c, (P, P))
    half = np.stack([i < 64, i >= 64], 1)
    return np.concatenate([np.asarray(t[k], np.float32) for k in CONSTS] + [half.astype(np.float32)], 1)


FCHUNKS = [(a, min(512, FF_D - a)) for a in range(0, FF_D, 512)]


EARLY = range(4)
MSPLIT = ("v", "vb", "r", "cva", "cvg", "qk", "kb", "qb")
COLUMNS = {"cva": (("cva", 0), ("cva", 1)), "cvg": (("cvg", 0), ("cvg", 1)), "qk": (("q",), ("k",)),
           "kb": (("kb", 0), ("kb", 1)), "qb": (("qb", 0), ("qb", 1))}


def plan():
    prods, units = [("vecs",)], []
    last = {}

    def p(*name):
        prods.append(name)

    def u(name, *users):
        units.append(name)
        last[name] = users[-1]

    def mod(l, i):
        p("mod", l, i), p("modT", l, i)
        u(("mod", l, i), ("mod", l, i))

    def w_token(l, name):
        for g in range(G):
            p(name, l, g)
        u((name, l), (name, l, G - 1))

    def mg(l, n):
        p("mg", l, 0, n), p("mg", l, 1, n)
        u((MG[n], l), ("mg", l, 1, n))

    for i in EARLY:
        mod(0, i)
    for l in range(DEPTH):
        if l:
            mod(l, 4)
        for g in range(G):
            p("hT", l, g, 0), p("hT", l, g, 1)
            if l and g == 0:
                mod(l, 5)
            p("v", l, g)
        u(("v", l), ("v", l, 1))
        w_token(l, "vb"), w_token(l, "r")
        for i in range(2):
            p("cva", l, i)
        for i in range(2):
            p("cvg", l, i)
        u(("cva", l), ("cva", l, 1)), u(("cvg", l), ("cvg", l, 1))
        if l == 0:
            mod(l, 4)
        p("gda", l), p("q", l), p("k", l)
        u(("qk", l), ("k", l))
        if l == 0:
            mod(l, 5)
        p("glog", l, 0), p("glog", l, 1)
        p("kb", l, 0), p("kb", l, 1), u(("kb", l), ("kb", l, 1))
        p("rope", l)
        mod(l, 6)
        p("cum", l, 0), p("cum", l, 1)
        p("qb", l, 0), p("qb", l, 1), u(("qb", l), ("qb", l, 1))
        mod(l, 7)
        mg(l, 0)
        mod(l, 8)
        p("keT", l, 0), p("att", l, 0, 0), p("att", l, 0, 1)
        mg(l, 1)
        mod(l, 9)
        p("kv", l, 0, 0), p("kv", l, 0, 1)
        mg(l, 2)
        p("o", l, 0)
        mg(l, 3)
        p("oT", l, 0)
        mg(l, 4)
        p("keT", l, 1), p("att", l, 1, 0), p("att", l, 1, 1)
        mg(l, 5)
        p("kv", l, 1, 0), p("kv", l, 1, 1)
        p("o", l, 1), p("oT", l, 1)
        p("kbtok", l), p("kctxT", l), p("bias", l, 0), p("bias", l, 1)
        p("sc", l, 0, 0), p("sc", l, 0, 1)
        p("cvtok", l, 0), p("cvtok", l, 1)
        p("cvT", l, 0), p("cvT", l, 1)
        p("PT", l, 0, 0), p("PT", l, 0, 1)
        for i in range(4):
            p("sc", l, 1, i)
        for b in (0, 2):
            for g in range(G):
                p("y", l, b, g, 0), p("y", l, b, g, 1)
            u(("br", l, b), ("y", l, b, 1, 1))
        p("attT", l, 0)
        for i in range(4):
            p("PT", l, 1, i)
        p("attT", l, 1)
        for g in range(G):
            p("y", l, 1, g, 0), p("y", l, 1, g, 1)
        u(("br", l, 1), ("y", l, 1, 1, 1))
        for g in range(G):
            p("gbc", l, 0, g, 0), p("gbc", l, 0, g, 1)
        mod(l, 10)
        for g in range(G):
            p("mT", l, g, 0), p("mT", l, g, 1)
        for g in range(G):
            p("mix", l, g, 0), p("mix", l, g, 1)
        u(("out", l, 0), ("mix", l, 1, 0)), u(("out", l, 1), ("mix", l, 1, 1))
        mod(l, 11)
        for g in range(G):
            p("h2T", l, g, 0), p("h2T", l, g, 1)
            if l == 0:
                p("G", 0, g)
        if l == 0:
            p("U", 0, 0), p("U", 0, 1)
            u(("wg", 0), ("G", 0, 1)), u(("wu", 0), ("U", 0, 1))
        for g in range(G):
            p("gbc", l, 1, g, 0), p("gbc", l, 1, g, 1)
        if l == 0:
            for i in range(len(FCHUNKS)):
                if i:
                    p("G", i, 0), p("G", i, 1), p("U", i, 0), p("U", i, 1)
                    u(("wg", i), ("G", i, 1)), u(("wu", i), ("U", i, 1))
                    p("aT", i - 1, 0), p("aT", i - 1, 1)
                if i in EARLY:
                    mod(1, i)
            for g in range(G):
                p("Y", g, 0), p("Y", g, 1)
            p("aT", len(FCHUNKS) - 1, 0), p("aT", len(FCHUNKS) - 1, 1)
            for i in range(len(FCHUNKS)):
                u(("wd", i), ("Y", 1, 1))
        else:
            for g in range(G):
                p("htok", g, 0), p("htok", g, 1)
            p("logits",), p("rank",)
    return prods, units, last


PRODS, UNITS, LAST = plan()
PIDX = {n: i for i, n in enumerate(PRODS)}
UIDX = {n: i for i, n in enumerate(UNITS)}
NB = 8
PBASE = [len([i for i in range(len(PRODS)) if i % NB == b]) for b in range(NB)]

SLOT, NTH, BEFORE = [], [], []
_first = 0
for _i, _u in enumerate(UNITS):
    if _u in (("wg", 0), ("v", 1)):
        _first = _i
    SLOT.append((_i - _first) % (XRING if ("wg", 0) in UNITS[:_i + 1] and ("v", 1) not in UNITS[:_i + 1] else RING))
    _same = [_j for _j in range(_i) if SLOT[_j] == SLOT[_i]]
    NTH.append(len(_same) + 1)
    BEFORE.append(UNITS[_same[-1]] if _same else None)
UBASE = [SLOT.count(s) for s in range(XRING)]

DQ, DUSED, DFIRST = [], [], {}
DPARTS = 4
_n = 0
_mixer = [[(k, l) for k in MSPLIT] for l in range(DEPTH)]
_dense = [(k, i) for i in range(len(FCHUNKS)) for k in ("wg", "wu")] + [("wd", i) for i in range(len(FCHUNKS))]
PHASE = {}
for _name, _us in (("mixer0", _mixer[0]), ("dense", _dense), ("mixer1", _mixer[1])):
    PHASE[_name] = len(DQ)
    for _k, _i in _us:
        _f = FCHUNKS[_i][1] if _k in ("wg", "wu", "wd") else 512
        _qs = [(2 * q * _f, 2 * _f) for q in range(4)] if _k != "wd" else [(q * D, D) for q in range(_f // P)]
        DFIRST[_k, _i] = len(DQ)
        for _q, (_a, _b) in enumerate(_qs):
            DQ.append(((_k, _i), _a, _b))
            _end = _q == len(_qs) - 1
            if _end and _k in ("wg", "wu"):
                DUSED.append(("G" if _k == "wg" else "U", _i, 1))
            elif _end and _k in COLUMNS:
                _c = COLUMNS[_k][1]
                DUSED.append((_c[0], _i) + _c[1:])
            elif _end and _k in MSPLIT:
                DUSED.append((_k, _i, 1))
            elif _end and (_k, _i) == ("wd", len(FCHUNKS) - 1):
                DUSED.append(("Y", 1, 1))
            else:
                _n += 1
                DUSED.append(_n)
    PHASE[_name + " end"] = len(DQ)
PART_BASE, USED_BASE, HI_BASE = len(DQ), _n, G * (DEPTH + 1 + len(FCHUNKS))
DLAST_TURN = DFIRST["wd", 1]

D0 = PHASE["dense"]


def phase_of(j):
    return "mixer0" if j < PHASE["dense"] else "dense" if j < PHASE["mixer1"] else "mixer1"

EC = FF_E // 512
EPRODS = [("hg", 0), ("hg", 1), ("ST",)]
EUNITS = []
for _i in range(EC):
    EPRODS += [("G", _i), ("U", _i)] + ([("T", _i - 1)] if _i else [])
    EUNITS += [("g", _i), ("u", _i)]
TAIL = 2
EPRODS += [("D", 0), ("D", 1), ("T", EC - 1)] + [("SC", g, n) for g in range(G) for n in range(2)]
EUNITS += [("d", _i) for _i in range(EC)]
EPIDX = {n: i for i, n in enumerate(EPRODS)}
EUIDX = {n: i for i, n in enumerate(EUNITS)}
EPER = [len([i for i in range(len(EPRODS)) if i % NB == b]) for b in range(NB)]
EUPER = [len([i for i in range(len(EUNITS)) if i % XRING == s]) for s in range(XRING)]
EQ = 4 * len(EUNITS)
EUSED, USED_PER = [], 0
for _u in EUNITS:
    for _q in range(4):
        if _q == 3 and _u[0] != "d":
            EUSED.append(("G" if _u[0] == "g" else "U", _u[1]))
        elif _q == 3 and _u[1] == EC - 1:
            EUSED.append(("D", 1))
        else:
            USED_PER += 1
            EUSED.append(USED_PER)
HI_PER = 2 + EC
LAST_TURN = 4 * (2 * EC + TAIL) + PARTS


def build(nc, a, outs):
    y_prompt, y_sample, new_k, new_v, new_state = outs
    with ExitStack() as ctx:
        def sb(name, n, parts=P):
            return ctx.enter_context(nc.sbuf_tensor(name, [parts, n], F32))

        def sem(name):
            return ctx.enter_context(nc.semaphore(name))

        ring = sb("ring", RING * W)
        x = sb("x", G * D)
        hT = sb("hT", KD * T)
        cst = sb("cst", len(CONSTS) * P + 2)
        vecs = sb("vecs", 392)
        condT = sb("condT", 48)
        modraw = sb("modraw", 48 * 8)
        modT = sb("modT", DEPTH * 48 * G)
        wgda = sb("wgda", KD * 32)
        gdaT = sb("gdaT", T)
        gup = sb("gup", 512)
        z = sb("z", CC * G * ZW)
        A = sb("A", GLA_H * P)
        stat = sb("stat", 64)
        route = sb("route", 256)
        flag = ctx.enter_context(nc.sbuf_tensor("flag", [P, 1], I32))
        arena = sb("arena", 27136)
        at = [0]

        def carve(n):
            at[0] += n
            assert at[0] <= 27136
            return arena[:, at[0] - n:at[0]]

        gates = carve(6 * T * 4)
        rows = gates[:, 0:4 * P]
        acc = carve(G * CONV)
        qT, kT = carve(512), carve(512)
        v = carve(G * 512)
        r = carve(G * 512)
        glog = carve(G * 512)
        gtmp = carve(G * 512)
        cum = carve(G * 512)
        pg = carve(6656)
        qarg, karg, klarg, ecum = pg[:, 0:512], pg[:, 512:2560], pg[:, 2560:3072], pg[:, 3072:3584]
        qpad, qepad, ke = pg[:, 3584:4608], pg[:, 4608:5632], pg[:, 5632:6656]
        S0, S1 = carve(512), carve(512)
        o = carve(G * 512)
        qbT = carve(NA_H * T)
        kbT = carve(PAIRS * T)
        vb = carve(G * 512)
        kctxT = carve(512)
        mrow = carve(512)
        Pm, PT = pg[:, 0:2048], pg[:, 2048:4096]
        bias, kctx = pg[:, 4096:5120], pg[:, 5120:5632]
        kbtok, vctx = qT, kT
        attT = cum
        diag1 = arena[:, 10240:12288]
        gbc1 = pg[:, 0:2048]
        ln1 = arena[:, 8192:10240]
        mtmp = pg[:, 2048:4096]
        diag2 = arena[:, 16384:18432]
        mrow2 = arena[:, 17408:17920]
        sil_d, act_d = arena[:, 18432:19456], arena[:, 19456:20480]
        ftmp = arena[:, 20480:20992]
        at[0] = 17408
        htok = carve(G * D)
        sil, act = carve(512), carve(1024)
        moe_y = carve(G * D)
        ln2 = carve(2 * D)
        gbc2 = carve(G * D)
        yd, S, S2, S2T = hT[:, 0:1024], hT[:, 1024:1280], hT[:, 1280:1536], hT[:, 1536:1792]
        ring_r = nc.alloc_sbuf_tensor_at("ring_r", [P, W], F32R, offset=nc.lookup_mloc(ring).addr + 4 * 3 * W)
        arena_r = nc.alloc_sbuf_tensor_at("arena_r", [P, 23040], F32R, offset=nc.lookup_mloc(arena).addr)
        hg_hi, hg_lo = arena_r[:, 8192:9216], arena_r[:, 9216:10240]
        eT_hi, eT_lo = arena_r[:, 10240:13824], arena_r[:, 13824:17408]

        h_hi, h_lo = arena_r[:, 4096:6144], arena_r[:, 20992:23040]
        dT_hi, dT_lo = arena_r[:, 6144:6144 + 22 * T], arena_r[:, 6144 + 22 * T:17408]

        hm_lo = arena_r[:, 13312:15360]

        def early_part(j):
            s = (j - PHASE[phase_of(j)]) % DPARTS
            if phase_of(j) == "dense":
                return split_part(s)
            b = (0, 2048, 15360, 17408)[s]
            return arena_r[:, b:b + PART], arena_r[:, b + PART:b + 2 * PART]

        def split_part(j):
            s = j % PARTS
            b = ring_r[:, s * 2 * PART:(s + 1) * 2 * PART] if s < 2 else arena_r[:, (s - 2) * 2 * PART:(s - 1) * 2 * PART]
            return b[:, 0:PART], b[:, PART:2 * PART]

        ps = ctx.enter_context(nc.psum_tensor("ps", [P, NB, 512], F32))

        def C(name):
            i = CONSTS.index(name)
            return cst[:, i * P:(i + 1) * P]

        half = [cst[:, len(CONSTS) * P + i:len(CONSTS) * P + i + 1] for i in range(2)]
        ident = C("ident")

        def slot(s):
            return ring[:, s * W:(s + 1) * W]

        bank_full = [sem(f"bank_full{b}") for b in range(NB)]
        bank_free = [sem(f"bank_free{b}") for b in range(NB)]
        w_loaded = [sem(f"w_loaded{s}") for s in range(RING)]
        part_hi, part_lo, part_used, act_hi = (sem(n) for n in ("part_hi", "part_lo", "part_used", "act_hi"))
        h_split = sem("h_split")
        consts_in, x_in, vecs_in, wgda_in, gup_in = (sem(n) for n in ("consts_in", "x_in", "vecs_in", "wgda_in", "gup_in"))
        state_in, bias_in, ctx_in, vctx_in, ln_in, router_in = (
            sem(n) for n in ("state_in", "bias_in", "ctx_in", "vctx_in", "ln_in", "router_in"))
        zeroed, stored, kv_stored, state_stored = (sem(n) for n in ("zeroed", "stored", "kv_stored", "state_stored"))
        cond_ready, mod_ready, x_ready, glog_part, glog_soft, glog_ready = (
            sem(n) for n in ("cond_ready", "mod_ready", "x_ready", "glog_part", "glog_soft", "glog_ready"))
        args_ready, exps_ready, gla_ready, A_ready, o_ready, gla_var, gla_std = (
            sem(n) for n in ("args_ready", "exps_ready", "gla_ready", "A_ready", "o_ready", "gla_var", "gla_std"))
        conv_summed, P_arg, P_exp, P_ready, m_ready, var_ready, std_ready = (
            sem(n) for n in ("conv_summed", "P_arg", "P_exp", "P_ready", "m_ready", "var_ready", "std_ready"))
        diag_ready, gate_arg, gate_exp, mask_ready, sel_ready, flag_ready, y_ready = (
            sem(n) for n in ("diag_ready", "gate_arg", "gate_exp", "mask_ready", "sel_ready", "flag_ready", "y_ready"))
        dve_step, act_step, pool_step = sem("dve_step"), sem("act_step"), sem("pool_step")

        def bank(name):
            return ps[:, PIDX[name] % NB, :]

        def await_product(eng, *name):
            i = PIDX[name]
            eng.wait_ge(bank_full[i % NB], i // NB + 1)

        def await_copied(eng, *name):
            i = PIDX[name]
            eng.wait_ge(bank_free[i % NB], i // NB + 1)

        def free(ins, *name):
            ins.then_inc(bank_free[PIDX[name] % NB], 1)

        def ebank(name):
            return ps[:, EPIDX[name] % NB, :]

        def e_await_product(eng, E, *name, back=0):
            i = EPIDX[name]
            eng.wait_ge(bank_full[i % NB], E * EPER[i % NB] + (PBASE[i % NB] + i // NB + 1 - back * EPER[i % NB]))

        def e_await_copied(eng, E, *name, back=0):
            i = EPIDX[name]
            eng.wait_ge(bank_free[i % NB], E * EPER[i % NB] + (PBASE[i % NB] + i // NB + 1 - back * EPER[i % NB]))

        def e_free(ins, *name):
            ins.then_inc(bank_free[EPIDX[name] % NB], 1)

        class Steps:

            def __init__(self, eng, own):
                self.eng, self.own, self.seen, self.made = eng, own, Counter(), Counter()

            def next(self, s, by=1):
                self.seen[s.name] += by
                self.eng.wait_ge(s, self.seen[s.name])

            def done(self, ins, s=None):
                s = s or self.own
                ins.then_inc(s, 1)
                self.made[s.name] += 1
                self.eng.wait_ge(s, self.made[s.name])

        def freed(eng, ins, *name):
            free(ins, *name)
            await_copied(eng, *name)

        def modcol(l, c, g):
            return modT[:, (48 * l + c) * G + g:(48 * l + c) * G + g + 1]

        def group_of(buf, g):
            return buf.rearrange("p (k t) -> p k t", k=KD)[:, :, g * P:(g + 1) * P]

        def turned_to(buf, i, g):
            f0, fn = FCHUNKS[i]
            return buf.rearrange("p (f t) -> p f t", t=T)[:, f0 // P:(f0 + fn) // P, g * P:(g + 1) * P]

        def turned_from(i, g):
            return bank(("aT", i, g))[:, 0:FCHUNKS[i][1]].rearrange("p (f t) -> p f t", t=P)

        block = ctx.enter_context(nc.Block())

        def unit_source(name):
            kind = name[0]
            if kind == "mod":
                return a["w_mod"][name[1], :, 512 * name[2]:512 * name[2] + 512].rearrange("(c p) n -> p c n", p=P)
            if kind in SPLIT:
                return a["w_in"][name[1], :, SPLIT[kind]:SPLIT[kind] + 512].rearrange("(c p) n -> p c n", p=P)
            if kind == "br":
                w = a[("w_br_gla", "w_br_na", "w_br_cv")[name[2]]]
                return w[name[1]].rearrange("(c p) n -> p c n", p=P)
            if kind == "out":
                return a["w_out"][name[1], :, 512 * name[2]:512 * name[2] + 512].rearrange("(c p) n -> p c n", p=P)
            f0, fn = FCHUNKS[name[1]]
            if kind == "wd":
                return a["ffd_w_down"][0, f0:f0 + fn, :].rearrange("(c p) n -> p c n", p=P)
            w = a["ffd_w_gate" if kind == "wg" else "ffd_w_up"]
            return w[0, :, f0:f0 + fn].rearrange("(c p) n -> p c n", p=P)

        def unit_shape(name):
            src = unit_source(name)
            return src.shape[1], src.shape[2]

        def unit(name):
            c, n = unit_shape(name)
            return slot(SLOT[UIDX[name]])[:, 0:c * n].rearrange("p (c n) -> p c n", c=c)

        def raw_part(j):
            return slot((j // 4) % XRING)[:, (j % 4) * PART:(j % 4 + 1) * PART]

        def await_part_free(eng, E, j):
            if j < PARTS:
                e_await_product(eng, E, "D", 1, back=1)
            elif isinstance(EUSED[j - PARTS], tuple):
                e_await_product(eng, E, *EUSED[j - PARTS])
            else:
                eng.wait_ge(part_used, E * USED_PER + (USED_BASE + EUSED[j - PARTS]))

        def e_source(name, e):
            f = slice(512 * name[1], 512 * name[1] + 512)
            if name[0] == "d":
                return a["moe_w_down"][0, e, f, :].rearrange("(c p) n -> p c n", p=P)
            return a["moe_w_gate" if name[0] == "g" else "moe_w_up"][0, e, :, f].rearrange("(c p) n -> p c n", p=P)

        @block.sync
        def _(sp):
            for i, name in enumerate(UNITS):
                if i == 1:
                    sp.wait_ge(vecs_in, 16 * 14)
                before = BEFORE[i]
                if before in DFIRST:
                    sp.wait_ge(part_lo, max(j for j in range(len(DQ)) if DQ[j][0] == before) + 1)
                elif before:
                    await_product(sp, *LAST[before])
                if name[0] not in ("mod", "wg", "wu", "wd") and name[-1] == 1 and SLOT[i] == RING - 1:
                    await_product(sp, "Y", 1, 1)
                sp.dma_start(unit(name), unit_source(name)).then_inc(w_loaded[SLOT[i]], 16)

            def experts(passes):
                with sp.Fori(0, EXPERTS) as e:
                    for i, name in enumerate(EUNITS):
                        sp.wait_ge(part_lo, (e + EXPERTS * passes) * EQ + (PART_BASE + 4 * (i - XRING + 1)))
                        dst = slot(i % XRING).rearrange("p (c n) -> p c n", c=4 if name[0] == "d" else 8)
                        sp.dma_start(dst, e_source(name, e)).then_inc(w_loaded[i % XRING], 16)

            await_product(sp, "h2T", DEPTH - 1, 1, 1)
            sp.wait_ge(kv_stored, 32 * DEPTH)
            experts(0)
            sp.wait_ge(flag_ready, 1)
            over = sp.value_load(flag[0:1, 0:1], min_val=0, max_val=T)
            with sp.If(over > P):
                experts(1)

        @block.gpsimd
        def _(pool):
            pool.memset(condT[:, :], 0.0).then_inc(zeroed, 1)
            pool.memset(gup[:, :], 0.0).then_inc(pool_step, 1)
            pool.memset(gdaT[:, :], 0.0).then_inc(pool_step, 1)
            pool.memset(z[:, :], 0.0).then_inc(zeroed, 1)
            pool.memset(A[:, :], 0.0).then_inc(zeroed, 1)
            pool.wait_ge(zeroed, 3)
            pool.wait_ge(pool_step, 2)
            pool.memset(gdaT[32:33, :], 1.0).then_inc(zeroed, 1)

            def last_layer_done_with(l, *name):
                if l:
                    await_product(pool, name[0], l - 1, *name[1:])

            def load_mixer(l):
                last_layer_done_with(l, "gda")
                pool.dma_start(wgda[:, :].rearrange("p (c n) -> p c n", c=KD),
                               a["w_in"][l, :, 1536:1568].rearrange("(c p) n -> p c n", p=P)).then_inc(wgda_in, 16)
                last_layer_done_with(l, "glog", 1)
                for n in range(2):
                    pool.dma_start(gup[RANK * n:RANK * n + RANK, 256 * n:256 * n + 256],
                                   a["gla_w_gup"][l, n]).then_inc(gup_in, 16)
                pool.dma_start(gup[32:33, :], a["gla_b_g"][l:l + 1].rearrange("o n k -> o (n k)")).then_inc(gup_in, 16)

            def load_state(l):
                if l:
                    pool.wait_ge(x_ready, 2 * G * l)
                for n in range(2):
                    pool.dma_start(S0[:, 256 * n:256 * n + 256].rearrange("p (h v) -> p h v", h=HP),
                                   a["state_gla"][0, l, n].rearrange("(h a) k v -> (a k) h v", a=2))\
                        .then_inc(state_in, 16)

            def na_loads(l):
                await_product(pool, "o", l, 1)
                pool.dma_start(kctx, a["cache_na_k"][0, l].rearrange("t h d -> t (h d)")).then_inc(ctx_in, 16)
                pool.dma_start(vctx, a["cache_na_v"][0, l].rearrange("t h d -> t (h d)")).then_inc(vctx_in, 16)
                w = a["na_rpb"][l]
                for rq in range(2):
                    for rk in range(2):
                        start = l * NA_H * 15 * 31 + (rk - rq + WIN_R - 1) * 31 + WIN_C - GRID_W
                        toeplitz = bass.AP(w.tensor, start, [[1, GRID_W], [15 * 31, NA_H], [1, GRID_W]])
                        pool.dma_start(bias[64 * rq:64 * rq + 64, :].rearrange("p (h k) -> p h k", h=NA_H)[
                            :, :, 64 * rk:64 * rk + 64], toeplitz).then_inc(bias_in, 16)

            def load_ln(dst, l, j):
                for i, name in enumerate(("ln_g", "ln_b")):
                    w = a[name][l, j]
                    pool.dma_start(dst[:, i * D:(i + 1) * D],
                                   bass.AP(w.tensor, (l * 2 + j) * D, [[0, P], [1, D]])).then_inc(ln_in, 16)

            def load_router():
                await_product(pool, "gda", DEPTH - 1)
                pool.dma_start(wgda[:, 0:KD * EXPERTS].rearrange("p (c n) -> p c n", c=KD),
                               a["moe_w_router"][0].rearrange("(c p) n -> p c n", p=P)).then_inc(router_in, 16)

            for l in range(DEPTH):
                load_mixer(l)
                load_state(l)
                await_copied(pool, "vb", l, 0)
                pool.dma_start(new_v[0, l].rearrange("t h d -> t (h d)"), vb[:, 0:512]).then_inc(kv_stored, 16)
                await_copied(pool, "kv", l, 0, 0)
                await_copied(pool, "kv", l, 0, 1)
                for n in range(2):
                    pool.dma_start(new_state[0, l, n].rearrange("(h a) k v -> (a k) h v", a=2),
                                   qarg[:, 256 * n:256 * n + 256].rearrange("p (h v) -> p h v", h=HP))\
                        .then_inc(state_stored, 16)
                na_loads(l)
                await_product(pool, "oT", l, 1)
                load_ln(ln1, l, 0)
                await_copied(pool, "kbtok", l)
                pool.dma_start(new_k[0, l].rearrange("t h d -> t (h d)"), kbtok).then_inc(kv_stored, 16)
                if l == DEPTH - 1:
                    load_router()
                await_product(pool, "h2T", l, 1, 1)
                pool.wait_ge(kv_stored, 32 * (l + 1))
                load_ln(ln2, l, 1)
            for g, out in enumerate((y_prompt, y_sample)):
                pool.wait_ge(y_ready, g + 1)
                pool.dma_start(out[0], x[:, g * D:(g + 1) * D]).then_inc(stored, 16)
            pool.wait_ge(stored, 32)
            pool.wait_ge(state_stored, 32 * DEPTH)
            pool.wait_ge(kv_stored, 32 * DEPTH)

        @block.tensor
        def _(pe):
            st = Steps(pe, None)

            def claim(*name):
                i = PIDX[name]
                if i >= NB:
                    pe.wait_ge(bank_free[i % NB], i // NB)
                return bank(name)

            def full(ins, *name):
                ins.then_inc(bank_full[PIDX[name] % NB], 1)

            def arrived(name):
                i = UIDX[name]
                pe.wait_ge(w_loaded[SLOT[i]], 16 * NTH[i])
                return unit(name)

            mm = nc.tensor.matmul
            tr = nc.tensor.transpose

            def tokens_times(name, lhs, w, n=512, ks=KD, n0=0):
                o_ = claim(*name)
                for k in range(ks):
                    ins = mm(o_[:, 0:n], lhs(k), w[:, k, n0:n0 + n], start=(k == 0), stop=(k == ks - 1))
                full(ins, *name)

            def hTk(g):
                return lambda k: hT[:, k * T + g * P:k * T + g * P + P]

            def features(kind, l):
                names = [(c[0], l) + c[1:] for c in COLUMNS[kind]]
                outs_ = [claim(*n) for n in names]
                for q in range(4):
                    j = DFIRST[kind, l] + q
                    pe.wait_ge(part_lo, j + 1)
                    w_hi, w_lo = early_part(j)
                    for k in (2 * q, 2 * q + 1):
                        ks = slice(k * T, (k + 1) * T)
                        for c in range(4):
                            ws = slice((k % 2) * 512 + c * P, (k % 2) * 512 + (c + 1) * P)
                            o_ = outs_[c // 2][:, (c % 2) * T:(c % 2 + 1) * T]
                            mm(o_, w_hi[:, ws], h_hi[:, ks], start=(k == 0 and c % 2 == 0), stop=False,
                               skip_group_check=True)
                            mm(o_, w_hi[:, ws], hm_lo[:, ks], start=False, stop=False, skip_group_check=True)
                            ins = mm(o_, w_lo[:, ws], h_hi[:, ks], start=False, stop=(k == KD - 1), skip_group_check=True)
                            if k == KD - 1 and c % 2:
                                full(ins, *names[c // 2])
                    if q < 3:
                        ins.then_inc(part_used, 1)

            def turned(name, sources, rows_=P):
                o_ = claim(*name)
                for j, s in enumerate(sources):
                    ins = tr(o_[:, j * P:j * P + rows_], s, ident[0:rows_, 0:rows_])
                full(ins, *name)

            def copied(*name):
                await_copied(pe, *name)

            pe.wait_ge(consts_in, 16)
            pe.wait_ge(vecs_in, 16 * 14)
            o_ = claim("vecs")
            tr(o_[:, 0:128], rows[:, 0:P], ident)
            tr(o_[:, 128:144], rows[0:16, P:2 * P], ident[0:16, 0:16])
            tr(o_[:, 144:268], rows[0:124, 2 * P:3 * P], ident[0:124, 0:124])
            full(tr(o_[:, 268:392], rows[0:124, 3 * P:4 * P], ident[0:124, 0:124]), "vecs")

            def mod_unit(l, i, buf):
                w = arrived(("mod", l, i))
                pe.wait_ge(cond_ready, 1)
                o_ = claim("mod", l, i)
                for k in range(KD):
                    j = k % 4
                    ins = mm(o_[32 * j:32 * j + 32, :], condT[:, G * k:G * k + 32], w[:, k, :],
                             start=(k < 4), stop=(k >= 4))
                full(ins, "mod", l, i)
                copied("mod", l, i)
                turned(("modT", l, i), [buf[:, j * P:(j + 1) * P] for j in range(4)])

            def split_mm(pairs, hi, lo, w_hi, w_lo, start, stop):
                for o_, n in pairs:
                    mm(o_, hi, w_hi[:, n], start=start, stop=False)
                    mm(o_, hi, w_lo[:, n], start=False, stop=False)
                return [mm(o_, lo, w_hi[:, n], start=False, stop=stop) for o_, n in pairs]

            def columns(kind, i, names, fn, rest):
                outs_ = {g: claim(*n) for g, n in names.items()}
                for q in range(4):
                    j = DFIRST[kind, i] + q
                    pe.wait_ge(part_lo, j + 1)
                    w_hi, w_lo = early_part(j)
                    for c in range(2):
                        k = 2 * q + c
                        for g in names:
                            ks = slice(k * T + g * P, k * T + (g + 1) * P)
                            ins = split_mm([(outs_[g][:, 0:fn], slice(c * fn, (c + 1) * fn))], h_hi[:, ks], rest[:, ks],
                                           w_hi, w_lo, k == 0, k == KD - 1)[0]
                            if k == KD - 1:
                                full(ins, *names[g])
                    if q < 3 and 1 in names:
                        ins.then_inc(part_used, 1)

            for i in EARLY:
                mod_unit(0, i, mrow)
            for l in range(DEPTH):
                def token_unit(kind, groups):
                    columns(kind, l, {g: (kind, l, g) for g in groups}, 512, hm_lo)

                if l:
                    mod_unit(l, 4, mrow2)
                for g in range(G):
                    if l == 0:
                        pe.wait_ge(x_in, 32)
                    else:
                        pe.wait_ge(x_ready, 2 * G * l - G + g + 1)
                    for h in range(2):
                        turned(("hT", l, g, h), [x[:, g * D + (4 * h + j) * P:g * D + (4 * h + j + 1) * P] for j in range(4)])
                    if l and g == 0:
                        mod_unit(l, 5, mrow2)
                    copied("hT", l, g, 0), copied("hT", l, g, 1)
                    pe.wait_ge(h_split, 2 * G * l + g + 1)
                    token_unit("v", [g])
                token_unit("vb", range(G)), token_unit("r", range(G))
                features("cva", l), features("cvg", l)
                if l == 0:
                    mod_unit(l, 4, mrow)
                pe.wait_ge(wgda_in, 16 * (l + 1))
                o_ = claim("gda", l)
                for k in range(KD):
                    ins = mm(o_[0:32, 0:T], wgda[:, k * 32:(k + 1) * 32], hT[:, k * T:(k + 1) * T],
                             start=(k == 0), stop=(k == KD - 1))
                full(ins, "gda", l)
                features("qk", l)
                if l == 0:
                    mod_unit(l, 5, mrow)
                copied("gda", l)
                pe.wait_ge(zeroed, 4)
                pe.wait_ge(gup_in, 48 * (l + 1))
                for g in range(G):
                    o_ = claim("glog", l, g)
                    full(mm(o_, gdaT[:, g * P:(g + 1) * P], gup[:, :], start=True, stop=True), "glog", l, g)
                features("kb", l)
                o_ = claim("rope", l)
                copied("q", l), copied("k", l)
                for j in range(4):
                    s = (qT, kT)[j // 2][:, (j % 2) * T + P:(j % 2) * T + T]
                    ins = mm(o_[:, j * P:(j + 1) * P], C("rot"), s, start=True, stop=True)
                full(ins, "rope", l)
                mod_unit(l, 6, mrow)
                for g in range(G):
                    o_ = claim("cum", l, g)
                    pe.wait_ge(glog_ready, G * l + g + 1)
                    for dr in range(2):
                        for hp in range(HP):
                            j = dr * HP + hp
                            ins = mm(o_[:, j * P:(j + 1) * P], glog[:, g * 512 + j * P:g * 512 + (j + 1) * P],
                                     C("mask_f" if dr == 0 else "mask_b"), start=True, stop=True)
                    full(ins, "cum", l, g)
                features("qb", l)
                mod_unit(l, 7, mrow)

                def gla_scores(g):
                    pe.wait_ge(gla_ready, G * l + g + 1)
                    turned(("keT", l, g), [klarg[:, j * P:(j + 1) * P] for j in range(4)])
                    k5 = karg.rearrange("p (n h b s) -> p n h b s", n=2, h=HP, b=8)
                    q5 = qpad.rearrange("p (n h a t) -> p n h a t", n=2, h=HP, a=2)
                    for dr in range(2):
                        o4 = claim("att", l, g, dr).rearrange("s (h a t) -> s h a t", h=HP, a=2)
                        for hp in range(HP):
                            for b in range(8):
                                c = b // 4
                                ins = mm(o4[64 * c:64 * c + 64, hp, :, b * SUB:(b + 1) * SUB], k5[:, dr, hp, b, :],
                                         q5[:, dr, hp, :, b * SUB:(b + 1) * SUB], start=True, stop=True)
                        full(ins, "att", l, g, dr)

                def gla_states(g):
                    copied("keT", l, g)
                    copied("v", l, g)
                    for dr in range(2):
                        o_ = claim("kv", l, g, dr)
                        for c in range(2):
                            for hp in range(HP):
                                for s in range(2):
                                    j = c * HP + hp
                                    k0 = c * 512 + (dr * HP + hp) * P + 64 * s
                                    ins = mm(o_[64 * s:64 * s + 64, j * P:(j + 1) * P], ke[:, k0:k0 + 64],
                                             v[:, g * 512 + (2 * hp + s) * P:g * 512 + (2 * hp + s + 1) * P],
                                             start=True, stop=True)
                        full(ins, "kv", l, g, dr)

                def gla_out(g):
                    pe.wait_ge(A_ready, G * l + g + 1)
                    copied("kv", l, g, 0), copied("kv", l, g, 1)
                    o_ = claim("o", l, g)
                    qe = qepad.rearrange("p (n h a t) -> p n h a t", n=2, h=HP, a=2)
                    for h in range(GLA_H):
                        hp, s = h // 2, h % 2
                        terms = [(0, 1, S1), (1, 0, S1)] + ([(0, 0, S0), (1, 1, S0)] if g == 1 else [])
                        mm(o_[:, h * P:(h + 1) * P], A[:, h * P:(h + 1) * P],
                           v[:, g * 512 + h * P:g * 512 + (h + 1) * P], start=True, stop=False, skip_group_check=True)
                        for n, (dr, c, state) in enumerate(terms):
                            ins = mm(o_[64 * c:64 * c + 64, h * P:(h + 1) * P], qe[:, dr, hp, s, 64 * c:64 * c + 64],
                                     state[:, (dr * HP + hp) * P:(dr * HP + hp + 1) * P],
                                     start=False, stop=(n == len(terms) - 1), skip_group_check=True)
                    full(ins, "o", l, g)

                def gla_turn(g):
                    pe.wait_ge(o_ready, G * l + g + 1)
                    turned(("oT", l, g), [o[:, g * 512 + j * P:g * 512 + (j + 1) * P] for j in range(4)])

                def mgate(n):
                    w = arrived((MG[n], l))
                    tokens_times(("mg", l, 0, n), hTk(0), w), tokens_times(("mg", l, 1, n), hTk(1), w)

                mgate(0)
                mod_unit(l, 8, mrow)
                gla_scores(0)
                mgate(1)
                mod_unit(l, 9, mrow)
                gla_states(0)
                mgate(2)
                gla_out(0)
                mgate(3)
                gla_turn(0)
                mgate(4)
                gla_scores(1)
                mgate(5)
                gla_states(1)
                gla_out(1)
                gla_turn(1)
                turned(("kbtok", l), [kbT[:, j * T:j * T + P] for j in range(4)])
                pe.wait_ge(ctx_in, 16 * (l + 1))
                turned(("kctxT", l), [kctx[:, j * P:(j + 1) * P] for j in range(4)])
                pe.wait_ge(bias_in, 64 * (l + 1))
                for i in range(2):
                    full(mm(claim("bias", l, i), C("flip"), bias[:, i * 512:(i + 1) * 512], start=True, stop=True),
                         "bias", l, i)
                for i in range(2):
                    o_ = claim("sc", l, 0, i)
                    for j in range(4):
                        h = 4 * i + j
                        ins = mm(o_[:, j * P:(j + 1) * P], qbT[:, h * T:h * T + P],
                                 kbT[:, (h // 2) * T:(h // 2) * T + P], start=True, stop=True)
                    full(ins, "sc", l, 0, i)
                for g in range(G):
                    pe.wait_ge(conv_summed, l + 1)
                    turned(("cvtok", l, g), [acc[:, g * 512 + j * P:g * 512 + (j + 1) * P] for j in range(4)])
                for g in range(G):
                    copied("cvtok", l, g)
                    turned(("cvT", l, g), [acc[:, g * 512 + j * P:g * 512 + (j + 1) * P] for j in range(4)])
                pe.wait_ge(P_ready, G * l + 1)
                for i in range(2):
                    turned(("PT", l, 0, i), [Pm[:, (4 * i + j) * P:(4 * i + j + 1) * P] for j in range(4)])
                copied("kctxT", l)
                for i in range(4):
                    o_ = claim("sc", l, 1, i)
                    for j in range(2):
                        h = 2 * i + j
                        q = qbT[:, h * T + P:h * T + T]
                        mm(o_[:, j * T:j * T + P], q, kbT[:, (h // 2) * T + P:(h // 2) * T + T], start=True, stop=True)
                        ins = mm(o_[:, j * T + P:(j + 1) * T], q, kctxT[:, (h // 2) * P:(h // 2 + 1) * P],
                                 start=True, stop=True)
                    full(ins, "sc", l, 1, i)

                def branch(b, src):
                    w = arrived(("br", l, b))
                    for g in range(G):
                        for n in range(2):
                            tokens_times(("y", l, b, g, n), (lambda k, g=g: src(g, k)), w, ks=4, n0=512 * n)

                copied("oT", l, 0), copied("oT", l, 1)
                branch(0, lambda g, k: o[:, g * 512 + k * P:g * 512 + (k + 1) * P])
                copied("cvT", l, 0), copied("cvT", l, 1)
                branch(2, lambda g, k: acc[:, g * 512 + k * P:g * 512 + (k + 1) * P])

                def na_values(g):
                    o_ = claim("attT", l, g)
                    if g:
                        pe.wait_ge(vctx_in, 16 * (l + 1))
                    kinds = 1 + g
                    for i in range(4 if g else 2):
                        copied("PT", l, g, i)
                    for h in range(NA_H):
                        for n in range(kinds):
                            val = (vb[:, g * 512:(g + 1) * 512] if n == 0 else vctx)[:, h * NA_DH:(h + 1) * NA_DH]
                            ins = mm(o_[64 * (h % 2):64 * (h % 2) + 64, (h // 2) * P:(h // 2 + 1) * P], val,
                                     PT[:, (h * kinds + n) * P:(h * kinds + n + 1) * P],
                                     start=(n == 0), stop=(n == kinds - 1))
                    full(ins, "attT", l, g)

                na_values(0)
                pe.wait_ge(P_ready, G * l + 2)
                for i in range(4):
                    turned(("PT", l, 1, i), [Pm[:, (4 * i + j) * P:(4 * i + j + 1) * P] for j in range(4)])
                na_values(1)
                copied("attT", l, 0), copied("attT", l, 1)
                branch(1, lambda g, k: attT[:, g * 512 + k * P:g * 512 + (k + 1) * P])

                def gate_rows(j, d):
                    pe.wait_ge(diag_ready, 2 * l + j + 1)
                    for g in range(G):
                        for n in range(2):
                            o_ = claim("gbc", l, j, g, n)
                            full(mm(o_, C("ones"), d[:, g * D + 512 * n:g * D + 512 * n + 512],
                                    start=True, stop=True), "gbc", l, j, g, n)

                gate_rows(0, diag1)
                mod_unit(l, 10, mrow)
                for g in range(G):
                    pe.wait_ge(m_ready, G * l + g + 1)
                    for h in range(2):
                        turned(("mT", l, g, h), [gates[:, g * 3 * D + (4 * h + j) * P:g * 3 * D + (4 * h + j + 1) * P]
                                                 for j in range(4)])
                for g in range(G):
                    copied("mT", l, g, 0), copied("mT", l, g, 1)
                for g in range(G):
                    for n in range(2):
                        tokens_times(("mix", l, g, n), hTk(g), arrived(("out", l, n)))
                mod_unit(l, 11, mrow)

                def dense_columns(kind, pn, i, groups):
                    columns(kind, i, {g: (pn, i, g) for g in groups}, FCHUNKS[i][1], h_lo)

                for g in range(G):
                    pe.wait_ge(x_ready, 2 * G * l + g + 1)
                    for h in range(2):
                        turned(("h2T", l, g, h), [x[:, g * D + (4 * h + j) * P:g * D + (4 * h + j + 1) * P] for j in range(4)])
                    copied("h2T", l, g, 0), copied("h2T", l, g, 1)
                    if l == 0:
                        pe.wait_ge(h_split, G + g + 1)
                        dense_columns("wg", "G", 0, [g])
                if l == 0:
                    dense_columns("wu", "U", 0, range(G))
                gate_rows(1, diag2)

                if l == 0:
                    def dense_turn(i):
                        for g in range(G):
                            copied("U", i, g)
                            b = act_d[:, g * 512:(g + 1) * 512]
                            turned(("aT", i, g), [b[:, j * P:(j + 1) * P] for j in range(FCHUNKS[i][1] // P)])

                    for i in range(len(FCHUNKS)):
                        if i:
                            dense_columns("wg", "G", i, range(G))
                            dense_columns("wu", "U", i, range(G))
                            dense_turn(i - 1)
                        if i in EARLY:
                            mod_unit(1, i, mrow2)
                    ys = {(g, n): claim("Y", g, n) for g in range(G) for n in range(2)}
                    for i, (f0, fn) in enumerate(FCHUNKS):
                        if DFIRST["wd", i] == DLAST_TURN:
                            dense_turn(len(FCHUNKS) - 1)
                        for g in range(G):
                            copied("aT", i, g)
                        for c in range(fn // P):
                            f, j = f0 // P + c, DFIRST["wd", i] + c
                            pe.wait_ge(part_lo, j + 1)
                            end = f == FF_D // P - 1
                            for g in range(G):
                                fs = slice(f * T + g * P, f * T + (g + 1) * P)
                                inss = split_mm([(ys[g, n], slice(512 * n, 512 * n + 512)) for n in range(2)],
                                                dT_hi[:, fs], dT_lo[:, fs], *early_part(j), f == 0, end)
                                if end:
                                    full(inss[0], "Y", g, 0), full(inss[1], "Y", g, 1)
                            if not end:
                                inss[1].then_inc(part_used, 1)
                else:
                    for g in range(G):
                        for h in range(2):
                            turned(("htok", g, h), [hTk(g)(4 * h + j) for j in range(4)])
                    pe.wait_ge(router_in, 16)
                    o_ = claim("logits")
                    for g in range(G):
                        for k in range(KD):
                            ins = mm(o_[:, 8 * g:8 * g + 8], hTk(g)(k), wgda[:, 8 * k:8 * k + 8],
                                     start=(k == 0), stop=(k == KD - 1))
                    full(ins, "logits")
                    o_ = claim("rank")
                    pe.wait_ge(mask_ready, 1)
                    m0, m1 = route[:, 64:72], route[:, 72:80]
                    mm(o_[:, 0:8], C("before"), m0, start=True, stop=True)
                    mm(o_[:, 8:16], C("before"), m1, start=True, stop=False)
                    mm(o_[:, 8:16], C("ones"), m0, start=False, stop=True)
                    mm(o_[:, 16:24], C("ones"), m0, start=True, stop=False)
                    full(mm(o_[:, 16:24], C("ones"), m1, start=False, stop=True), "rank")

            def e_claim(E, *name):
                i = EPIDX[name]
                pe.wait_ge(bank_free[i % NB], E * EPER[i % NB] + (PBASE[i % NB] + i // NB))
                return ebank(name)

            def e_full(ins, *name):
                ins.then_inc(bank_full[EPIDX[name] % NB], 1)

            def experts(passes):
                with pe.Fori(0, EXPERTS) as e:
                    E = e + EXPERTS * passes
                    pe.wait_ge(sel_ready, E + 1)
                    for h in range(2):
                        o_ = e_claim(E, "hg", h)
                        for j in range(4):
                            for g in range(G):
                                ins = mm(o_[:, j * P:(j + 1) * P], htok[:, g * D + (4 * h + j) * P:g * D + (4 * h + j + 1) * P],
                                         S[:, g * P:(g + 1) * P], start=(g == 0), stop=(g == 1))
                        e_full(ins, "hg", h)
                    o_ = e_claim(E, "ST")
                    for g in range(G):
                        ins = tr(o_[:, g * P:(g + 1) * P], S2[:, g * P:(g + 1) * P], ident)
                    e_full(ins, "ST")
                    e_await_copied(pe, E, "hg", 0)
                    e_await_copied(pe, E, "hg", 1)

                    def turn(i):
                        o_ = e_claim(E, "T", i)
                        e_await_copied(pe, E, "U", i)
                        for j in range(4):
                            ins = tr(o_[:, j * P:(j + 1) * P], act[:, (i % 2) * 512 + j * P:(i % 2) * 512 + (j + 1) * P], ident)
                        e_full(ins, "T", i)

                    for i in range(EC):
                        for kind, pn in (("g", "G"), ("u", "U")):
                            o_ = e_claim(E, pn, i)
                            for q in range(4):
                                j = 4 * EUIDX[kind, i] + q
                                pe.wait_ge(part_lo, E * EQ + (PART_BASE + j + 1))
                                w_hi, w_lo = split_part(j)
                                for c in range(2):
                                    k = 2 * q + c
                                    ks = slice(k * P, (k + 1) * P)
                                    ins = split_mm([(o_, slice(512 * c, 512 * c + 512))], hg_hi[:, ks], hg_lo[:, ks],
                                                   w_hi, w_lo, k == 0, k == KD - 1)[0]
                                if q < 3:
                                    ins.then_inc(part_used, 1)
                            e_full(ins, pn, i)
                        if i:
                            turn(i - 1)
                    ds = [(e_claim(E, "D", 0), slice(0, 512)), (e_claim(E, "D", 1), slice(512, 1024))]
                    for i in range(EC):
                        if i == TAIL:
                            turn(EC - 1)
                        e_await_copied(pe, E, "T", i)
                        for q in range(4):
                            j = 4 * EUIDX["d", i] + q
                            pe.wait_ge(part_lo, E * EQ + (PART_BASE + j + 1))
                            f = 4 * i + q
                            fs = slice(f * P, (f + 1) * P)
                            inss = split_mm(ds, eT_hi[:, fs], eT_lo[:, fs], *split_part(j), f == 0, f == 4 * EC - 1)
                            if f < 4 * EC - 1:
                                inss[1].then_inc(part_used, 1)
                    for n in range(2):
                        e_full(inss[n], "D", n)
                    e_await_copied(pe, E, "ST")
                    e_await_copied(pe, E, "D", 0)
                    e_await_copied(pe, E, "D", 1)
                    for g in range(G):
                        for n in range(2):
                            o_ = e_claim(E, "SC", g, n)
                            e_full(mm(o_, S2T[:, g * P:(g + 1) * P], yd[:, 512 * n:512 * n + 512],
                                      start=True, stop=True), "SC", g, n)

            for h in range(2):
                for g in range(G):
                    copied("htok", g, h)
            experts(0)
            pe.wait_ge(flag_ready, 1)
            over = pe.value_load(flag[0:1, 0:1], min_val=0, max_val=T)
            with pe.If(over > P):
                experts(1)

        @block.scalar
        def _(sc):
            st = Steps(sc, act_step)
            act_ = nc.scalar.activation

            def take(out, name, func=ACT.Copy, src=None, **kw):
                await_product(sc, *name)
                free(act_(out, bank(name) if src is None else src, func, **kw), *name)

            sc.dma_start(cst[:, :], a["const_tables"]).then_inc(consts_in, 16)
            cr = rows[:, P:2 * P]
            sc.dma_start(cr[0:KD, :], a["c_ctx"].rearrange("(c p) -> c p", p=P)).then_inc(vecs_in, 16)
            sc.dma_start(cr[KD:2 * KD, :], a["c"].rearrange("b (c p) -> (b c) p", p=P)).then_inc(vecs_in, 16)
            for l in range(DEPTH):
                b = 64 * l
                for name, n in (("b_mod", 48), ("cv_b", 4), ("cv_ln_g", 4), ("cv_ln_b", 4)):
                    sc.dma_start(rows[b:b + n, 0:P], a[name][l].rearrange("(c p) -> c p", p=P)).then_inc(vecs_in, 16)
                    b += n
                sc.dma_start(rows[b:b + 4, 0:P], a["gla_norm"][l]).then_inc(vecs_in, 16)
                sc.dma_start(rows[0:TAPS * CC, (2 + l) * P:(3 + l) * P],
                               a["cv_w"][l].rearrange("t (c p) -> (t c) p", p=P)).then_inc(vecs_in, 16)
            sc.dma_start(x[:, 0:D], a["x_prompt"][0]).then_inc(x_in, 16)
            sc.dma_start(x[:, D:2 * D], a["x_sample"][0]).then_inc(x_in, 16)
            sc.wait_ge(zeroed, 4)
            await_copied(sc, "vecs")
            act_(condT[:, 0:16].rearrange("p (k g) -> p g k", g=G), vecs[:, 128:144].rearrange("p (g k) -> p g k", g=G),
                 ACT.Silu).then_inc(cond_ready, 1)

            def mod_rows(l, i, buf):
                take(buf, ("mod", l, i))
                take(modraw[:, 32 * i:32 * i + 32].rearrange("p (c j g) -> p c j g", c=4, j=4), ("modT", l, i),
                     src=bank(("modT", l, i)).rearrange("p (c j r) -> p c j r", c=4, j=4)[:, :, :, 0:G])

            def early_hi(j):
                name, first_, n = DQ[j]
                if j == DFIRST[name]:
                    sc.wait_ge(w_loaded[SLOT[UIDX[name]]], 16 * NTH[UIDX[name]])
                if j - PHASE[phase_of(j)] < DPARTS:
                    if j == PHASE["dense"]:
                        await_product(sc, *LAST[[u_ for i_, u_ in enumerate(UNITS[:UIDX["wg", 0]])
                                                 if SLOT[i_] == RING - 1][-1]])
                elif isinstance(DUSED[j - DPARTS], tuple):
                    await_product(sc, *DUSED[j - DPARTS])
                else:
                    sc.wait_ge(part_used, DUSED[j - DPARTS])
                act_(early_part(j)[0][:, 0:n], slot(SLOT[UIDX[name]])[:, first_:first_ + n],
                     ACT.Copy).then_inc(part_hi, 1)

            def high_h(kind, l, g):
                await_copied(sc, kind, l, g, 0)
                await_copied(sc, kind, l, g, 1)
                act_(group_of(h_hi, g), group_of(hT[:, :], g), ACT.Copy).then_inc(act_hi, 1)

            for i in EARLY:
                mod_rows(0, i, mrow)

            for l in range(DEPTH):
                def modulated(kind, sh, scl, g):
                    await_product(sc, kind, l, g, 1)
                    for j in range(4):
                        k = 4 + j
                        ins = act_(hT[:, k * T + g * P:k * T + (g + 1) * P], bank((kind, l, g, 1))[:, j * P:(j + 1) * P],
                                   ACT.Identity, bias=modcol(l, sh + k, g), scale=modcol(l, scl + k, g))
                    free(ins, kind, l, g, 1)

                def norm_sqrt(n):
                    for _ in range(n):
                        st.next(var_ready)
                        act_(stat[:, 40:41], stat[:, 39:40], ACT.Sqrt).then_inc(std_ready, 1)

                sc.wait_ge(mod_ready, 2 * l + 1)
                def hi_unit(kind):
                    for j in range(4):
                        early_hi(DFIRST[kind, l] + j)

                for g in range(G):
                    modulated("hT", 0, 8, g)
                    high_h("hT", l, g)
                    if g == 0:
                        hi_unit("v")
                hi_unit("vb")
                for g in range(G):
                    take(v[:, g * 512:(g + 1) * 512], ("v", l, g))
                hi_unit("r")
                for g in range(G):
                    take(vb[:, g * 512:(g + 1) * 512], ("vb", l, g))
                hi_unit("cva")
                for g in range(G):
                    take(r[:, g * 512:(g + 1) * 512], ("r", l, g), ACT.Silu)
                hi_unit("cvg")
                hi_unit("qk")
                for i in range(2):
                    take(gtmp[:, i * 512:(i + 1) * 512], ("cvg", l, i), ACT.Sigmoid)
                if l == 0:
                    mod_rows(l, 4, mrow)
                hi_unit("kb")
                take(kT, ("k", l))
                if l == 0:
                    mod_rows(l, 5, mrow)
                for g in range(G):
                    s = gtmp[:, g * 512:(g + 1) * 512]
                    st.next(glog_part)
                    st.done(act_(s, s, ACT.Exp))
                    act_(s, s, ACT.Ln, bias=1.0).then_inc(glog_soft, 1)
                hi_unit("qb")
                for i in range(2):
                    take(kbT[:, i * 512:(i + 1) * 512], ("kb", l, i))
                mod_rows(l, 6, mrow)
                for i in range(2):
                    await_product(sc, "qb", l, i)
                    for j in range(2):
                        for s in range(2):
                            h = 2 * (2 * i + j) + s
                            ins = act_(qbT[:, h * T:(h + 1) * T], bank(("qb", l, i))[:, j * T:(j + 1) * T], ACT.Copy,
                                       scale=half[s])
                    free(ins, "qb", l, i)
                mod_rows(l, 7, mrow)

                def gla_exps(g):
                    st.next(args_ready)
                    act_(qarg, qarg, ACT.Exp)
                    act_(ecum, cum[:, g * 512:(g + 1) * 512], ACT.Exp)
                    act_(klarg, klarg, ACT.Exp)
                    act_(karg, karg, ACT.Exp).then_inc(exps_ready, 1)

                def gla_keys(g):
                    await_product(sc, "keT", l, g)
                    for c in range(2):
                        ins = act_(ke[:, c * 512:(c + 1) * 512], bank(("keT", l, g)), ACT.Copy, scale=half[c])
                    free(ins, "keT", l, g)

                def gla_turned(g):
                    await_product(sc, "oT", l, g)
                    for j in range(4):
                        ins = act_(o[:, g * 512 + j * P:g * 512 + (j + 1) * P], bank(("oT", l, g))[:, j * P:(j + 1) * P],
                                   ACT.Copy, scale=vecs[:, 64 * l + 60 + j:64 * l + 61 + j])
                    free(ins, "oT", l, g)

                def mgate(n):
                    for g in range(G):
                        take(gates[:, g * 3 * D + n * 512:g * 3 * D + (n + 1) * 512], ("mg", l, g, n), ACT.Sigmoid)

                def gla_sqrt():
                    st.next(gla_var)
                    act_(stat[:, 50:54], stat[:, 42:46], ACT.Sqrt).then_inc(gla_std, 1)

                gla_exps(0)
                mgate(0)
                mod_rows(l, 8, mrow)
                gla_keys(0)
                mgate(1)
                mod_rows(l, 9, mrow)
                mgate(2)
                gla_sqrt()
                mgate(3)
                gla_turned(0)
                gla_exps(1)
                mgate(4)
                gla_keys(1)
                mgate(5)
                gla_sqrt()
                gla_turned(1)
                take(kbtok, ("kbtok", l))
                take(kctxT, ("kctxT", l))
                norm_sqrt(2)

                def softmax_exp(n):
                    st.next(P_arg)
                    act_(Pm[:, 0:n], Pm[:, 0:n], ACT.Exp).then_inc(P_exp, 1)

                for g in range(G):
                    await_product(sc, "cvT", l, g)
                    for j in range(4):
                        ins = act_(acc[:, g * 512 + j * P:g * 512 + (j + 1) * P], bank(("cvT", l, g))[:, j * P:(j + 1) * P],
                                   ACT.Silu, scale=vecs[:, 64 * l + 52 + j:64 * l + 53 + j],
                                   bias=vecs[:, 64 * l + 56 + j:64 * l + 57 + j])
                    free(ins, "cvT", l, g)
                softmax_exp(1024)
                for i in range(2):
                    take(PT[:, i * 512:(i + 1) * 512], ("PT", l, 0, i))
                softmax_exp(2048)
                take(attT[:, 0:512], ("attT", l, 0))
                for i in range(4):
                    take(PT[:, i * 512:(i + 1) * 512], ("PT", l, 1, i))
                take(attT[:, 512:1024], ("attT", l, 1))
                for g in range(G):
                    for n in range(2):
                        take(gbc1[:, g * D + n * 512:g * D + (n + 1) * 512], ("gbc", l, 0, g, n))
                mod_rows(l, 10, mrow)
                for g in range(G):
                    for h in range(2):
                        await_product(sc, "mT", l, g, h)
                        for j in range(4):
                            k = 4 * h + j
                            ins = act_(hT[:, k * T + g * P:k * T + (g + 1) * P], bank(("mT", l, g, h))[:, j * P:(j + 1) * P],
                                       ACT.Copy)
                        free(ins, "mT", l, g, h)
                for g in range(G):
                    norm_sqrt(1)
                    if g == 0:
                        mod_rows(l, 11, mrow)
                    sc.wait_ge(mod_ready, 2 * l + 2)
                    modulated("h2T", 24, 32, g)
                    if l == 0:
                        high_h("h2T", l, g)
                        if g == 0:
                            for j in range(D0, D0 + DPARTS):
                                early_hi(j)
                if l == 0:
                    for g in range(G):
                        take(sil_d[:, g * 512:g * 512 + FCHUNKS[0][1]], ("G", 0, g), ACT.Silu)
                    for j in range(D0 + DPARTS, D0 + 2 * DPARTS):
                        early_hi(j)
                sc.wait_ge(kv_stored, 32 * (l + 1))
                for g in range(G):
                    for n in range(2):
                        take(gbc2[:, g * D + n * 512:g * D + (n + 1) * 512], ("gbc", l, 1, g, n))
                if l == 0:
                    def dense_turned(i):
                        for g in range(G):
                            await_product(sc, "aT", i, g)
                            act_(turned_to(dT_hi, i, g), turned_from(i, g), ACT.Copy).then_inc(act_hi, 1)

                    for j in range(D0 + 2 * DPARTS, PHASE["dense end"]):
                        i = (j - D0 - 8) // 8
                        if (j - D0) % 8 == 0 and 0 < i < len(FCHUNKS):
                            fn = FCHUNKS[i][1]
                            for g in range(G):
                                await_copied(sc, "U", i - 1, g)
                                take(sil_d[:, g * 512:g * 512 + fn], ("G", i, g), ACT.Silu, src=bank(("G", i, g))[:, 0:fn])
                        i = (j - D0 - 12) // 8
                        if (j - D0) % 8 == 4 and 0 <= i < len(FCHUNKS):
                            if i:
                                dense_turned(i - 1)
                            if i in EARLY:
                                mod_rows(1, i, mrow2)
                        if j == DLAST_TURN + DPARTS:
                            dense_turned(len(FCHUNKS) - 1)
                        early_hi(j)
                    norm_sqrt(1)
                    mod_rows(1, 4, mrow2)
                    norm_sqrt(1)
                    mod_rows(1, 5, mrow2)
                else:
                    for g in range(G):
                        for h in range(2):
                            take(htok[:, g * D + h * 512:g * D + (h + 1) * 512], ("htok", g, h))
                    st.next(gate_arg)
                    act_(route[:, 100:102], route[:, 98:100], ACT.Exp).then_inc(gate_exp, 1)

            def experts(passes):
                with sc.Fori(0, EXPERTS) as e:
                    E = e + EXPERTS * passes

                    def e_take(out, *name, func=ACT.Copy, src=None):
                        e_await_product(sc, E, *name)
                        e_free(act_(out, ebank(name) if src is None else src, func), *name)

                    def high(out, *name):
                        e_await_product(sc, E, *name)
                        act_(out, ebank(name), ACT.Copy).then_inc(act_hi, 1)

                    for j in range(EQ):
                        if j == 3:
                            for h in range(2):
                                high(hg_hi[:, h * 512:(h + 1) * 512], "hg", h)
                            e_take(S2T, "ST", src=ebank(("ST",))[:, 0:256])
                        i = (j - 10) // 8
                        if j % 8 == 2 and 0 <= i < EC:
                            if i:
                                e_await_copied(sc, E, "U", i - 1)
                            else:
                                e_await_copied(sc, E, "U", EC - 1, back=1)
                            e_take(sil, "G", i, func=ACT.Silu)
                        if j % 8 == 6 and 0 < i < EC:
                            high(eT_hi[:, (i - 1) * 512:i * 512], "T", i - 1)
                        if j == LAST_TURN:
                            high(eT_hi[:, (EC - 1) * 512:EC * 512], "T", EC - 1)
                        s_ = (j // 4) % XRING
                        if j % 4 == 0:
                            sc.wait_ge(w_loaded[s_], E * (16 * EUPER[s_]) + 16 * (UBASE[s_] + j // 4 // XRING + 1))
                        await_part_free(sc, E, j)
                        act_(split_part(j)[0], raw_part(j), ACT.Copy).then_inc(part_hi, 1)
                    e_take(yd[:, 512:1024], "D", 1)

            experts(0)
            sc.wait_ge(flag_ready, 1)
            over = sc.value_load(flag[0:1, 0:1], min_val=0, max_val=T)
            with sc.If(over > P):
                experts(1)
            for _ in range(G):
                st.next(var_ready)
                act_(stat[:, 40:41], stat[:, 39:40], ACT.Sqrt).then_inc(std_ready, 1)

        @block.vector
        def _(dv):
            st = Steps(dv, dve_step)
            V = nc.vector

            def lag(ins, n):
                ins.then_inc(dve_step, 1)
                st.made[dve_step.name] += 1
                if st.made[dve_step.name] > n:
                    dv.wait_ge(dve_step, st.made[dve_step.name] - n)

            def settle():
                dv.wait_ge(dve_step, st.made[dve_step.name])

            def rstd(src_var, out):
                st.done(V.tensor_scalar(stat[:, 39:40], src_var, EPS, None, ALU.add), var_ready)
                st.next(std_ready)
                st.done(V.reciprocal(out, stat[:, 40:41]))

            def moments(halves):
                for i, h in enumerate(halves):
                    st.done(V.bn_stats(stat[:, 6 * i:6 * i + 6], h))
                st.done(V.bn_aggr(stat[:, 36:38], stat[:, 0:6 * len(halves)]))

            def layer_norm(xg, gain, bias_, sig):
                moments([xg[:, 0:512], xg[:, 512:1024]])
                rstd(stat[:, 37:38], stat[:, 38:39])
                st.done(V.tensor_scalar(xg, xg, stat[:, 36:37], stat[:, 38:39], ALU.subtract, ALU.mult))
                st.done(V.tensor_tensor(xg, xg, gain, ALU.mult))
                st.done(V.tensor_tensor(xg, xg, bias_, ALU.add), sig)

            def early_lo(j):
                name, first_, n = DQ[j]
                dv.wait_ge(part_hi, j + 1)
                w_hi, w_lo = early_part(j)
                V.tensor_tensor(w_lo[:, 0:n], slot(SLOT[UIDX[name]])[:, first_:first_ + n], w_hi[:, 0:n].bitcast(F32),
                                ALU.subtract).then_inc(part_lo, 1)

            def low_h(rest, g):
                st.next(act_hi)
                V.tensor_tensor(group_of(rest, g), group_of(hT[:, :], g), group_of(h_hi, g).bitcast(F32),
                                ALU.subtract).then_inc(h_split, 1)

            await_product(dv, "vecs")
            freed(dv, V.tensor_copy(vecs[:, :], bank(("vecs",))[:, 0:392]), "vecs")

            for l in range(DEPTH):
                vl = 64 * l
                mod3 = modT[:, 96 * l:96 * (l + 1)].rearrange("p (c g) -> p c g", g=G)

                def mod_columns(u0, u1, scales):
                    for i in range(u0, u1):
                        await_copied(dv, "modT", l, i)
                    c0, c1 = 4 * u0, 4 * u1
                    st.done(V.tensor_reduce(mod3[:, c0:c1], modraw[:, 8 * c0:8 * c1].rearrange(
                        "p (c j g) -> p c g j", j=4, g=G), X, ALU.add))
                    st.done(V.tensor_tensor(mod3[:, c0:c1], mod3[:, c0:c1],
                                            vecs[:, vl + c0:vl + c1].unsqueeze(2).to_broadcast([P, c1 - c0, G]), ALU.add))
                    if scales is None:
                        return
                    sc_ = modT[:, 96 * l + G * scales:96 * l + G * (scales + KD)]
                    st.done(V.tensor_scalar(sc_, sc_, 1.0, None, ALU.add), mod_ready)

                mod_columns(0, 4, 8)

                def modulated(kind, sh, scl, g):
                    await_product(dv, kind, l, g, 0)
                    for k in range(4):
                        ins = V.tensor_scalar(hT[:, k * T + g * P:k * T + (g + 1) * P],
                                              bank((kind, l, g, 0))[:, k * P:(k + 1) * P],
                                              modcol(l, scl + k, g), modcol(l, sh + k, g), ALU.mult, ALU.add)
                    free(ins, kind, l, g, 0)

                def lo_unit(kind):
                    for j in range(4):
                        early_lo(DFIRST[kind, l] + j)

                for g in range(G):
                    modulated("hT", 0, 8, g)
                    low_h(hm_lo, g)
                    if g == 0:
                        lo_unit("v")
                for kind in ("vb", "r", "cva", "cvg", "qk"):
                    lo_unit(kind)
                dv.wait_ge(zeroed, 4)
                z4 = z[:, :].rearrange("p (c g w) -> p c g w", c=CC, g=G)
                for i in range(2):
                    await_copied(dv, "cvg", l, i)
                    await_product(dv, "cva", l, i)
                    for j in range(2):
                        ins = V.tensor_tensor(z4[:, 2 * i + j, :, TAPS // 2:TAPS // 2 + P],
                                              bank(("cva", l, i))[:, j * T:(j + 1) * T].rearrange("p (g t) -> p g t", g=G),
                                              gtmp[:, i * 512 + j * T:i * 512 + (j + 1) * T].rearrange("p (g t) -> p g t", g=G),
                                              ALU.mult)
                    freed(dv, ins, "cva", l, i)
                lo_unit("kb")
                await_product(dv, "gda", l)
                free(V.tensor_copy(gdaT[0:32, :], bank(("gda", l))[0:32, 0:T]), "gda", l)
                await_product(dv, "q", l)
                if l:
                    dv.wait_ge(kv_stored, 32 * l)
                freed(dv, V.tensor_scalar(qT, bank(("q", l)), GLA_DK ** -0.5, None, ALU.mult), "q", l)
                for g in range(G):
                    lg, tmp = glog[:, g * 512:(g + 1) * 512], gtmp[:, g * 512:(g + 1) * 512]
                    await_product(dv, "glog", l, g)
                    freed(dv, V.tensor_copy(lg, bank(("glog", l, g))), "glog", l, g)
                    st.done(V.scalar_tensor_tensor(out=tmp, in0=lg, scalar=-1.0, in1=lg, op0=ALU.mult, op1=ALU.min),
                            glog_part)
                for g in range(G):
                    lg, tmp = glog[:, g * 512:(g + 1) * 512], gtmp[:, g * 512:(g + 1) * 512]
                    st.next(glog_soft)
                    st.done(V.scalar_tensor_tensor(out=lg, in0=lg, scalar=0.0, in1=tmp, op0=ALU.min, op1=ALU.subtract),
                            glog_ready)
                lo_unit("qb")
                await_copied(dv, "k", l)
                await_product(dv, "rope", l)
                o4 = bank(("rope", l)).rearrange("p (w h t) -> p w h t", w=2, h=HP)
                tmp = gtmp[:, 0:512].rearrange("p (w h t) -> p w h t", w=2, h=HP)
                sin_b = C("sin").unsqueeze(1).to_broadcast([P, 4, P])
                cos_b = C("cos").unsqueeze(1).to_broadcast([P, HP, P])
                freed(dv, V.tensor_tensor(gtmp[:, 0:512].rearrange("p (w t) -> p w t", w=4),
                                          bank(("rope", l)).rearrange("p (w t) -> p w t", w=4), sin_b, ALU.mult), "rope", l)
                for n, w in enumerate((qT, kT)):
                    s = w.rearrange("p (h t) -> p h t", h=HP)[:, :, P:T]
                    st.done(V.tensor_tensor(s, s, cos_b, ALU.mult))
                    st.done(V.tensor_tensor(s, s, tmp[:, n], ALU.add))
                for g in range(G):
                    await_product(dv, "cum", l, g)
                    freed(dv, V.tensor_scalar(cum[:, g * 512:(g + 1) * 512], bank(("cum", l, g)), 1.0 / TAU, None,
                                              ALU.mult), "cum", l, g)

                def gla_prepare(g):
                    if g:
                        await_product(dv, "o", l, 0)
                        dv.wait_ge(state_stored, 32 * (l + 1))
                    cg = cum[:, g * 512:(g + 1) * 512]
                    for dr in range(2):
                        cd = cg[:, dr * 256:(dr + 1) * 256]
                        first = 0 if dr == 0 else SUB - 1
                        end = CHUNK - 1 if dr == 0 else 0
                        V.tensor_tensor(qarg[:, dr * 256:(dr + 1) * 256].rearrange("p (b s) -> p b s", s=SUB),
                                        cd.rearrange("p (b s) -> p b s", s=SUB),
                                        cd[:, first:256:SUB].unsqueeze(2).to_broadcast([P, 16, SUB]), ALU.subtract)
                        V.tensor_tensor(klarg[:, dr * 256:(dr + 1) * 256].rearrange("p (c s) -> p c s", s=CHUNK),
                                        cd[:, end:256:CHUNK].unsqueeze(2).to_broadcast([P, 4, CHUNK]),
                                        cd.rearrange("p (c s) -> p c s", s=CHUNK), ALU.subtract)
                        for hp in range(HP):
                            ch = cd[:, hp * P:(hp + 1) * P]
                            kd = karg[:, (dr * HP + hp) * 512:(dr * HP + hp + 1) * 512]
                            for c in range(2):
                                kc = kd[:, c * 256:(c + 1) * 256].rearrange("p (b s) -> p b s", s=CHUNK)
                                lag(V.tensor_tensor(kc, ch[:, c * CHUNK + first:(c + 1) * CHUNK:SUB].unsqueeze(2)
                                                    .to_broadcast([P, 4, CHUNK]),
                                                    ch[:, c * CHUNK:(c + 1) * CHUNK].unsqueeze(1)
                                                    .to_broadcast([P, 4, CHUNK]), ALU.subtract), 99999)
                    settle()
                    st.done(V.tensor_scalar(karg, karg, EXP_CAP, None, ALU.min), args_ready)
                    st.next(exps_ready)
                    qg = [w.rearrange("p (h t) -> p h t", h=HP)[:, :, g * P:(g + 1) * P] for w in (qT, kT)]
                    for dr in range(2):
                        for dst, e_ in ((qpad, qarg), (qepad, ecum)):
                            d4 = dst[:, dr * 512:(dr + 1) * 512].rearrange("p (h a t) -> p h a t", h=HP, a=2)
                            e3 = e_[:, dr * 256:(dr + 1) * 256].rearrange("p (h t) -> p h t", h=HP)
                            for s in range(2):
                                V.scalar_tensor_tensor(out=d4[:, :, s, :], in0=qg[0], scalar=half[s], in1=e3,
                                                       op0=ALU.mult, op1=ALU.mult)
                        kl = klarg[:, dr * 256:(dr + 1) * 256].rearrange("p (h t) -> p h t", h=HP)
                        V.tensor_tensor(kl, kl, qg[1], ALU.mult)
                        for hp in range(HP):
                            kd = karg[:, (dr * HP + hp) * 512:(dr * HP + hp + 1) * 512].rearrange(
                                "p (c b s) -> p c b s", c=2, b=4)
                            kk = qg[1][:, hp, :].rearrange("p (c s) -> p c s", c=2).unsqueeze(2)\
                                .to_broadcast([P, 2, 4, CHUNK])
                            ins = V.tensor_tensor(kd, kd, kk, ALU.mult)
                    st.done(ins, gla_ready)

                def gla_mask(g):
                    A3 = A[:, :].rearrange("p (h t) -> p h t", h=GLA_H)
                    T3 = gtmp[:, 0:512].rearrange("p (h t) -> p h t", h=GLA_H)
                    if g:
                        await_product(dv, "o", l, 0)
                    elif l:
                        await_product(dv, "o", l - 1, 1)
                    for dr, dst in ((0, A3), (1, T3)):
                        await_product(dv, "att", l, g, dr)
                        src = bank(("att", l, g, dr)).rearrange("p (h t) -> p h t", h=GLA_H)
                        for c in range(2):
                            q = slice(64 * c, 64 * c + 64)
                            m = C("mask_f" if dr == 0 else "mask_b")[q, q].unsqueeze(1).to_broadcast([64, GLA_H, 64])
                            ins = V.tensor_tensor(dst[q, :, q], src[q, :, q], m, ALU.mult)
                        freed(dv, ins, "att", l, g, dr)
                    for c in range(2):
                        q = slice(64 * c, 64 * c + 64)
                        ins = V.tensor_tensor(A3[q, :, q], A3[q, :, q], T3[q, :, q], ALU.add)
                    st.done(ins, A_ready)

                def gla_carry(g):
                    if g:
                        dv.wait_ge(state_in, 32 * (l + 1))
                        await_product(dv, "o", l, 0)
                    for dr in range(2):
                        await_product(dv, "kv", l, g, dr)
                        kv = bank(("kv", l, g, dr))
                        c0 = 0 if dr == 0 else 1
                        end = CHUNK - 1 if dr == 0 else 0
                        for hp in range(HP):
                            j = dr * HP + hp
                            s1 = S1[:, j * P:(j + 1) * P]
                            first = kv[:, (c0 * HP + hp) * P:(c0 * HP + hp + 1) * P]
                            second = kv[:, ((1 - c0) * HP + hp) * P:((1 - c0) * HP + hp + 1) * P]

                            def decay(c):
                                t = j * P + c * CHUNK + end
                                return ecum[:, t:t + 1]

                            if g == 0:
                                st.done(V.tensor_copy(s1, first))
                                ins = V.scalar_tensor_tensor(out=qarg[:, j * P:(j + 1) * P], in0=s1, scalar=decay(1 - c0),
                                                             in1=second, op0=ALU.mult, op1=ALU.add)
                            else:
                                ins = V.scalar_tensor_tensor(out=s1, in0=S0[:, j * P:(j + 1) * P], scalar=decay(c0),
                                                             in1=first, op0=ALU.mult, op1=ALU.add)
                        freed(dv, ins, "kv", l, g, dr)

                def gla_norm(g):
                    og = o[:, g * 512:(g + 1) * 512]
                    o3 = og.rearrange("p (h v) -> p h v", h=GLA_H)
                    sq = gtmp[:, 512:1024]
                    await_product(dv, "o", l, g)
                    freed(dv, V.tensor_copy(og, bank(("o", l, g))), "o", l, g)
                    st.done(V.tensor_tensor(sq, og, og, ALU.mult))
                    st.done(V.tensor_reduce(stat[:, 42:46], sq.rearrange("p (h v) -> p h v", h=GLA_H), X, ALU.add))
                    st.done(V.tensor_scalar(stat[:, 42:46], stat[:, 42:46], 1.0 / GLA_DV, EPS, ALU.mult, ALU.add), gla_var)
                    st.next(gla_std)
                    st.done(V.reciprocal(stat[:, 46:50], stat[:, 50:54]))
                    st.done(V.tensor_tensor(o3, o3, stat[:, 46:50].unsqueeze(2).to_broadcast([P, GLA_H, GLA_DV]), ALU.mult))
                    await_copied(dv, "r", l, g)
                    st.done(V.tensor_tensor(og, og, r[:, g * 512:(g + 1) * 512], ALU.mult), o_ready)

                def conv_taps(t0, t1):
                    if t0 == 0 and l:
                        await_product(dv, "y", l - 1, 2, 1, 1)
                    a4 = acc.rearrange("p (g c t) -> p c g t", g=G, c=CC)
                    for t in range(t0, t1):
                        for c in range(CC):
                            src = z4[:, c, :, t:t + P]
                            w = vecs[:, 144 + 124 * l + t * CC + c:145 + 124 * l + t * CC + c]
                            if t == 0:
                                ins = V.tensor_scalar(a4[:, c], src, w, vecs[:, vl + 48 + c:vl + 49 + c], ALU.mult, ALU.add)
                            else:
                                ins = V.scalar_tensor_tensor(out=a4[:, c], in0=src, scalar=w, in1=a4[:, c],
                                                             op0=ALU.mult, op1=ALU.add)
                            if t == TAPS - 1 and c == CC - 1:
                                ins.then_inc(conv_summed, 1)
                            else:
                                lag(ins, CC - 1)

                def conv_norm():
                    for g in range(G):
                        await_product(dv, "cvtok", l, g)
                        b = bank(("cvtok", l, g))
                        moments([b])
                        rstd(stat[:, 37:38], stat[:, 38:39])
                        freed(dv, V.tensor_scalar(acc[:, g * 512:(g + 1) * 512], b, stat[:, 36:37], stat[:, 38:39],
                                                  ALU.subtract, ALU.mult), "cvtok", l, g)

                def softmax(g):
                    keys = P * (1 + g)
                    n = NA_H * keys
                    Pn = Pm[:, 0:n]
                    P4 = Pn.rearrange("p (h k) -> p h k", h=NA_H)
                    if g:
                        await_product(dv, "PT", l, 0, 1)
                        b3 = bias.rearrange("p (h k) -> p h k", h=NA_H)
                    for i in range(2 * (1 + g)):
                        await_product(dv, "sc", l, g, i)
                        s = bank(("sc", l, g, i))
                        if g == 0:
                            free(V.tensor_scalar(Pn[:, i * 512:(i + 1) * 512], s, NA_DH ** -0.5, None, ALU.mult), "sc", l, g, i)
                        else:
                            s3 = s.rearrange("p (h k) -> p h k", h=2)
                            d3 = P4[:, 2 * i:2 * i + 2, :]
                            V.scalar_tensor_tensor(out=d3[:, :, 0:P], in0=s3[:, :, 0:P], scalar=NA_DH ** -0.5,
                                                   in1=b3[:, 2 * i:2 * i + 2, :], op0=ALU.mult, op1=ALU.add)
                            free(V.tensor_scalar(d3[:, :, P:2 * P], s3[:, :, P:2 * P], NA_DH ** -0.5, None, ALU.mult),
                                 "sc", l, g, i)
                    await_copied(dv, "sc", l, g, 2 * (1 + g) - 1)
                    st.done(V.tensor_reduce(stat[:, 12:20], P4, X, ALU.max))
                    st.done(V.tensor_tensor(P4, P4, stat[:, 12:20].unsqueeze(2).to_broadcast([P, NA_H, keys]),
                                            ALU.subtract), P_arg)
                    st.next(P_exp)
                    st.done(V.tensor_reduce(stat[:, 20:28], P4, X, ALU.add))
                    st.done(V.reciprocal(stat[:, 28:36], stat[:, 20:28]))
                    st.done(V.tensor_tensor(P4, P4, stat[:, 28:36].unsqueeze(2).to_broadcast([P, NA_H, keys]),
                                            ALU.mult), P_ready)

                await_product(dv, "qb", l, 1)
                gla_prepare(0)
                conv_taps(0, 12)
                gla_mask(0)
                gla_carry(0)
                gla_norm(0)
                gla_prepare(1)
                conv_taps(12, 22)
                gla_mask(1)
                gla_carry(1)
                gla_norm(1)
                conv_taps(22, TAPS)
                mod_columns(4, 10, 32)
                await_product(dv, "bias", l, 1)
                for i in range(2):
                    freed(dv, V.tensor_tensor(bias[:, i * 512:(i + 1) * 512].rearrange("p (h k) -> p h k", h=4),
                                              bank(("bias", l, i)).rearrange("p (h k) -> p h k", h=4),
                                              C("window").unsqueeze(1).to_broadcast([P, 4, P]), ALU.add), "bias", l, i)
                conv_norm()
                softmax(0)
                softmax(1)

                def diagonal(dst, c0, j):
                    for g in range(G):
                        ins = V.tensor_tensor(dst[:, g * D:(g + 1) * D].rearrange("p (c n) -> p c n", c=KD),
                                              ident.unsqueeze(1).to_broadcast([P, KD, P]),
                                              mod3[:, c0:c0 + KD, g:g + 1].to_broadcast([P, KD, P]), ALU.mult)
                    st.done(ins, diag_ready)

                def gated(b):
                    for g in range(G):
                        for n in range(2):
                            await_copied(dv, "mg", l, g, 2 * b + n)
                            await_product(dv, "y", l, b, g, n)
                            s = gates[:, g * 3 * D + b * D + 512 * n:g * 3 * D + b * D + 512 * n + 512]
                            free(V.tensor_tensor(s, s, bank(("y", l, b, g, n)), ALU.mult), "y", l, b, g, n)

                gated(0)
                gated(2)
                diagonal(diag1, 16, 0)
                gated(1)
                await_copied(dv, "y", l, 1, 1, 1)
                for g in range(G):
                    m = [gates[:, g * 3 * D + b * D:g * 3 * D + (b + 1) * D] for b in range(3)]
                    st.done(V.tensor_tensor(m[0], m[0], m[1], ALU.add))
                    st.done(V.tensor_tensor(m[0], m[0], m[2], ALU.add), m_ready)

                def block_norm(j, lnw, gbc, name, sig, g):
                    dv.wait_ge(ln_in, 32 * (2 * l + j + 1))
                    for n in range(2):
                        xs = x[:, g * D + 512 * n:g * D + 512 * n + 512]
                        tmp = mtmp[:, 0:512] if j == 0 else ftmp[:, 0:512]
                        await_copied(dv, "gbc", l, j, g, n)
                        await_product(dv, *name(g, n))
                        freed(dv, V.tensor_tensor(tmp, gbc[:, g * D + 512 * n:g * D + 512 * n + 512],
                                                  bank(name(g, n)), ALU.mult), *name(g, n))
                        st.done(V.scalar_tensor_tensor(out=xs, in0=xs, scalar=ALPHA, in1=tmp, op0=ALU.mult,
                                                       op1=ALU.add))
                    layer_norm(x[:, g * D:(g + 1) * D], lnw[:, 0:D], lnw[:, D:2 * D], sig)

                def dense_act(i, g):
                    fn = FCHUNKS[i][1]
                    if i:
                        await_product(dv, "aT", i - 1, g)
                    await_copied(dv, "G", i, g)
                    await_product(dv, "U", i, g)
                    free(V.tensor_tensor(act_d[:, g * 512:g * 512 + fn], sil_d[:, g * 512:g * 512 + fn],
                                         bank(("U", i, g))[:, 0:fn], ALU.mult), "U", i, g)

                for g in range(G):
                    block_norm(0, ln1, gbc1, lambda g, n: ("mix", l, g, n), x_ready, g)
                    modulated("h2T", 24, 32, g)
                    if l == 0:
                        low_h(h_lo, g)
                        if g == 0:
                            for j in range(D0, D0 + DPARTS):
                                early_lo(j)
                await_product(dv, "h2T", l, 1, 1)
                if l == 0:
                    for j in range(D0 + DPARTS, D0 + 2 * DPARTS):
                        early_lo(j)
                mod_columns(10, 12, None)
                diagonal(diag2, 40, 1)
                if l == 0:
                    def dense_rest(i):
                        for g in range(G):
                            st.next(act_hi)
                            free(V.tensor_tensor(turned_to(dT_lo, i, g), turned_from(i, g),
                                                 turned_to(dT_hi, i, g).bitcast(F32), ALU.subtract), "aT", i, g)

                    for j in range(D0 + 2 * DPARTS, PHASE["dense end"]):
                        i = (j - D0 - 12) // 8
                        if (j - D0) % 8 == 4 and 0 <= i < len(FCHUNKS):
                            for g in range(G):
                                dense_act(i, g)
                            if i:
                                dense_rest(i - 1)
                        if j == DLAST_TURN + DPARTS:
                            dense_rest(len(FCHUNKS) - 1)
                        early_lo(j)
                    for g in range(G):
                        block_norm(1, ln2, gbc2, lambda g, n: ("Y", g, n), x_ready, g)

            def R(i, n):
                return route[:, i:i + n]

            def GE(i):
                return R(i, 16).rearrange("p (g e) -> p g e", g=G)

            def EG(i):
                return R(i, 16).rearrange("p (e g) -> p g e", g=G)

            def over_e(i):
                return R(i, G).unsqueeze(2).to_broadcast([P, G, EXPERTS])

            LOG, TMP, TOP1, TOP2, MASK, V1, V2, AT, DIFF, GATE1, GATE2, NUM = 0, 16, 32, 48, 64, 80, 82, 84, 98, 102, 104, 106
            nums = R(NUM, EXPERTS).unsqueeze(1).to_broadcast([P, G, EXPERTS])
            st.done(V.memset(route[:, 128:256], -BIG))
            st.done(V.memset(moe_y, 0.0))
            st.done(V.tensor_scalar(R(NUM, EXPERTS), C("slots")[:, 0:EXPERTS], -1.0 * EXPERTS, None, ALU.add))
            await_product(dv, "logits")
            freed(dv, V.tensor_copy(R(LOG, 16), bank(("logits",))[:, 0:16]), "logits")

            def pick(src, top, onehot):
                st.done(V.tensor_reduce(R(top, G), GE(src), X, ALU.max))
                st.done(V.tensor_tensor(GE(onehot), GE(src), over_e(top), ALU.is_equal))
                st.done(V.tensor_tensor(GE(onehot), GE(onehot), nums, ALU.mult))
                st.done(V.tensor_reduce(R(AT, G), GE(onehot), X, ALU.min))
                st.done(V.tensor_tensor(GE(onehot), nums, over_e(AT), ALU.is_equal))

            pick(LOG, V1, TOP1)
            st.done(V.scalar_tensor_tensor(out=R(TMP, 16), in0=R(TOP1, 16), scalar=-1e30, in1=R(LOG, 16),
                                           op0=ALU.mult, op1=ALU.add))
            pick(TMP, V2, TOP2)
            st.done(V.tensor_tensor(R(MASK, 16), R(TOP1, 16), R(TOP2, 16), ALU.add), mask_ready)
            st.done(V.tensor_tensor(R(DIFF, 2), R(V2, 2), R(V1, 2), ALU.subtract), gate_arg)
            st.next(gate_exp)
            st.done(V.tensor_scalar(R(GATE1, 2), R(100, 2), 1.0, None, ALU.add))
            st.done(V.reciprocal(R(GATE1, 2), R(GATE1, 2)))
            st.done(V.tensor_tensor(R(GATE2, 2), R(100, 2), R(GATE1, 2), ALU.mult))
            st.done(V.tensor_tensor(GE(TOP1), GE(TOP1), over_e(GATE1), ALU.mult))
            st.done(V.tensor_tensor(GE(TOP2), GE(TOP2), over_e(GATE2), ALU.mult))
            POS, WT = 128, 192
            for n in range(2):
                st.done(V.tensor_tensor(EG(WT + 16 * n), GE(TOP1), GE(TOP2), ALU.add))
            await_product(dv, "rank")
            rank = bank(("rank",))
            st.done(V.tensor_scalar(R(TMP, 16), rank[:, 0:16], BIG, None, ALU.add))
            st.done(V.tensor_tensor(R(TMP, 16), R(TMP, 16), R(MASK, 16), ALU.mult))
            st.done(V.tensor_scalar(EG(POS), GE(TMP), -BIG, None, ALU.add))
            st.done(V.tensor_scalar(EG(POS + 16), GE(TMP), -BIG - P, None, ALU.add))
            freed(dv, V.tensor_reduce(R(DIFF, 1), rank[:, 16:24], X, ALU.max), "rank")
            st.done(V.tensor_copy(flag[:, :], R(DIFF, 1)), flag_ready)

            def select(E):
                for g in range(G):
                    pos = route[:, bass.ds(POS + 2 * E + g, 1)]
                    wt = route[:, bass.ds(WT + 2 * E + g, 1)]
                    V.tensor_scalar(S[:, g * P:(g + 1) * P], C("slots"), pos, None, ALU.is_equal)
                    ins = V.tensor_scalar(S2[:, g * P:(g + 1) * P], C("slots"), pos, wt, ALU.is_equal, ALU.mult)
                ins.then_inc(sel_ready, 1)

            def experts(passes):
                with dv.Fori(0, EXPERTS) as e:
                    E = e + EXPERTS * passes
                    def low(hi, lo, n, *name):
                        dv.wait_ge(act_hi, E * HI_PER + (HI_BASE + n))
                        e_free(V.tensor_tensor(lo, ebank(name), hi.bitcast(F32), ALU.subtract), *name)

                    for j in range(EQ):
                        if j == 3:
                            for h in range(2):
                                hs = slice(h * 512, (h + 1) * 512)
                                low(hg_hi[:, hs], hg_lo[:, hs], h + 1, "hg", h)
                            e_await_product(dv, E, "ST")
                            select(E + 1)
                        i = (j - 14) // 8
                        if j % 8 == 6 and 0 <= i < EC:
                            if i >= 2:
                                e_await_product(dv, E, "T", i - 2)
                            e_await_copied(dv, E, "G", i)
                            e_await_product(dv, E, "U", i)
                            b = slice((i % 2) * 512, (i % 2 + 1) * 512)
                            e_free(V.tensor_tensor(act[:, b], sil, ebank(("U", i)), ALU.mult), "U", i)
                            if i:
                                fs = slice((i - 1) * 512, i * 512)
                                low(eT_hi[:, fs], eT_lo[:, fs], 2 + i, "T", i - 1)
                        if j == LAST_TURN:
                            fs = slice((EC - 1) * 512, EC * 512)
                            low(eT_hi[:, fs], eT_lo[:, fs], 2 + EC, "T", EC - 1)
                        dv.wait_ge(part_hi, E * EQ + (PART_BASE + j + 1))
                        w_hi, w_lo = split_part(j)
                        V.tensor_tensor(w_lo, raw_part(j), w_hi.bitcast(F32), ALU.subtract).then_inc(part_lo, 1)
                    e_await_product(dv, E, "D", 0)
                    e_free(V.tensor_copy(yd[:, 0:512], ebank(("D", 0))), "D", 0)
                    for g in range(G):
                        for n in range(2):
                            e_await_product(dv, E, "SC", g, n)
                            y = moe_y[:, g * D + 512 * n:g * D + 512 * n + 512]
                            e_free(V.tensor_tensor(y, y, ebank(("SC", g, n)), ALU.add), "SC", g, n)
                    e_await_copied(dv, E, "SC", 1, 1)

            select(0)
            experts(0)
            over = dv.value_load(flag[0:1, 0:1], min_val=0, max_val=T)
            with dv.If(over > P):
                experts(1)
            dv.wait_ge(ln_in, 32 * 2 * DEPTH)
            await_copied(dv, "gbc", DEPTH - 1, 1, 1, 1)
            for g in range(G):
                xg, yg = x[:, g * D:(g + 1) * D], moe_y[:, g * D:(g + 1) * D]
                st.done(V.tensor_tensor(yg, yg, gbc2[:, g * D:(g + 1) * D], ALU.mult))
                st.done(V.scalar_tensor_tensor(out=xg, in0=xg, scalar=ALPHA, in1=yg, op0=ALU.mult, op1=ALU.add))
                layer_norm(xg, ln2[:, 0:D], ln2[:, D:2 * D], y_ready)


_INS = ["x_prompt", "x_sample", "cache_na_k", "cache_na_v", "state_gla", "c", "c_ctx", "w_mod", "b_mod", "w_in",
        "gla_w_gup", "gla_b_g", "gla_norm", "w_br_gla", "na_rpb", "w_br_na", "cv_w", "cv_b", "cv_ln_g", "cv_ln_b",
        "w_br_cv", "w_out", "ln_g", "ln_b", "ffd_w_gate", "ffd_w_up", "ffd_w_down",
        "moe_w_router", "moe_w_gate", "moe_w_up", "moe_w_down"]
_OUTS = [(1, P, D), (1, P, D), (1, DEPTH, P, NA_H, NA_DH), (1, DEPTH, P, NA_H, NA_DH),
         (1, DEPTH, 2, GLA_H, GLA_DK, GLA_DV)]


def kernel(**inputs):
    import numpy as _np
    import concourse.bacc as _bacc
    from concourse.bass_utils import run_bass_kernel_spmd as _run

    nc = _bacc.Bacc("TRN2", target_bir_lowering=False, num_devices=1)
    arrays, args = {}, {}
    for name in _INS:
        arrays[f"in_{name}"] = _np.ascontiguousarray(inputs[name])
        args[name] = nc.dram_tensor(f"in_{name}", arrays[f"in_{name}"].shape, F32, kind="ExternalInput").ap()
    arrays["const_tables"] = shape_constants()
    args["const_tables"] = nc.dram_tensor("const_tables", arrays["const_tables"].shape, F32, kind="ExternalInput").ap()
    outs = [nc.dram_tensor(f"out_{i}", shape, F32, kind="ExternalOutput").ap() for i, shape in enumerate(_OUTS)]
    build(nc, args, outs)
    r = _run(nc, [arrays], core_ids=[0])
    return tuple(r.results[0][f"out_{i}"] for i in range(len(_OUTS)))
```
